# Optimizing a Trainium2 kernel written in Bass

```python
import jax
import jax.numpy as jnp
from jax import lax
import numpy as np

D_MODEL = 1024
BATCH = 1
SEQ = 256
DEPTH = 2

CTX_LEN = 256
GRID_W = 64
EPS = 1e-6
ROPE_THETA = 10000.0
Q_BLOCK = 128

M_HEADS = 4
M_DH = 96
M_WIDTH = M_HEADS * M_DH
M_CHUNK = 64
M_CONV = 3

A_HEADS = 6
A_KV = 2
A_DH = 64
A_WIDTH = A_HEADS * A_DH

L_HEADS = 4
L_NOPE = 64
L_ROPE = 32
L_QK = L_NOPE + L_ROPE
L_DV = 64
L_QRANK = 256
L_KVRANK = 128
L_WIDTH = L_HEADS * L_DV

MIX_WIDTH = M_WIDTH + A_WIDTH + L_WIDTH
IN_SIZES = (M_WIDTH, M_WIDTH, M_WIDTH, M_WIDTH, 4 * M_HEADS,
            A_WIDTH, A_KV * A_DH, A_KV * A_DH,
            L_QRANK, L_KVRANK, L_ROPE)
IN_WIDTH = sum(IN_SIZES)

D_FF = 3584
N_EXPERTS = 8
TOP_K = 2

F32 = jnp.float32

kernel_name = 'hybrid_mlstm_gqa_mla_prefix_dit'

def rmsnorm(x, g):
    xf = x.astype(F32)
    y = xf * lax.rsqrt(jnp.mean(xf * xf, axis=-1, keepdims=True) + EPS)
    return (y * g.astype(F32)).astype(x.dtype)

def modulate(x, g, shift, scale):
    return rmsnorm(x, g) * (1 + scale) + shift

def to_heads(a, n_heads):
    b, t, _ = a.shape
    return a.reshape(b, t, n_heads, -1).transpose(0, 2, 1, 3)

def merge_heads(o):
    b, hk, g, t, dv = o.shape
    return o.transpose(0, 3, 1, 2, 4).reshape(b, t, hk * g * dv)

def axial_rope_angles(rows, cols, rot_dim):
    nf = rot_dim // 4
    inv = ROPE_THETA ** (-jnp.arange(nf, dtype=F32) / nf)
    ar = rows[:, None] * inv
    ac = cols[:, None] * inv
    ang = jnp.concatenate([ar, ar, ac, ac], axis=-1)
    return jnp.cos(ang), jnp.sin(ang)

def apply_rope(x, cos, sin):
    half = x.shape[-1] // 2
    quarter = half // 2

    def rotate_half(u):
        return jnp.concatenate([-u[..., quarter:], u[..., :quarter]], axis=-1)

    rot = jnp.concatenate([rotate_half(x[..., :half]), rotate_half(x[..., half:])], axis=-1)
    return (x.astype(F32) * cos + rot.astype(F32) * sin).astype(x.dtype)

def centred_dwconv(x, w):
    k, ch = w.shape
    pad = k // 2
    return lax.conv_general_dilated(x, w.astype(x.dtype)[:, None, :], window_strides=(1,),
                                    padding=[(pad, pad)], dimension_numbers=('NWC', 'WIO', 'NWC'),
                                    feature_group_count=ch)

def attend_blocked(q, k, v, scale):
    b, hk, g, tq, d = q.shape
    nb = tq // Q_BLOCK
    qb = jnp.moveaxis(q.reshape(b, hk, g, nb, Q_BLOCK, d), 3, 0)

    def one_block(qi):
        s = jnp.einsum('bhgqd,bhkd->bhgqk', qi, k, preferred_element_type=F32) * scale
        p = jax.nn.softmax(s, axis=-1)
        return jnp.einsum('bhgqk,bhkd->bhgqd', p.astype(v.dtype), v)

    o = lax.map(one_block, qb)
    return jnp.moveaxis(o, 0, 3).reshape(b, hk, g, tq, v.shape[-1])

def mlstm_scan(q, k, v, log_i, log_f, state):
    b, h, t, dh = q.shape
    nc = t // M_CHUNK

    def to_chunks(a):
        a = a.reshape(b, h, nc, M_CHUNK, *a.shape[3:])
        return jnp.moveaxis(a, 2, 0)

    tril = jnp.tril(jnp.ones((M_CHUNK, M_CHUNK), dtype=bool))

    def step(carry, xs):
        c_st, n_st, m_st = carry
        qc, kc, vc, ic, fc = xs
        bcum = jnp.cumsum(fc, axis=-1)
        dmat = jnp.where(tril, bcum[..., :, None] - bcum[..., None, :] + ic[..., None, :], -jnp.inf)
        m_inter = bcum + m_st[..., None]
        m_t = jnp.maximum(m_inter, jnp.max(dmat, axis=-1))
        w = jnp.exp(dmat - m_t[..., None]) * jnp.einsum('bhtd,bhsd->bhts', qc, kc)
        a_inter = jnp.exp(m_inter - m_t)
        num = a_inter[..., None] * jnp.einsum('bhtd,bhde->bhte', qc, c_st) + jnp.einsum('bhts,bhse->bhte', w, vc)
        den = a_inter * jnp.einsum('bhtd,bhd->bht', qc, n_st) + jnp.sum(w, axis=-1)
        h_out = num / jnp.maximum(jnp.abs(den), jnp.exp(-m_t))[..., None]
        g = bcum[..., -1:] - bcum + ic
        m_new = jnp.maximum(bcum[..., -1] + m_st, jnp.max(g, axis=-1))
        decay = jnp.exp(bcum[..., -1] + m_st - m_new)
        wk = jnp.exp(g - m_new[..., None])
        c_new = decay[..., None, None] * c_st + jnp.einsum('bhs,bhsd,bhse->bhde', wk, kc, vc)
        n_new = decay[..., None] * n_st + jnp.einsum('bhs,bhsd->bhd', wk, kc)
        return (c_new, n_new, m_new), h_out

    state, hs = lax.scan(step, state, tuple(to_chunks(a) for a in (q, k, v, log_i, log_f)))
    return jnp.moveaxis(hs, 0, 2).reshape(b, h, t, dh), state

def mlstm_prep(mq, mk, mv, mg, conv_w, gate_b):
    b, t, _ = mq.shape
    qk = jax.nn.silu(centred_dwconv(jnp.concatenate([mq, mk], axis=-1), conv_w))
    q = to_heads(qk[..., :M_WIDTH], M_HEADS).astype(F32)
    k = to_heads(qk[..., M_WIDTH:], M_HEADS).astype(F32) * (M_DH ** -0.5)
    v = to_heads(mv, M_HEADS).astype(F32)
    g = (mg + gate_b).astype(F32).transpose(0, 2, 1).reshape(b, 4, M_HEADS, t)
    log_i = g[:, 0::2]
    log_f = jax.nn.log_sigmoid(g[:, 1::2])
    return q, k, v, log_i, log_f

def mlstm_bidirectional(ctx_in, lat_in):
    qc, kc, vc, ic, fc = ctx_in
    ql, kl, vl, il, fl = lat_in
    b, h, _, dh = qc.shape
    zero = (jnp.zeros((b, h, dh, dh), F32), jnp.zeros((b, h, dh), F32), jnp.zeros((b, h), F32))

    def flip(a):
        return jnp.flip(a, axis=2)

    hc_f, st_f = mlstm_scan(qc, kc, vc, ic[:, 0], fc[:, 0], zero)
    hl_f, _ = mlstm_scan(ql, kl, vl, il[:, 0], fl[:, 0], st_f)
    hc_b, st_b = mlstm_scan(flip(qc), flip(kc), flip(vc), flip(ic[:, 1]), flip(fc[:, 1]), zero)
    hl_b, _ = mlstm_scan(flip(ql), flip(kl), flip(vl), flip(il[:, 1]), flip(fl[:, 1]), st_b)
    return hc_f + flip(hc_b), hl_f + flip(hl_b)

def mlstm_out(h, o, norm_g):
    b, nh, t, dh = h.shape
    hn = rmsnorm(h.transpose(0, 2, 1, 3), norm_g.reshape(nh, dh)).reshape(b, t, nh * dh)
    return (hn * jax.nn.sigmoid(o.astype(F32))).astype(o.dtype)

def gqa_prep(aq, ak, av, qn, kn, rope):
    q = rmsnorm(to_heads(aq, A_HEADS), qn)
    k = rmsnorm(to_heads(ak, A_KV), kn)
    v = to_heads(av, A_KV)
    if rope is not None:
        q = apply_rope(q, *rope)
        k = apply_rope(k, *rope)
    b, _, t, _ = q.shape
    return q.reshape(b, A_KV, A_HEADS // A_KV, t, A_DH), k, v

def mla_prep(cq, ckv, kr, cq_norm, ckv_norm, wuq, wukv, qn, kn, rope):
    q = to_heads(rmsnorm(cq, cq_norm) @ wuq, L_HEADS)
    kv = to_heads(rmsnorm(ckv, ckv_norm) @ wukv, L_HEADS)
    k_nope = rmsnorm(kv[..., :L_NOPE], kn[:L_NOPE])
    v = kv[..., L_NOPE:]
    q_nope = rmsnorm(q[..., :L_NOPE], qn[:L_NOPE])
    q_rope = rmsnorm(q[..., L_NOPE:], qn[L_NOPE:])
    k_rope = rmsnorm(kr, kn[L_NOPE:])
    if rope is not None:
        q_rope = apply_rope(q_rope, *rope)
        k_rope = apply_rope(k_rope, *rope)
    b, h, t, _ = q.shape
    q = jnp.concatenate([q_nope, q_rope], axis=-1)
    k = jnp.concatenate([k_nope, jnp.broadcast_to(k_rope[:, None], (b, h, t, L_ROPE))], axis=-1)
    return q[:, :, None], k, v

def hybrid_mixer(h_lat, h_ctx, need_ctx, w_in, m_conv, m_gate_b, m_norm, a_qnorm, a_knorm,
                 l_cq_norm, l_ckv_norm, l_wuq, l_wukv, l_qnorm, l_knorm, w_out, rope_a, rope_l):
    split_at = np.cumsum(IN_SIZES)[:-1].tolist()
    pl = jnp.split(h_lat @ w_in, split_at, axis=-1)
    pc = jnp.split(h_ctx @ w_in, split_at, axis=-1)
    hm_ctx, hm_lat = mlstm_bidirectional(mlstm_prep(pc[0], pc[1], pc[2], pc[4], m_conv, m_gate_b),
                                         mlstm_prep(pl[0], pl[1], pl[2], pl[4], m_conv, m_gate_b))
    qa_l, ka_l, va_l = gqa_prep(pl[5], pl[6], pl[7], a_qnorm, a_knorm, rope_a)
    qa_c, ka_c, va_c = gqa_prep(pc[5], pc[6], pc[7], a_qnorm, a_knorm, None)
    oa_lat = merge_heads(attend_blocked(qa_l, jnp.concatenate([ka_c, ka_l], axis=2),
                                        jnp.concatenate([va_c, va_l], axis=2), A_DH ** -0.5))
    ql_l, kl_l, vl_l = mla_prep(pl[8], pl[9], pl[10], l_cq_norm, l_ckv_norm, l_wuq, l_wukv, l_qnorm, l_knorm, rope_l)
    ql_c, kl_c, vl_c = mla_prep(pc[8], pc[9], pc[10], l_cq_norm, l_ckv_norm, l_wuq, l_wukv, l_qnorm, l_knorm, None)
    ol_lat = merge_heads(attend_blocked(ql_l, jnp.concatenate([kl_c, kl_l], axis=2),
                                        jnp.concatenate([vl_c, vl_l], axis=2), L_QK ** -0.5))
    o_lat = jnp.concatenate([mlstm_out(hm_lat, pl[3], m_norm), oa_lat, ol_lat], axis=-1) @ w_out
    if not need_ctx:
        return o_lat, None
    oa_ctx = merge_heads(attend_blocked(qa_c, ka_c, va_c, A_DH ** -0.5))
    ol_ctx = merge_heads(attend_blocked(ql_c, kl_c, vl_c, L_QK ** -0.5))
    o_ctx = jnp.concatenate([mlstm_out(hm_ctx, pc[3], m_norm), oa_ctx, ol_ctx], axis=-1) @ w_out
    return o_lat, o_ctx

def swiglu(x, wg, wu, wd):
    return (jax.nn.silu(x @ wg) * (x @ wu)) @ wd

def moe_swiglu(x, router, wg, wu, wd):
    b, t, d = x.shape
    xt = x.reshape(b * t, d)
    logits = (xt @ router).astype(F32)
    top_val, top_idx = lax.top_k(logits, TOP_K)
    top_w = jax.nn.softmax(top_val, axis=-1)
    combine = jnp.einsum('nk,nke->ne', top_w, jax.nn.one_hot(top_idx, N_EXPERTS, dtype=F32)).astype(x.dtype)
    out = jnp.zeros_like(xt)
    for e in range(N_EXPERTS):
        out = out + combine[:, e:e + 1] * swiglu(xt, wg[e], wu[e], wd[e])
    return out.reshape(b, t, d)

def setup_inputs(seed: int = 0) -> dict:
    key = jax.random.key(seed)
    ks = iter(jax.random.split(key, 32))

    def nrm(shape, scale):
        return jax.random.normal(next(ks), shape, F32) * scale

    def gain(shape):
        return 1.0 + nrm(shape, 0.1)

    nd = (DEPTH + 1) // 2
    nm = DEPTH // 2
    d = D_MODEL
    gate_offset = jnp.tile(jnp.repeat(jnp.array([0.0, 3.0], F32), M_HEADS), 2)
    return {
        'x': nrm((BATCH, SEQ, d), 1.0),
        'c': nrm((BATCH, d), 1.0),
        'ctx': nrm((BATCH, CTX_LEN, d), 1.0),
        'c_ctx': nrm((d,), 1.0),
        'mod_w': nrm((DEPTH, d, 6 * d), 0.5 * d ** -0.5),
        'mod_b': nrm((DEPTH, 6 * d), 0.01),
        'norm_mix': gain((DEPTH, d)),
        'norm_ffn': gain((DEPTH, d)),
        'w_in': nrm((DEPTH, d, IN_WIDTH), d ** -0.5),
        'm_conv': nrm((DEPTH, M_CONV, 2 * M_WIDTH), M_CONV ** -0.5),
        'm_gate_b': gate_offset + nrm((DEPTH, 4 * M_HEADS), 0.5),
        'm_norm': gain((DEPTH, M_WIDTH)),
        'a_qnorm': gain((DEPTH, A_DH)),
        'a_knorm': gain((DEPTH, A_DH)),
        'l_cq_norm': gain((DEPTH, L_QRANK)),
        'l_ckv_norm': gain((DEPTH, L_KVRANK)),
        'l_wuq': nrm((DEPTH, L_QRANK, L_HEADS * L_QK), L_QRANK ** -0.5),
        'l_wukv': nrm((DEPTH, L_KVRANK, L_HEADS * (L_NOPE + L_DV)), L_KVRANK ** -0.5),
        'l_qnorm': gain((DEPTH, L_QK)),
        'l_knorm': gain((DEPTH, L_QK)),
        'w_out': nrm((DEPTH, MIX_WIDTH, d), MIX_WIDTH ** -0.5),
        'ffn_wg': nrm((nd, d, D_FF), d ** -0.5),
        'ffn_wu': nrm((nd, d, D_FF), d ** -0.5),
        'ffn_wd': nrm((nd, D_FF, d), D_FF ** -0.5),
        'moe_router': nrm((nm, d, N_EXPERTS), d ** -0.5),
        'moe_wg': nrm((nm, N_EXPERTS, d, D_FF), d ** -0.5),
        'moe_wu': nrm((nm, N_EXPERTS, d, D_FF), d ** -0.5),
        'moe_wd': nrm((nm, N_EXPERTS, D_FF, d), D_FF ** -0.5),
    }

def reference(x, c, ctx, c_ctx, mod_w, mod_b, norm_mix, norm_ffn, w_in, m_conv, m_gate_b, m_norm,
              a_qnorm, a_knorm, l_cq_norm, l_ckv_norm, l_wuq, l_wukv, l_qnorm, l_knorm, w_out,
              ffn_wg, ffn_wu, ffn_wd, moe_router, moe_wg, moe_wu, moe_wd):
    seq = x.shape[1]
    ROWS = seq // GRID_W
    rows = jnp.repeat(jnp.arange(ROWS, dtype=F32), GRID_W)
    cols = jnp.tile(jnp.arange(GRID_W, dtype=F32), ROWS)
    rope_a = axial_rope_angles(rows, cols, A_DH)
    rope_l = axial_rope_angles(rows, cols, L_ROPE)
    silu_c = jax.nn.silu(c)
    silu_cc = jax.nn.silu(c_ctx)
    for i in range(DEPTH):
        need_ctx = i < DEPTH - 1
        mod_lat = (silu_c @ mod_w[i] + mod_b[i])[:, None, :]
        mod_ctx = silu_cc @ mod_w[i] + mod_b[i]
        sh_a, sc_a, g_a, sh_f, sc_f, g_f = jnp.split(mod_lat, 6, axis=-1)
        csh_a, csc_a, cg_a, csh_f, csc_f, cg_f = jnp.split(mod_ctx, 6, axis=-1)
        o_lat, o_ctx = hybrid_mixer(modulate(x, norm_mix[i], sh_a, sc_a),
                                    modulate(ctx, norm_mix[i], csh_a, csc_a), need_ctx,
                                    w_in[i], m_conv[i], m_gate_b[i], m_norm[i], a_qnorm[i], a_knorm[i],
                                    l_cq_norm[i], l_ckv_norm[i], l_wuq[i], l_wukv[i], l_qnorm[i], l_knorm[i],
                                    w_out[i], rope_a, rope_l)
        x = x + g_a * o_lat
        j = i // 2
        if i % 2 == 0:
            ffn = lambda u: swiglu(u, ffn_wg[j], ffn_wu[j], ffn_wd[j])
        else:
            ffn = lambda u: moe_swiglu(u, moe_router[j], moe_wg[j], moe_wu[j], moe_wd[j])
        x = x + g_f * ffn(modulate(x, norm_ffn[i], sh_f, sc_f))
        if need_ctx:
            ctx = ctx + cg_a * o_ctx
            ctx = ctx + cg_f * ffn(modulate(ctx, norm_ffn[i], csh_f, csc_f))
    return x


_drawn_inputs = setup_inputs


def setup_inputs(seed=0):
    import zlib

    import numpy as np

    out = dict(_drawn_inputs(seed))
    spreads = {}
    factors = {'mod_b': 3.657,
     'm_norm': 2.774,
     'a_qnorm': 8.0,
     'a_knorm': 8.0,
     'l_cq_norm': 8.0,
     'l_ckv_norm': 6.788,
     'l_qnorm': 8.0,
     'l_knorm': 8.0}
    for name, (base, spread) in spreads.items():
        noise = np.random.default_rng([zlib.crc32(name.encode()), seed]).standard_normal(out[name].shape)
        drawn = base * np.exp(spread * noise) if base else spread * noise
        out[name] = jnp.asarray(drawn.astype(out[name].dtype))
    for name, factor in factors.items():
        out[name] = (out[name] * factor).astype(out[name].dtype)
    return out
```

```python
from contextlib import ExitStack

import numpy as np
import concourse.bass as bass
from concourse import mybir

F32 = mybir.dt.float32
I32 = mybir.dt.int32
U32 = mybir.dt.uint32
ALU = mybir.AluOpType
ACT = mybir.ActivationFunctionType
AX = mybir.AxisListType

P = 128
NT = 4
TOK = NT * P
D = 1024
KT = D // P
EPS = 1e-6
DEPTH = 2
MH, MD = 4, 96
MW = MH * MD
AH, AKV, AD = 6, 2, 64
LH, NOPE, ROPE = 4, 64, 32
LQK = NOPE + ROPE
QRANK, KVRANK = 256, 128
FF = 3584
NE = 8
FS = 512
NJ = FF // FS
NEG = -1e30
RING = 14
LOW = 7
SLOT = 4 * 512

C_ID, C_SEL, C_MF, C_MB = 0, 128, 640, 1024
C_COSA, C_SINA, C_COSL, C_SINL = 1408, 1536, 1664, 1728
C_TRI, C_ONE, C_IOTA, C_END = 1792, 1920, 2048, 2304
G_M, G_AQ, G_AK, G_LQ, G_LK, G_GB, G_END = 0, 384, 448, 512, 608, 704, 720
W_Q, W_K, W_OG, W_GQA, W_AVCQ, W_CKV, W_MV = (0, 384), (384, 384), (1152, 400), (1552, 512), (2064, 384), (2448, 160), (768, 384)
ROWS_OF_W = (W_OG, W_GQA, W_AVCQ, W_CKV, W_MV)


def constants():
    c = np.zeros((P, C_END), np.float32)
    c[:, C_ID:C_ID + P] = np.eye(P)
    for h in range(4):
        c[h, C_SEL + h * P:C_SEL + (h + 1) * P] = 1
    t, s = np.arange(P)[:, None], np.arange(P)[None, :]
    c[:, C_MF + 128:C_MF + 256] = np.where(s <= t, 0, NEG)
    c[:, C_MF + 256:C_MF + 384] = NEG
    c[:, C_MB:C_MB + 128] = NEG
    c[:, C_MB + 128:C_MB + 256] = np.where(s >= t, 0, NEG)
    tok = np.arange(256)
    rows, cols = (tok // 64).astype(np.float32), (tok % 64).astype(np.float32)
    for dim, cc, cs in ((AD, C_COSA, C_SINA), (ROPE, C_COSL, C_SINL)):
        nf = dim // 4
        inv = (np.float32(10000.0) ** (-np.arange(nf, dtype=np.float32) / np.float32(nf))).astype(np.float32)
        ar, ac = rows[:, None] * inv, cols[:, None] * inv
        ang = np.concatenate([ar, ar, ac, ac], -1)
        sign = np.tile(np.repeat(np.array([-1.0, 1.0], np.float32), nf), 2)
        cos, sin = np.cos(ang), np.sin(ang) * sign
        for i in range(2):
            c[:, cc + i * dim:cc + (i + 1) * dim] = cos[i * P:(i + 1) * P]
            c[:, cs + i * dim:cs + (i + 1) * dim] = sin[i * P:(i + 1) * P]
    c[:, C_TRI:C_TRI + P] = t < s
    c[:, C_ONE:C_ONE + P] = 1
    c[:, C_IOTA:C_IOTA + 256] = np.arange(256)
    return c


class BankPlan:

    def __init__(self):
        self.count = [0] * 8
        self.at = {}

    def add(self, name, bank):
        self.at[name] = (bank, self.count[bank])
        self.count[bank] += 1


def query_tiles(layer):
    return [0, 1, 2, 3] if layer == 0 else [2, 3]


def mixer_units(layer):
    att = [("A", h, t) for t in query_tiles(layer) for h in range(AH + LH)]
    mem = [("M", h, t) for t in query_tiles(layer) for h in range(MH)]
    out = []
    for i, u in enumerate(att):
        out.append(u)
        if (i + 1) * len(mem) // len(att) > i * len(mem) // len(att):
            out.append(mem.pop(0))
    return out + mem


def plan_banks():
    plan = BankPlan()
    for L in range(DEPTH):
        for i in range(12):
            plan.add(("mod", L, i), i % 2)
            if i:
                plan.add(("modT", L, i - 1), 2 + (i - 1) % 2)
        plan.add(("modT", L, 11), 3)
        for k in range(KT):
            plan.add(("norm", L, "a", k), k % 4)
        for h in range(8):
            plan.add(("conv", L, h), 4 + h % 4)
        n = 0
        for s in range(len(ROWS_OF_W)):
            for t in range(NT):
                plan.add(("proj", L, s, t), n % 4)
                n += 1
        for g in range(4):
            plan.add(("gateT", L, g), 4 + g)
        for g in range(4):
            plan.add(("gqaT", L, g), g)
        plan.add(("stab", L), 7)
        for g in range(3):
            plan.add(("mlaT", L, g), 4 + g)
        for t in range(NT):
            plan.add(("mlaq", L, t), 2 * (t % 2))
            plan.add(("mlakv", L, t), 2 * (t % 2) + 1)
        for g in range(8):
            plan.add(("mlaH", L, g), g)
        for unit in mixer_units(L):
            for part, b in ((("S", 0), ("T", 1), ("O", 2)) if unit[0] == "A" else
                            (("CF", 3), ("CB", 4), ("S", 5), ("T", 6), ("O", 7))):
                plan.add((part, L, unit), b)
        gs = (0, 1) if L == 0 else (1,)
        for k in range(KT):
            plan.add(("outT", L, k), k % 4)
        for g in gs:
            for half in range(2):
                plan.add(("gateA", L, g, half), 4 + half)
        n = 0
        for half in range(2):
            for t in query_tiles(L):
                plan.add(("out", L, half, t), n % 4)
                n += 1
        for k in range(KT):
            plan.add(("norm", L, "f", k), 4 + k % 4)
        if L == 0:
            for j in range(NJ):
                for t in range(NT):
                    s = j * NT + t
                    plan.add(("G", s), s % 2)
                    plan.add(("U", s), 2 + s % 2)
                    plan.add(("HT", s), 4)
                    plan.add(("Y", s, 0), 6)
                    plan.add(("Y", s, 1), 7)
            for g in gs:
                for half in range(2):
                    plan.add(("gateF", L, g, half), 4 + half)
        else:
            for t in range(2):
                plan.add(("router", t), 4 + t)
            plan.add(("pos",), 4)
            for half in range(2):
                plan.add(("gateF", L, 1, half), 6 + half)
    return plan


MOE_USES = {0: 4, 1: 3, 2: 4, 3: 3, 4: 7, 5: 7, 6: 1, 7: 1}


def moe_place(name):
    kind, i = name
    if kind == "G":
        return i % 2, i // 2
    if kind == "U":
        return 2 + i % 2, i // 2
    if kind == "HT":
        return 4, i
    if kind == "SC":
        return 5, i
    if kind == "ST":
        return 5, 4
    if kind == "GA":
        return 5, 5 + i
    return 6 + i, 0


def moe_tiles():
    out = []
    for j in range(NJ):
        out += [("g", j, 0), ("g", j, 1), ("u", j, 0), ("u", j, 1)]
        if j:
            out += [("d", j - 1, 0), ("d", j - 1, 1)]
    return out + [("d", NJ - 1, 0), ("d", NJ - 1, 1)]


def build(nc, a, consts, out):
    plan = plan_banks()
    tiles = moe_tiles()
    PER = len(tiles)
    assert PER % RING == 0

    with ExitStack() as ctx:
        def sb(name, shape, dt=F32):
            return ctx.enter_context(nc.sbuf_tensor(name, shape, dt))

        sems = {}

        def sem(name):
            if name not in sems:
                sems[name] = ctx.enter_context(nc.semaphore(name))
            return sems[name]

        ring = sb("ring", [P, RING * SLOT])
        X = sb("X", [P, NT, D])
        hT = sb("hT", [P, KT * TOK])
        bigA = sb("bigA", [P, NT * D])
        bigB = sb("bigB", [P, 8 * 512])
        cst = sb("cst", [P, C_END])
        gains = sb("gains", [P, DEPTH, G_END])
        scr = sb("scr", [P, 2048])
        crow = sb("crow", [4, 2, 512])
        small = sb("small", [P, 360])
        modT = sb("modT", [P, 6, KT, 2])
        cvec = sb("cvec", [P, KT, 2])
        convw = sb("convw", [MD, DEPTH, 8, 3])
        idx = sb("idx", [P, 8], U32)
        flag = sb("flag", [P, 1], I32)

        def view(t, at, *dims):
            n = int(np.prod(dims))
            v = t[:, at:at + n]
            if len(dims) == 1:
                return v
            if len(dims) == 2:
                return v.rearrange("p (a b) -> p a b", a=dims[0])
            return v.rearrange("p (a b c) -> p a b c", a=dims[0], b=dims[1])

        UP = LOW * SLOT
        PMO = view(ring, UP, NT, 400)
        PG = view(ring, UP + 1600, NT, 512)
        PAVCQ = view(ring, UP + 3648, NT, 384)
        PCKV = view(ring, UP + 5184, NT, 160)
        PMV = view(ring, UP + 5824, NT, 384)
        QK = view(ring, UP + 7360, 8, TOK)
        GT = view(ring, UP + 11456, 4, TOK)
        GA = view(ring, UP + 13504, NT, 16)
        LF = view(ring, UP + 13568, NT, 8)
        gtmp = view(ring, UP + 13632, NT, 8)
        assert UP + 13632 + 64 <= RING * SLOT
        PROJ = {W_OG: PMO, W_GQA: PG, W_AVCQ: PAVCQ, W_CKV: PCKV, W_MV: PMV}
        HT = view(hT, 0, KT, TOK)
        VM = view(hT, 0, NT, LH, 64)
        CT = view(hT, 1024, 3, TOK)
        PA = view(hT, 1024, 2, 512)
        PT = view(hT, 2048, 512)
        EF = view(hT, 2560, 512)
        EB = view(hT, 3072, 512)
        WT = view(hT, 3584, 512)
        PTM = view(ring, UP + 1600, 512)
        XN = view(bigA, 0, NT, D)
        OROW = XN
        QR = view(bigA, 0, NT, LH, LQK)
        KR = view(bigA, 1536, NT, LH, LQK)
        rows_f = view(bigA, 3072, 2, 512)
        rows_b = view(hT, 2560, 2, 512)
        MT = view(bigB, 0, 8, TOK)
        YACC = view(bigB, 0, NT, D)
        GBC_A = view(bigB, 0, 2, D)
        ACC = view(bigB, 0, 2, D)
        XT = view(bigB, 2048, KT, P)
        YROW = view(bigB, 3072, D)
        GM = view(bigA, 0, 2, P)
        SM = view(bigA, 256, 2, P)
        SMT = view(bigA, 512, 2, P)
        GBC_F = {0: view(bigA, 0, 2, D), 1: view(hT, 0, 2, D)}
        SQ = view(scr, 0, NT, 512)
        SIL = view(scr, 0, 2, 512)
        H = view(scr, 1024, 512)
        HTT = view(scr, 1536, 512)
        MODROW = view(scr, 0, 2, 512)
        MODB = view(scr, 1024, 2, 512)
        ident = cst[:, C_ID:C_ID + P]

        at_small = [0]

        def tiny(n):
            at_small[0] += n
            assert at_small[0] <= 360
            return small[:, at_small[0] - n:at_small[0]]

        normG = tiny(32).rearrange("p (l w k) -> p l w k", l=2, w=2)
        cqG = tiny(6).rearrange("p (l k) -> p l k", l=2)
        ss, rs = tiny(8), tiny(4)
        gss = tiny(48)
        grs = tiny(48)
        nmax, rsum, rinv = tiny(1), tiny(4), tiny(1)
        den = tiny(2)
        dabs = tiny(2)
        stab = tiny(64).rearrange("p (k t h) -> p k t h", k=4, t=4)
        LG = tiny(16).rearrange("p (t e) -> p t e", t=2)
        RT = tiny(64).rearrange("p (k e) -> p k e", k=8)
        MX, IDXF = tiny(8), tiny(4)
        wts = tiny(4)
        TOT = tiny(8)
        rt = sb("rt", [P, 3, 2, 9])
        SELM, COMB, POS = rt[:, 0], rt[:, 1], rt[:, 2]
        OH = view(scr, 0, 2, 8)

        bank = [ctx.enter_context(nc.psum_tensor(f"bank{b}", [P, 512], F32)) for b in range(8)]
        bank_full = [sem(f"bank_full{b}") for b in range(8)]
        bank_free = [sem(f"bank_free{b}") for b in range(8)]
        slot_full = [sem(f"slot_full{s}") for s in range(RING)]
        down_used = sem("down_used")

        def take_out(eng, name):
            b, n = plan.at[name]
            eng.wait_ge(bank_full[b], n + 1)
            return bank[b], bank_free[b]

        def evacuated(eng, name):
            b, n = plan.at[name]
            eng.wait_ge(bank_free[b], n + 1)

        def ffn_place(kind, s0):
            return plan.at[(kind, s0) if kind[0] != "Y" else ("Y", s0, int(kind[1]))]

        FFN_STRIDE = {"G": NT, "U": NT, "HT": 2 * NT, "Y0": 2 * NT, "Y1": 2 * NT}
        SC_PER, GA_PRO = 4, 2

        def moe_base(p, b):
            per_pass = NE * MOE_USES[b] + ((GA_PRO + SC_PER) if b == 5 else 0)
            return plan.count[b] + p * per_pass + (GA_PRO if b == 5 else 0)

        def moe_at(p, e, kind, i=0):
            b, k = moe_place((kind, i))
            return b, e * MOE_USES[b] + (moe_base(p, b) + k)

        loads = []

        def kn(ap, k0, nk, c0, n):
            return ap[k0 * P:(k0 + nk) * P, c0:c0 + n].rearrange("(k p) n -> p k n", p=P)

        low = [0]

        def load_low(src, nk, n, last):
            loads.append((low[0] % LOW, src, nk, n, last))
            low[0] += 1

        W2 = 12
        for L in range(DEPTH):
            for i in range(12):
                for half in range(2):
                    load_low(kn(a["mod_w"][L], 4 * half, 4, 512 * i, 512), 4, 512, ("mod", L, i))
            for s, (c0, n) in enumerate((W_Q, W_K) + ROWS_OF_W):
                last = ("conv", L, 4 * s + 3) if s < 2 else ("proj", L, s - 2, NT - 1)
                for half in range(2):
                    load_low(kn(a["w_in"][L], 4 * half, 4, c0, n), 4, n, last)
            load_low(kn(a["l_wuq"][L], 0, 2, 0, LH * LQK), 2, LH * LQK, ("mlaq", L, NT - 1))
            load_low(kn(a["l_wukv"][L], 0, 1, 0, 512), 1, 512, ("mlakv", L, NT - 1))
            for c in range(2):
                for half in range(2):
                    load_low(kn(a["w_out"][L], 4 * half, 4, 512 * c, 512), 4, 512, ("out", L, c, NT - 1))
            if L == 0:
                ffn_from = len(loads)
                for j in range(NJ):
                    s = NT * j + NT - 1
                    at = 6 * (j % 2)
                    for c in range(2):
                        loads.append((at + c, kn(a["ffn_wg"][0], 4 * c, 4, FS * j, FS), 4, FS, ("G", s)))
                        loads.append((at + 2 + c, kn(a["ffn_wu"][0], 4 * c, 4, FS * j, FS), 4, FS, ("U", s)))
                        loads.append((at + 4 + c, kn(a["ffn_wd"][0], 4 * j, 4, 512 * c, 512), 4, 512, ("Y", s, c)))
                ffn_to = len(loads)
                loads[ffn_from:ffn_to] = [x for j in range(NJ) for x in
                                          sorted(loads[ffn_from + 6 * j:ffn_from + 6 * j + 6], key=lambda x: x[0])]
                low[0] = 0
        uses = [0] * RING
        owner = [None] * RING
        placed = []
        for n, (slot, *_) in enumerate(loads):
            placed.append((uses[slot], owner[slot]))
            uses[slot] += 1
            owner[slot] = n
        slot_base = list(uses)

        def slot_ap(slot, nk, n):
            return view(ring, slot * SLOT, nk * n).rearrange("p (k n) -> p k n", k=nk)

        def moe_src(e, tile):
            m, j, c = tile
            w = {"g": "moe_wg", "u": "moe_wu", "d": "moe_wd"}[m]
            w = a[w][0].rearrange("e r c -> (e r) c")
            if m == "d":
                src = w[bass.ds(e * FF + FS * j, FS), 512 * c:512 * (c + 1)]
            else:
                src = w[bass.ds(e * D + 512 * c, 512), FS * j:FS * (j + 1)]
            return src.rearrange("(k p) n -> p k n", p=P)

        def moe_released(eng, p, e, tile):
            m, j, c = tile
            if m == "d" and j < NJ - 1:
                eng.wait_ge(down_used, (e + p * NE) * (NJ - 1) + (j + 1))
            else:
                b, n = moe_at(p, e, {"g": "G", "u": "U", "d": "Y"}[m], j if m != "d" else c)
                eng.wait_ge(bank_full[b], n + 1)

        def overflow(eng):
            eng.wait_ge(sem("flag_ready"), 1)
            return eng.value_load(flag[0:1, 0:1], min_val=0, max_val=1)

        def groups(L):
            return (0, 1) if L == 0 else (1,)

        def rope_swap(x, n, q):
            v = x.rearrange("p (a b c) -> p a b c", b=2, c=n // 4)
            return v[:, :, q, :]

        def paired(t, o):
            return (PG[:, t, 0:384].rearrange("p (n g d) -> p g n d", g=AKV, d=AD),
                    o[:, 0:384].rearrange("p (g n d) -> p g n d", g=AKV, d=AD))

        def columns(eng, L, w, k, g0):
            shift, scale = (0, 1) if w == "a" else (3, 4)
            o, free = take_out(eng, ("norm", L, w, k))
            for g in range(g0, 2):
                cols = slice(256 * g, 256 * (g + 1))
                sc, sh = modT[:, scale, k, g:g + 1], modT[:, shift, k, g:g + 1]
                if k % 2 == 0:
                    ins = eng.activation(HT[:, k, cols], o[:, cols], ACT.Identity, scale=sc, bias=sh)
                else:
                    ins = eng.tensor_scalar(HT[:, k, cols], o[:, cols], sc, sh, ALU.mult, ALU.add)
            ins.then_inc(free, 1)

        block = ctx.enter_context(nc.Block())

        @block.sync
        def _(sp):
            def mixer_through(L):
                evacuated(sp, ("outT", L, KT - 2))
                evacuated(sp, ("outT", L, KT - 1))

            def load(n):
                slot, src, nk, w, _ = loads[n]
                before = placed[n][1]
                if before is not None:
                    b, k = plan.at[loads[before][4]]
                    sp.wait_ge(bank_full[b], k + 1)
                sp.dma_start(slot_ap(slot, nk, w), src).then_inc(slot_full[slot], 16)

            for n in range(ffn_from + 12):
                if n == ffn_from + LOW:
                    mixer_through(0)
                load(n)
            wg, wu, wd = a["ffn_wg"][0], a["ffn_wu"][0], a["ffn_wd"][0]
            with sp.Fori(1, 3) as m:
                for jj in range(2):
                    for i in range(6):
                        kind = ("G", "U", f"Y{i % 2}")[i // 2]
                        b, k = ffn_place(kind, NT * jj + NT - 1)
                        sp.wait_ge(bank_full[b], (m - 1) * FFN_STRIDE[kind] + (k + 1))
                        if i < 4:
                            src = (wg, wu)[i // 2][512 * (i % 2):512 * (i % 2 + 1), bass.ds(m * (2 * FS) + jj * FS, FS)]
                        else:
                            src = wd[bass.ds(m * (2 * FS) + jj * FS, FS), 512 * (i % 2):512 * (i % 2 + 1)]
                        sp.dma_start(slot_ap(6 * jj + i, 4, 512), src.rearrange("(k p) n -> p k n", p=P))\
                          .then_inc(slot_full[6 * jj + i], 16)
            for n in range(ffn_to - 6, len(loads)):
                load(n)

            def expert(p, e, i):
                slot = i % RING
                sp.dma_start(slot_ap(slot, 4, 512), moe_src(e, tiles[i])).then_inc(slot_full[slot], 16)

            for i in range(PER):
                if i >= RING:
                    moe_released(sp, 0, 0, tiles[i - RING])
                elif owner[i] is not None:
                    b, k = plan.at[loads[owner[i]][4]]
                    sp.wait_ge(bank_full[b], k + 1)
                if i == LOW:
                    mixer_through(1)
                expert(0, 0, i)

            def experts(p, first):
                with sp.Fori(first, NE) as e:
                    for i in range(PER):
                        if i < RING:
                            moe_released(sp, p, e - 1, tiles[i - RING + PER])
                        else:
                            moe_released(sp, p, e, tiles[i - RING])
                        expert(p, e, i)

            experts(0, 1)
            over = overflow(sp)
            with sp.If(over > 0):
                for i in range(PER):
                    if i < RING:
                        moe_released(sp, 0, NE - 1, tiles[i - RING + PER])
                    else:
                        moe_released(sp, 1, 0, tiles[i - RING])
                    expert(1, 0, i)
                experts(1, 1)
            for t in range(2):
                sp.wait_ge(sem("out_row_ready"), t + 1)
                sp.dma_start(out[0, t * P:(t + 1) * P, :], X[:, 2 + t, :]).then_inc(sem("stored"), 16)
            sp.wait_ge(sem("stored"), 32)

        @block.gpsimd
        def _(pool):
            with nc.allow_non_contiguous_dma("small parameters"):
                pool.dma_start(cst[:, :], consts).then_inc(sem("consts_loaded"), 16)
                for i in range(2):
                    pool.dma_start(MODB[0:2, i, :], a["mod_b"][0, 512 * i:512 * (i + 1)].partition_broadcast(2))\
                        .then_inc(sem(f"modb_loaded{i}"), 16)
                for L in range(DEPTH):
                    for w, name in enumerate(("norm_mix", "norm_ffn")):
                        pool.dma_start(normG[:, L, w, :], a[name][L].rearrange("(k p) -> p k", p=P)).then_inc(sem("params_loaded"), 16)
                    pool.dma_start(cqG[:, L, 0:2], a["l_cq_norm"][L].rearrange("(k p) -> p k", p=P)).then_inc(sem("params_loaded"), 16)
                    pool.dma_start(cqG[:, L, 2:3], a["l_ckv_norm"][L].rearrange("(k p) -> p k", p=P)).then_inc(sem("params_loaded"), 16)
                    for at, name, n in ((G_M, "m_norm", MW), (G_AQ, "a_qnorm", AD), (G_AK, "a_knorm", AD),
                                        (G_LQ, "l_qnorm", LQK), (G_LK, "l_knorm", LQK), (G_GB, "m_gate_b", 16)):
                        pool.dma_start(gains[:, L, at:at + n], a[name][L].partition_broadcast(P)).then_inc(sem("params_loaded"), 16)
                    for h in range(8):
                        pool.dma_start(convw[:, L, h, :], a["m_conv"][L, :, h * MD:(h + 1) * MD].rearrange("k c -> c k"))\
                            .then_inc(sem("params_loaded"), 16)
                pool.dma_start(RT[:, :, :], a["moe_router"][0].rearrange("(k p) e -> p k e", p=P)).then_inc(sem("params_loaded"), 16)
                for L in range(DEPTH):
                    for i in range(12):
                        if L == 0 and i < 2:
                            continue
                        if i < 2:
                            evacuated(pool, ("Y", NJ * NT - 1, 1))
                        else:
                            evacuated(pool, ("mod", L, i - 2))
                        pool.dma_start(MODB[0:2, i % 2, :], a["mod_b"][L, 512 * i:512 * (i + 1)].partition_broadcast(2))\
                            .then_inc(sem(f"modb_loaded{i % 2}"), 16)
        PARAMS = 16 * (DEPTH * (2 + 2 + 6 + 8) + 1)

        @block.tensor
        def _(pe):
            taken = [0]

            def tile():
                n = taken[0]
                taken[0] += 1
                slot, _, nk, w, _ = loads[n]
                pe.wait_ge(slot_full[slot], 16 * (placed[n][0] + 1))
                return slot_ap(slot, nk, w)

            def product(name):
                b, n = plan.at[name]
                if n:
                    pe.wait_ge(bank_free[b], n)
                return bank[b], bank_full[b]

            def mod(L):
                def turn(i):
                    evacuated(pe, ("mod", L, i))
                    o, full = product(("modT", L, i))
                    for k in range(4):
                        mm = pe.transpose(o[:, 2 * k:2 * k + 2], MODROW[0:2, i % 2, k * P:(k + 1) * P], ident[0:2, 0:2])
                    mm.then_inc(full, 1)
                for i in range(12):
                    o, full = product(("mod", L, i))
                    for half in range(2):
                        w = tile()
                        for k in range(4):
                            kk = 4 * half + k
                            mm = pe.matmul(o[0:2, :], cvec[:, kk, :], w[:, k, :], start=kk == 0, stop=kk == KT - 1)
                    mm.then_inc(full, 1)
                    if i:
                        turn(i - 1)
                turn(11)

            def norm(L, w):
                ts = [t for g in (groups(L) if w == "f" else (0, 1)) for t in (2 * g, 2 * g + 1)]
                pe.wait_ge(sem(f"normed_{L}{w}"), len(ts))
                for k in range(KT):
                    o, full = product(("norm", L, w, k))
                    for t in ts:
                        mm = pe.transpose(o[:, t * P:(t + 1) * P], XN[:, t, k * P:(k + 1) * P], ident)
                    mm.then_inc(full, 1)

            def columns_ready(L, kind, *w):
                evacuated(pe, (kind, L, *w, KT - 2))
                evacuated(pe, (kind, L, *w, KT - 1))

            def project(L):
                columns_ready(L, "norm", "a")
                for c in range(2):
                    w = [tile(), tile()]
                    for h in range(4):
                        o, full = product(("conv", L, 4 * c + h))
                        for k in range(KT):
                            mm = pe.matmul(o[0:MD, :], w[k // 4][:, k % 4, h * MD:(h + 1) * MD], HT[:, k, :],
                                           start=k == 0, stop=k == KT - 1)
                        mm.then_inc(full, 1)
                for s, (_, n) in enumerate(ROWS_OF_W):
                    w = [tile(), tile()]
                    for t in range(NT):
                        o, full = product(("proj", L, s, t))
                        for k in range(KT):
                            mm = pe.matmul(o[:, 0:n], HT[:, k, t * P:(t + 1) * P], w[k // 4][:, k % 4, :],
                                           start=k == 0, stop=k == KT - 1)
                        mm.then_inc(full, 1)

            def prepare(L):
                pe.wait_ge(sem(f"gates_ready{L}"), 1)
                for g, src in enumerate((GA[:, :, 0:4], LF[:, :, 0:4], GA[:, :, 8:12], LF[:, :, 4:8])):
                    o, full = product(("gateT", L, g))
                    for t in range(NT):
                        mm = pe.transpose(o[0:4, t * P:(t + 1) * P], src[:, t, :], ident)
                    mm.then_inc(full, 1)
                pe.wait_ge(sem(f"gqa_ready{L}"), 1)
                for g in range(4):
                    o, full = product(("gqaT", L, g))
                    for t in range(NT):
                        mm = pe.transpose(o[:, t * P:(t + 1) * P], PG[:, t, g * P:(g + 1) * P], ident)
                    mm.then_inc(full, 1)
                pe.wait_ge(sem(f"stabilisers{L}"), 2)
                o, full = product(("stab", L))
                for k, (rows, r) in enumerate(((rows_f, 1), (rows_b, 1), (rows_f, 0), (rows_b, 0))):
                    for t in range(NT):
                        mm = pe.transpose(o[:, 16 * k + 4 * t:16 * k + 4 * t + 4], rows[0:4, r, t * P:(t + 1) * P],
                                          ident[0:4, 0:4])
                mm.then_inc(full, 1)
                pe.wait_ge(sem(f"latent_ready{L}"), 1)
                for g in range(3):
                    o, full = product(("mlaT", L, g))
                    for t in range(NT):
                        src = PAVCQ[:, t, 128 + g * P:128 + (g + 1) * P] if g < 2 else PCKV[:, t, 0:P]
                        mm = pe.transpose(o[:, t * P:(t + 1) * P], src, ident)
                    mm.then_inc(full, 1)
                for g in range(3):
                    evacuated(pe, ("mlaT", L, g))
                wq, wkv = tile(), tile()
                for t in range(NT):
                    o, full = product(("mlaq", L, t))
                    for k in range(2):
                        mm = pe.matmul(o[:, 0:LH * LQK], CT[:, k, t * P:(t + 1) * P], wq[:, k, :], start=k == 0, stop=k == 1)
                    mm.then_inc(full, 1)
                    o, full = product(("mlakv", L, t))
                    pe.matmul(o[:, :], CT[:, 2, t * P:(t + 1) * P], wkv[:, 0, :], start=True, stop=True).then_inc(full, 1)
                pe.wait_ge(sem(f"mla_ready{L}"), 1)
                for g in range(8):
                    o, full = product(("mlaH", L, g))
                    for t in range(NT):
                        mm = pe.transpose(o[0:LQK, t * P:(t + 1) * P], (QR if g < 4 else KR)[:, t, g % 4, :], ident)
                    mm.then_inc(full, 1)

            def heads(L):
                for g in range(4):
                    evacuated(pe, ("gqaT", L, g))
                for g in range(8):
                    evacuated(pe, ("mlaH", L, g))
                pe.wait_ge(sem(f"qk_ready{L}"), 2)

                def scores(u):
                    kind, h, t = u
                    nk = 256 if t < 2 else TOK
                    rows = slice(t * P, (t + 1) * P)
                    if kind == "A":
                        o, full = product(("S", L, u))
                        if h < AH:
                            p = slice(64 * (h // 3), 64 * (h // 3) + 64)
                            mm = pe.matmul(o[:, 0:nk], GT[p, h % 3, rows], GT[p, 3, 0:nk], start=True, stop=True)
                        else:
                            m = h - AH
                            mm = pe.matmul(o[:, 0:nk], MT[0:LQK, m, rows], MT[0:LQK, 4 + m, 0:nk], start=True, stop=True)
                        mm.then_inc(full, 1)
                        return
                    for i, (part, mask) in enumerate((("CF", C_MF), ("CB", C_MB))):
                        o, full = product((part, L, u))
                        m0 = mask + (0 if t % 2 else P)
                        pe.matmul(o[:, 0:nk], cst[0:4, C_SEL + h * P:C_SEL + (h + 1) * P], crow[0:4, i, 0:nk],
                                  start=True, stop=False)
                        pe.matmul(o[:, nk - 256:nk], ident, cst[:, m0:m0 + 256], start=False, stop=True).then_inc(full, 1)
                    o, full = product(("S", L, u))
                    pe.matmul(o[:, 0:nk], QK[0:MD, h, rows], QK[0:MD, 4 + h, 0:nk], start=True, stop=True).then_inc(full, 1)

                def turn(u, n):
                    kind, h, t = u
                    src = PA[:, n % 2, :] if kind == "A" else WT
                    if kind == "A":
                        evacuated(pe, ("S", L, u))
                    else:
                        pe.wait_ge(sem(f"weights_ready{L}"), n + 1)
                    o, full = product(("T", L, u))
                    for b in range(2 if t < 2 else NT):
                        mm = pe.transpose(o[:, b * P:(b + 1) * P], src[:, b * P:(b + 1) * P], ident)
                    mm.then_inc(full, 1)

                def values(u):
                    kind, h, t = u
                    evacuated(pe, ("T", L, u))
                    o, full = product(("O", L, u))
                    nb = 2 if t < 2 else NT
                    for b in range(nb):
                        if kind == "M":
                            w, v, n = PTM, PMV[:, b, h * MD:(h + 1) * MD], MD
                        elif h < AH:
                            w, v, n = PT, PAVCQ[:, b, 64 * (h // 3):64 * (h // 3) + 64], 64
                        else:
                            w, v, n = PT, VM[:, b, h - AH, :], 64
                        mm = pe.matmul(o[:, 0:n], w[:, b * P:(b + 1) * P], v, start=b == 0, stop=b == nb - 1)
                    mm.then_inc(full, 1)

                done = {"A": [], "M": []}
                for u in mixer_units(L):
                    d = done[u[0]]
                    scores(u)
                    if len(d) > 1:
                        values(d[-2])
                    if d:
                        turn(d[-1], len(d) - 1)
                    d.append(u)
                for d in done.values():
                    values(d[-2])
                    turn(d[-1], len(d) - 1)
                    values(d[-1])

            def spread(L, kind, sec):
                for g in groups(L):
                    for half in range(2):
                        o, full = product((kind, L, g, half))
                        for k in range(4):
                            col = modT[:, sec, 4 * half + k, g:g + 1].broadcast_to([P, P])
                            mm = pe.matmul(o[:, k * P:(k + 1) * P], col, ident, start=True, stop=True)
                        mm.then_inc(full, 1)

            def out_project(L):
                pe.wait_ge(sem(f"mix_ready{L}"), 1)
                for k in range(KT):
                    o, full = product(("outT", L, k))
                    for t in query_tiles(L):
                        mm = pe.transpose(o[:, t * P:(t + 1) * P], OROW[:, t, k * P:(k + 1) * P], ident)
                    mm.then_inc(full, 1)
                spread(L, "gateA", 2)
                columns_ready(L, "outT")
                for c in range(2):
                    w = [tile(), tile()]
                    for t in query_tiles(L):
                        o, full = product(("out", L, c, t))
                        for k in range(KT):
                            mm = pe.matmul(o[:, :], HT[:, k, t * P:(t + 1) * P], w[k // 4][:, k % 4, :],
                                           start=k == 0, stop=k == KT - 1)
                        mm.then_inc(full, 1)

            def bank_ready(b, n):
                pe.wait_ge(bank_free[b], n)
                return bank[b], bank_full[b]

            def ffn():
                columns_ready(0, "norm", "f")

                def gate_or_up(kind, s0, r, w, t):
                    b, n = ffn_place(kind, s0)
                    o, full = bank_ready(b, r * FFN_STRIDE[kind] + n)
                    for k in range(KT):
                        mm = pe.matmul(o[:, :], HT[:, k, t * P:(t + 1) * P], w[k // 4][:, k % 4, :],
                                       start=k == 0, stop=k == KT - 1)
                    mm.then_inc(full, 1)

                def turn(s0, r):
                    b, n = ffn_place("U", s0)
                    pe.wait_ge(bank_free[b], r * FFN_STRIDE["U"] + (n + 1))
                    b, n = ffn_place("HT", s0)
                    o, full = bank_ready(b, r * FFN_STRIDE["HT"] + n)
                    for k in range(4):
                        mm = pe.transpose(o[:, k * P:(k + 1) * P], H[:, k * P:(k + 1) * P], ident)
                    mm.then_inc(full, 1)

                def down(s0, r, w):
                    b, n = ffn_place("HT", s0)
                    pe.wait_ge(bank_free[b], r * FFN_STRIDE["HT"] + (n + 1))
                    for c in range(2):
                        b, n = ffn_place(f"Y{c}", s0)
                        o, full = bank_ready(b, r * FFN_STRIDE[f"Y{c}"] + n)
                        for k in range(4):
                            mm = pe.matmul(o[:, :], HTT[:, k * P:(k + 1) * P], w[c][:, k, :], start=k == 0, stop=k == 3)
                        mm.then_inc(full, 1)

                def tiles_of(at):
                    return [slot_ap(at + i, 4, 512) for i in range(6)]

                def step(j, r, s0, before):
                    at = 6 * (j % 2)
                    w = tiles_of(at)
                    u = placed[ffn_from + 6 * j][0]
                    for t in range(NT):
                        if t == 0:
                            for i in range(2):
                                pe.wait_ge(slot_full[at + i], r * 16 + 16 * (placed[ffn_from + 6 * j + i][0] + 1))
                        gate_or_up("G", s0 + t, r, w[0:2], t)
                        if before is not None:
                            turn(*before)
                        if t == 0:
                            for i in range(2, 4):
                                pe.wait_ge(slot_full[at + i], r * 16 + 16 * (placed[ffn_from + 6 * j + i][0] + 1))
                        gate_or_up("U", s0 + t, r, w[2:4], t)
                        if before is not None:
                            down(*before, tiles_of(6 - at)[4:6] if t == 0 else w[4:6])
                        if t == 0:
                            for i in range(4, 6):
                                pe.wait_ge(slot_full[at + i], r * 16 + 16 * (placed[ffn_from + 6 * j + i][0] + 1))
                        before = (s0 + t, r)

                step(0, 0, 0, None)
                with pe.Fori(0, 3) as m:
                    step(1, m, NT, (NT - 1, m))
                    step(2, m, 2 * NT, (2 * NT - 1, m))
                last = NJ * NT - 1
                turn(last, 0)
                down(last, 0, tiles_of(0)[4:6])
                taken[0] = ffn_to
                spread(0, "gateF", 5)

            def route():
                columns_ready(1, "norm", "f")
                for t in range(2):
                    o, full = product(("router", t))
                    for k in range(KT):
                        mm = pe.matmul(o[:, 0:NE], HT[:, k, (2 + t) * P:(3 + t) * P], RT[:, k, :], start=k == 0, stop=k == KT - 1)
                    mm.then_inc(full, 1)
                spread(1, "gateF", 5)
                pe.wait_ge(sem("routed"), 1)
                o, full = product(("pos",))
                tri, one = cst[:, C_TRI:C_TRI + P], cst[:, C_ONE:C_ONE + P]
                s0, s1 = SELM[:, 0, 0:NE], SELM[:, 1, 0:NE]
                pe.matmul(o[:, 0:NE], tri, s0, start=True, stop=True)
                pe.matmul(o[:, NE:2 * NE], one, s0, start=True, stop=False)
                pe.matmul(o[:, NE:2 * NE], tri, s1, start=False, stop=True)
                pe.matmul(o[:, 2 * NE:3 * NE], one, s0, start=True, stop=False)
                pe.matmul(o[:, 2 * NE:3 * NE], one, s1, start=False, stop=True).then_inc(full, 1)

            def experts(p):
                def gather(half, b, n):
                    o, full = bank_ready(b, n)
                    for k in range(4):
                        f = 4 * half + k
                        for t in range(2):
                            mm = pe.matmul(o[:, k * P:(k + 1) * P], XN[:, 2 + t, f * P:(f + 1) * P], GM[:, t, :],
                                           start=t == 0, stop=t == 1)
                    mm.then_inc(full, 1)

                def scatter(i, b, n):
                    o, full = bank_ready(b, n)
                    t, c = i // 2, i % 2
                    pe.matmul(o[:, :], SMT[:, t, :], YROW[:, 512 * c:512 * (c + 1)], start=True, stop=True).then_inc(full, 1)

                def expert(e):
                    at = [0]

                    def next_tile():
                        i = at[0]
                        at[0] += 1
                        slot = i % RING
                        pe.wait_ge(slot_full[slot], e * (16 * PER // RING) +
                                   16 * (slot_base[slot] + p * NE * (PER // RING) + i // RING + 1))
                        return slot_ap(slot, 4, 512)

                    def gate_or_up(kind, j):
                        o, full = bank_ready(*moe_at(p, e, kind, j))
                        for c in range(2):
                            w = next_tile()
                            for k in range(4):
                                mm = pe.matmul(o[:, :], XT[:, 4 * c + k, :], w[:, k, :], start=c + k == 0, stop=c + k == 4)
                        mm.then_inc(full, 1)

                    def turn(j):
                        b, n = moe_at(p, e, "U", j)
                        pe.wait_ge(bank_free[b], n + 1)
                        o, full = bank_ready(*moe_at(p, e, "HT", j))
                        for k in range(4):
                            mm = pe.transpose(o[:, k * P:(k + 1) * P], H[:, k * P:(k + 1) * P], ident)
                        mm.then_inc(full, 1)

                    def down(j):
                        b, n = moe_at(p, e, "HT", j)
                        pe.wait_ge(bank_free[b], n + 1)
                        for c in range(2):
                            b, n = moe_at(p, e, "Y", c)
                            if j == 0:
                                pe.wait_ge(bank_free[b], n)
                            w = next_tile()
                            for k in range(4):
                                mm = pe.matmul(bank[b][:, :], HTT[:, k * P:(k + 1) * P], w[:, k, :],
                                               start=j + k == 0, stop=j == NJ - 1 and k == 3)
                            if j == NJ - 1:
                                mm.then_inc(bank_full[b], 1)
                        if j < NJ - 1:
                            mm.then_inc(down_used, 1)

                    b, n = moe_at(p, e, "GA", 0)
                    pe.wait_ge(bank_free[b], n - 5)
                    for j in range(NJ):
                        gate_or_up("G", j)
                        if j < 2:
                            if j == 0:
                                for c in range(2):
                                    b, n = moe_at(p, e, "Y", c)
                                    pe.wait_ge(bank_free[b], n)
                            scatter(2 * j, *moe_at(p, e, "SC", 2 * j))
                        if j:
                            turn(j - 1)
                        gate_or_up("U", j)
                        if j < 2:
                            scatter(2 * j + 1, *moe_at(p, e, "SC", 2 * j + 1))
                        if j == NJ - 1:
                            pe.wait_ge(sem("gather_ready"), e + (p * (NE + 1) + 2))
                            gather(0, *moe_at(p, e, "GA", 0))
                        if j:
                            down(j - 1)
                        if j == 3:
                            pe.wait_ge(sem("scatter_ready"), e + (p * NE + 1))
                            o, full = bank_ready(*moe_at(p, e, "ST"))
                            for t in range(2):
                                mm = pe.transpose(o[:, t * P:(t + 1) * P], SM[:, t, :], ident)
                            mm.then_inc(full, 1)
                    turn(NJ - 1)
                    gather(1, *moe_at(p, e, "GA", 1))
                    down(NJ - 1)

                pe.wait_ge(sem("moe_cleared"), p + 1)
                pe.wait_ge(sem("gather_ready"), p * (NE + 1) + 1)
                for half in range(2):
                    gather(half, 5, moe_base(p, 5) - GA_PRO + half)
                with pe.Fori(0, NE) as e:
                    expert(e)
                for c in range(2):
                    b, n = moe_at(p, NE, "Y", c)
                    pe.wait_ge(bank_free[b], n)
                for i in range(4):
                    scatter(i, 5, moe_base(p, 5) + NE * MOE_USES[5] + i)

            pe.wait_ge(sem("consts_loaded"), 16)
            pe.wait_ge(sem("cvec_ready"), 1)
            for L in range(DEPTH):
                mod(L)
                norm(L, "a")
                project(L)
                prepare(L)
                heads(L)
                out_project(L)
                norm(L, "f")
                if L == 0:
                    ffn()
            route()
            experts(0)
            over = overflow(pe)
            with pe.If(over > 0):
                experts(1)

        @block.scalar
        def _(act):
            step = sem("act_step")
            steps = [0]

            def then(ins):
                steps[0] += 1
                ins.then_inc(step, 1)
                act.wait_ge(step, steps[0])

            def sqrt_of(L, name, v):
                act.wait_ge(sem(f"{name}_mean{L}"), 1)
                act.activation(v, v, ACT.Sqrt).then_inc(sem(f"{name}_root{L}"), 1)

            def norm(L, w):
                g0 = groups(L)[0] if w == "f" else 0
                if L == 0 and w == "a":
                    act.wait_ge(sem("x_loaded"), 32)
                else:
                    act.wait_ge(sem(f"x_updated_{L}{w}"), 1)
                for t in range(2 * g0, NT):
                    act.activation(bigB[:, t * D:(t + 1) * D], X[:, t, :], ACT.Square, accum_out=ss[:, t:t + 1]).then_inc(sem(f"squares_{L}{w}"), 1)
                sqrt_of(L, f"x{w}", rs[:, 2 * g0:NT])
                evacuated(act, ("modT", L, 11))
                for k in range(0, KT, 2):
                    columns(act, L, w, k, g0)

            def scatter_moved(i):
                pass

            act.dma_start(cvec[:, :, 1], a["c"][0].rearrange("(k p) -> p k", p=P), allow_slow_non_contiguous=True).then_inc(sem("cvec_loaded"), 16)
            act.dma_start(cvec[:, :, 0], a["c_ctx"].rearrange("(k p) -> p k", p=P), allow_slow_non_contiguous=True).then_inc(sem("cvec_loaded"), 16)
            act.dma_start(X[:, 0:2, :], a["ctx"][0].rearrange("(t p) d -> p t d", p=P)).then_inc(sem("x_loaded"), 16)
            act.dma_start(X[:, 2:4, :], a["x"][0].rearrange("(t p) d -> p t d", p=P)).then_inc(sem("x_loaded"), 16)
            act.wait_ge(sem("cvec_loaded"), 32)
            act.activation(cvec[:, :, :], cvec[:, :, :], ACT.Silu).then_inc(sem("cvec_ready"), 1)
            act.wait_ge(sem("params_loaded"), PARAMS)

            def project(L):
                for h in range(8):
                    o, _ = take_out(act, ("conv", L, h))
                    act.activation(QK[0:MD, h, :], o[0:MD, :], ACT.Identity, scale=convw[:, L, h, 1:2]).then_inc(sem(f"middle_tap{L}"), 1)
                for s, w in enumerate(ROWS_OF_W):
                    for t in (0, 2):
                        o, free = take_out(act, ("proj", L, s, t))
                        if w == W_GQA:
                            to, src = paired(t, o)
                            act.activation(to, src, ACT.Copy)
                            act.activation(PG[:, t, 384:512], o[:, 384:512], ACT.Copy).then_inc(free, 1)
                        else:
                            act.activation(PROJ[w][:, t, :], o[:, 0:w[1]], ACT.Copy).then_inc(free, 1)

            def prepare(L):
                for c in range(2):
                    evacuated(act, ("conv", L, 4 + 3))
                    evacuated(act, ("conv", L, 4 + 2))
                    act.activation(QK[0:MD, 4 * c:4 * c + 4, :], QK[0:MD, 4 * c:4 * c + 4, :], ACT.Silu).then_inc(sem(f"qk_ready{L}"), 1)
                act.wait_ge(sem(f"gate_negated{L}"), 1)
                then(act.activation(gtmp[:, :, :], gtmp[:, :, :], ACT.Exp))
                act.activation(gtmp[:, :, :], gtmp[:, :, :], ACT.Ln, bias=1.0).then_inc(sem(f"gate_log{L}"), 1)
                for t in (1, 3):
                    evacuated(act, ("proj", L, 1, t))
                act.activation(SQ[:, :, :], PG[:, :, :], ACT.Square).then_inc(sem(f"gqa_squares{L}"), 1)
                sqrt_of(L, "gqa", grs[:, 0:32])
                for t in (1, 3):
                    evacuated(act, ("proj", L, 2, t))
                    evacuated(act, ("proj", L, 3, t))
                act.wait_ge(sem(f"gqa_ready{L}"), 1)
                act.activation(SQ[:, :, 0:256], PAVCQ[:, :, 128:384], ACT.Square)
                act.activation(SQ[:, :, 256:416], PCKV[:, :, :], ACT.Square).then_inc(sem(f"latent_squares{L}"), 1)
                sqrt_of(L, "latent", grs[:, 0:12])
                o, free = take_out(act, ("stab", L))
                act.activation(stab[:, :, :, :], o[:, 0:64].rearrange("p (k t h) -> p k t h", k=4, t=4), ACT.Copy, scale=-1.0)\
                    .then_inc(free, 1)
                evacuated(act, ("stab", L))
                act.activation(stab[:, 2:4, :, :], stab[:, 2:4, :, :], ACT.Exp).then_inc(sem(f"stab_exp{L}"), 1)
                for g in range(3):
                    o, free = take_out(act, ("mlaT", L, g))
                    act.activation(CT[:, g, :], o[:, :], ACT.Identity, scale=cqG[:, L, g:g + 1]).then_inc(free, 1)
                for t in range(NT):
                    o, free = take_out(act, ("mlaq", L, t))
                    act.activation(QR[:, t, :, :], o[:, 0:LH * LQK].rearrange("p (h d) -> p h d", h=LH), ACT.Copy).then_inc(free, 1)
                for t in range(NT):
                    evacuated(act, ("mlaq", L, t))
                    evacuated(act, ("mlakv", L, t))
                act.activation(SQ[:, :, 0:384].rearrange("p t (h d) -> p t h d", h=LH), QR[:, :, :, :], ACT.Square).then_inc(sem(f"mla_squares{L}"), 1)
                act.wait_ge(sem(f"mla_squares_read{L}"), 1)
                act.activation(SQ[:, :, 0:256].rearrange("p t (h d) -> p t h d", h=LH), KR[:, :, :, 0:64], ACT.Square).then_inc(sem(f"mla_squares{L}"), 1)
                sqrt_of(L, "mla", grs[:, 0:48])
                for g in range(0, 8, 2):
                    o, free = take_out(act, ("mlaH", L, g))
                    act.activation(MT[0:LQK, g, :], o[0:LQK, :], ACT.Copy).then_inc(free, 1)

            def heads(L):
                count = {"A": 0, "M": 0}
                before = {"A": None, "M": None}

                def turned(u):
                    kind, h, t = u
                    nk = 256 if t < 2 else TOK
                    o, free = take_out(act, ("T", L, u))
                    act.activation((PT if kind == "A" else PTM)[:, 0:nk], o[:, 0:nk], ACT.Copy).then_inc(free, 1)

                for u in mixer_units(L):
                    kind, h, t = u
                    n = count[kind]
                    count[kind] += 1
                    nk = 256 if t < 2 else TOK
                    if before[kind]:
                        pass
                    if kind == "A":
                        act.wait_ge(sem(f"row_max{L}"), n + 1)
                        o, free = take_out(act, ("S", L, u))
                        act.activation(PA[:, n % 2, 0:nk], o[:, 0:nk], ACT.Exp, bias=nmax[:, 0:1],
                                       accum_out=rsum[:, n % 4:n % 4 + 1]).then_inc(free, 1)
                    else:
                        if n:
                            act.wait_ge(sem(f"weights_ready{L}"), n)
                        for i, (part, e) in enumerate((("CF", EF), ("CB", EB))):
                            o, free = take_out(act, (part, L, u))
                            act.activation(e[:, 0:nk], o[:, 0:nk], ACT.Exp, bias=stab[:, i, t, h:h + 1]).then_inc(free, 1)
                    if before[kind]:
                        turned(before[kind])
                    before[kind] = u
                turned(before["A"])
                turned(before["M"])

            def out_project(L):
                t0 = query_tiles(L)[0]
                last = [u for u in mixer_units(L) if u[0] == "M"][-1]
                evacuated(act, ("O", L, last))
                act.activation(SQ[:, t0:NT, 0:MW], OROW[:, t0:NT, 0:MW], ACT.Square).then_inc(sem(f"mlstm_squares{L}"), 1)
                sqrt_of(L, "mlstm", grs[:, 0:4 * (NT - t0)])
                act.activation(PMO[:, t0:NT, 0:MW], PMO[:, t0:NT, 0:MW], ACT.Sigmoid).then_inc(sem(f"out_gate{L}"), 1)
                for k in range(0, KT, 2):
                    o, free = take_out(act, ("outT", L, k))
                    act.activation(HT[:, k, t0 * P:], o[:, t0 * P:], ACT.Copy).then_inc(free, 1)
                spread(L, "gateA", GBC_A)

            def spread(L, kind, to):
                for g in groups(L):
                    for half in range(2):
                        o, free = take_out(act, (kind, L, g, half))
                        act.activation(to[:, g, 512 * half:512 * (half + 1)], o[:, :], ACT.Copy).then_inc(free, 1)

            def ffn():
                def silu(s0, r):
                    b, n = ffn_place("G", s0)
                    act.wait_ge(bank_full[b], r * FFN_STRIDE["G"] + (n + 1))
                    act.activation(SIL[:, s0 % 2, :], bank[b][:, :], ACT.Silu).then_inc(bank_free[b], 1)

                def turned(s0, r):
                    b, n = ffn_place("HT", s0)
                    act.wait_ge(bank_full[b], r * FFN_STRIDE["HT"] + (n + 1))
                    act.activation(HTT[:, :], bank[b][:, :], ACT.Copy).then_inc(bank_free[b], 1)

                for s in range(NT):
                    silu(s, 0)
                    if s:
                        turned(s - 1, 0)
                with act.Fori(0, 3) as m:
                    for s in range(NT, 3 * NT):
                        silu(s, m)
                        turned(s - 1, m)
                turned(NJ * NT - 1, 0)
                spread(0, "gateF", GBC_F[0])

            def experts(p):
                with act.Fori(0, NE) as e:
                    for j in range(NJ):
                        b, n = moe_at(p, e, "G", j)
                        act.wait_ge(bank_full[b], n + 1)
                        act.activation(SIL[:, j % 2, :], bank[b][:, :], ACT.Silu).then_inc(bank_free[b], 1)
                        for i in ([j - 1] if j else []) + ([j] if j == NJ - 1 else []):
                            b, n = moe_at(p, e, "HT", i)
                            act.wait_ge(bank_full[b], n + 1)
                            act.activation(HTT[:, :], bank[b][:, :], ACT.Copy).then_inc(bank_free[b], 1)
                        if j == 3:
                            b, n = moe_at(p, e, "ST")
                            act.wait_ge(bank_full[b], n + 1)
                            act.activation(SMT[:, :, :], bank[b][:, 0:2 * P].rearrange("p (t s) -> p t s", t=2), ACT.Copy)\
                                .then_inc(bank_free[b], 1)
                    for c in range(2):
                        b, n = moe_at(p, e, "Y", c)
                        act.wait_ge(bank_full[b], n + 1)
                        act.activation(YROW[:, 512 * c:512 * (c + 1)], bank[b][:, :], ACT.Copy).then_inc(bank_free[b], 1)

            for L in range(DEPTH):
                norm(L, "a")
                project(L)
                prepare(L)
                heads(L)
                out_project(L)
                norm(L, "f")
                if L == 0:
                    ffn()
            act.wait_ge(sem("expert_gap"), 1)
            act.activation(wts[:, 0:2], wts[:, 0:2], ACT.Exp).then_inc(sem("expert_gap_exp"), 1)
            spread(1, "gateF", GBC_F[1])
            act.wait_ge(sem("moe_cleared"), 1)
            experts(0)
            over = overflow(act)
            with act.If(over > 0):
                act.wait_ge(sem("moe_cleared"), 2)
                experts(1)

        @block.vector
        def _(dve):
            step = sem("dve_step")
            steps = [0]

            def then(ins):
                steps[0] += 1
                ins.then_inc(step, 1)
                dve.wait_ge(step, steps[0])

            def mean(L, name, dst, src, n):
                then(dve.tensor_scalar(dst, src, 1.0 / n, EPS, ALU.mult, ALU.add)) if name is None else \
                    dve.tensor_scalar(dst, src, 1.0 / n, EPS, ALU.mult, ALU.add).then_inc(sem(f"{name}_mean{L}"), 1)

            def rstd(L, name, v):
                dve.wait_ge(sem(f"{name}_root{L}"), 1)
                then(dve.reciprocal(v, v))

            dve.wait_ge(sem("params_loaded"), PARAMS)
            dve.wait_ge(sem("consts_loaded"), 16)
            for L in range(DEPTH):
                then(dve.tensor_scalar(gains[:, L, G_AQ:G_AQ + AD], gains[:, L, G_AQ:G_AQ + AD], AD ** -0.5, None, ALU.mult))
                then(dve.tensor_scalar(gains[:, L, G_LQ:G_LQ + LQK], gains[:, L, G_LQ:G_LQ + LQK], LQK ** -0.5, None, ALU.mult))
            then(dve.memset(rt[:, :, :, :], 0.0))

            def mod(L):
                def columns_of(i):
                    s, half = i // 2, i % 2
                    o, free = take_out(dve, ("modT", L, i))
                    src = o[:, 0:8].rearrange("p (k g) -> p k g", g=2)
                    dst = modT[:, s, 4 * half:4 * half + 4, :]
                    if s in (1, 4):
                        g = normG[:, L, s // 4, 4 * half:4 * half + 4].unsqueeze(2).broadcast_to([P, 4, 2])
                        ins = dve.scalar_tensor_tensor(out=dst, in0=src, scalar=1.0, in1=g, op0=ALU.add, op1=ALU.mult)
                    else:
                        ins = dve.tensor_copy(dst, src)
                    ins.then_inc(free, 1)
                for i in range(12):
                    if i > 1:
                        b, n = plan.at[("modT", L, i - 2)]
                        dve.wait_ge(bank_full[b], n + 1)
                    dve.wait_ge(sem(f"modb_loaded{i % 2}"), 16 * (6 * L + i // 2 + 1))
                    o, free = take_out(dve, ("mod", L, i))
                    dve.tensor_tensor(MODROW[0:2, i % 2, :], o[0:2, :], MODB[0:2, i % 2, :], ALU.add).then_inc(free, 1)
                    if i:
                        columns_of(i - 1)
                columns_of(11)

            def norm(L, w):
                g0 = groups(L)[0] if w == "f" else 0
                dve.wait_ge(sem(f"squares_{L}{w}"), NT - 2 * g0)
                mean(L, f"x{w}", rs[:, 2 * g0:NT], ss[:, 2 * g0:NT], D)
                rstd(L, f"x{w}", rs[:, 2 * g0:NT])
                for t in range(2 * g0, NT):
                    dve.tensor_scalar(XN[:, t, :], X[:, t, :], rs[:, t:t + 1], None, ALU.mult).then_inc(sem(f"normed_{L}{w}"), 1)
                for k in range(1, KT, 2):
                    columns(dve, L, w, k, g0)

            def project(L):
                two = "p (s t) -> p s t"
                for h in range(8):
                    dve.wait_ge(sem(f"middle_tap{L}"), h + 1)
                    o, free = take_out(dve, ("conv", L, h))
                    src, dst = o[0:MD, :].rearrange(two, s=2), QK[0:MD, h, :].rearrange(two, s=2)
                    then(dve.scalar_tensor_tensor(out=dst[:, :, 1:256], in0=src[:, :, 0:255], scalar=convw[:, L, h, 0:1],
                                                  in1=dst[:, :, 1:256], op0=ALU.mult, op1=ALU.add))
                    dve.scalar_tensor_tensor(out=dst[:, :, 0:255], in0=src[:, :, 1:256], scalar=convw[:, L, h, 2:3],
                                             in1=dst[:, :, 0:255], op0=ALU.mult, op1=ALU.add).then_inc(free, 1)
                for s, w in enumerate(ROWS_OF_W):
                    for t in (1, 3):
                        o, free = take_out(dve, ("proj", L, s, t))
                        if w == W_GQA:
                            dve.tensor_copy(*paired(t, o))
                            dve.tensor_copy(PG[:, t, 384:512], o[:, 384:512]).then_inc(free, 1)
                        else:
                            dve.tensor_copy(PROJ[w][:, t, :], o[:, 0:w[1]]).then_inc(free, 1)

            def rope(xs, dim, cos_at, sin_at, heads_n, tmp):
                for i in range(2):
                    x, tm = xs(2 + i), tmp(i)
                    for q in range(2):
                        sin = cst[:, sin_at + i * dim:sin_at + (i + 1) * dim].rearrange("p (a b c) -> p a b c", a=2, b=2)[:, :, q, :]
                        xo = x.rearrange("p h (a b c) -> p h a b c", a=2, b=2)[:, :, :, 1 - q, :]
                        to = tm.rearrange("p h (a b c) -> p h a b c", a=2, b=2)[:, :, :, q, :]
                        for half in range(2):
                            ins = dve.tensor_tensor(to[:, :, half, :], xo[:, :, half, :],
                                                    sin[:, half, :].unsqueeze(1).broadcast_to([P, heads_n, dim // 4]), ALU.mult)
                    then(ins)
                    cos = cst[:, cos_at + i * dim:cos_at + (i + 1) * dim].unsqueeze(1).broadcast_to([P, heads_n, dim])
                    then(dve.tensor_tensor(x, x, cos, ALU.mult))
                    then(dve.tensor_tensor(x, x, tm, ALU.add))

            def prepare(L):
                for t in range(NT):
                    evacuated(dve, ("proj", L, 0, t))
                bias = gains[:, L, G_GB:G_GB + 16].unsqueeze(1).broadcast_to([P, NT, 16])
                then(dve.tensor_tensor(GA[:, :, :], PMO[:, :, 384:400], bias, ALU.add))
                f = GA[:, :, :].rearrange("p t (d x h) -> p t d x h", d=2, x=2)[:, :, :, 1, :]
                g = gtmp[:, :, :].rearrange("p t (d h) -> p t d h", d=2)
                for d in range(2):
                    ins = dve.scalar_tensor_tensor(out=g[:, :, d, :], in0=f[:, :, d, :], scalar=-1.0, in1=f[:, :, d, :],
                                                   op0=ALU.mult, op1=ALU.min)
                ins.then_inc(sem(f"gate_negated{L}"), 1)
                dve.wait_ge(sem(f"gate_log{L}"), 1)
                lf = LF[:, :, :].rearrange("p t (d h) -> p t d h", d=2)
                for d in range(2):
                    ins = dve.scalar_tensor_tensor(out=lf[:, :, d, :], in0=f[:, :, d, :], scalar=0.0, in1=g[:, :, d, :],
                                                   op0=ALU.min, op1=ALU.subtract)
                ins.then_inc(sem(f"gates_ready{L}"), 1)

                dve.wait_ge(sem(f"gqa_squares{L}"), 1)
                then(dve.tensor_reduce(gss[:, 0:32].rearrange("p (t h) -> p t h", t=NT),
                                       SQ[:, :, :].rearrange("p t (h d) -> p t h d", d=AD), AX.X, ALU.add))
                mean(L, "gqa", grs[:, 0:32], gss[:, 0:32], AD)
                rstd(L, "gqa", grs[:, 0:32])
                for t in range(NT):
                    evacuated(dve, ("proj", L, 1, t))
                heads_v = PG[:, :, :].rearrange("p t (h d) -> p t h d", d=AD)
                then(dve.tensor_tensor(heads_v, heads_v, grs[:, 0:32].rearrange("p (t h) -> p t h", t=NT).unsqueeze(3)
                                       .broadcast_to([P, NT, 8, AD]), ALU.mult))
                for h0, h1, at in ((0, AH, G_AQ), (AH, 8, G_AK)):
                    for t in range(NT):
                        ins = dve.tensor_tensor(heads_v[:, t, h0:h1, :], heads_v[:, t, h0:h1, :],
                                                gains[:, L, at:at + AD].unsqueeze(1).broadcast_to([P, h1 - h0, AD]), ALU.mult)
                then(ins)
                rope(lambda t: PG[:, t, :].rearrange("p (h d) -> p h d", d=AD), AD, C_COSA, C_SINA, 8,
                     lambda i: SQ[:, i, :].rearrange("p (h d) -> p h d", d=AD))
                then(dve.tensor_copy(den[:, 0:1], grs[:, 0:1]))
                dve.tensor_copy(den[:, 1:2], grs[:, 0:1]).then_inc(sem(f"gqa_ready{L}"), 1)

                ones = cst[0:4, C_ONE:C_ONE + 1]
                parts_f = [(slice(0, 512), None)]
                for d, (rows, ki, kf) in enumerate(((rows_f, 0, 1), (rows_b, 2, 3))):
                    fo, f_free = take_out(dve, ("gateT", L, kf))
                    io, i_free = take_out(dve, ("gateT", L, ki))
                    parts = ((0, 512),) if d == 0 else ((0, 256), (256, 512))

                    def seg(x, lo, hi):
                        return x[:, lo:hi] if d == 0 else x[:, lo:hi][:, ::-1]
                    for n, (lo, hi) in enumerate(parts):
                        init = 0.0 if n == 0 else rows[0:4, 0, 0:1]
                        then(dve.tensor_tensor_scan(seg(rows[0:4, 0, :], lo, hi), ones.broadcast_to([4, hi - lo]),
                                                    seg(fo[0:4, :], lo, hi), init, ALU.mult, ALU.add))
                    dve.tensor_copy(rinv[0:4, 0:1], fo[0:4, 0:1]).then_inc(f_free, 1)
                    dve.tensor_tensor(crow[0:4, d, :], io[0:4, :], rows[0:4, 0, :], ALU.subtract).then_inc(i_free, 1)
                    evacuated(dve, ("gateT", L, ki))
                    for n, (lo, hi) in enumerate(parts):
                        init = 0.0 if n == 0 else rows[0:4, 1, 0:1]
                        c = seg(crow[0:4, d, :], lo, hi)
                        then(dve.tensor_tensor_scan(seg(rows[0:4, 1, :], lo, hi), c, c, init, ALU.max, ALU.max))
                    dve.tensor_tensor(rows[0:4, 0, :], rows[0:4, 0, :], rows[0:4, 1, :], ALU.add).then_inc(sem(f"stabilisers{L}"), 1)

                for g in range(4):
                    o, free = take_out(dve, ("gqaT", L, g))
                    dve.tensor_copy(GT[:, g, :], o[:, :]).then_inc(free, 1)
                dve.wait_ge(sem(f"latent_squares{L}"), 1)
                dve.tensor_reduce(gss[:, 0:4], SQ[:, :, 0:256], AX.X, ALU.add)
                dve.tensor_reduce(gss[:, 4:8], SQ[:, :, 256:384], AX.X, ALU.add)
                then(dve.tensor_reduce(gss[:, 8:12], SQ[:, :, 384:416], AX.X, ALU.add))
                dve.tensor_scalar(grs[:, 0:4], gss[:, 0:4], 1.0 / QRANK, EPS, ALU.mult, ALU.add)
                dve.tensor_scalar(grs[:, 4:8], gss[:, 4:8], 1.0 / KVRANK, EPS, ALU.mult, ALU.add)
                mean(L, "latent", grs[:, 8:12], gss[:, 8:12], ROPE)
                rstd(L, "latent", grs[:, 0:12])
                for t in range(NT):
                    evacuated(dve, ("proj", L, 2, t))
                    evacuated(dve, ("proj", L, 3, t))
                for x, n, at in ((PAVCQ[:, :, 128:384], 256, 0), (PCKV[:, :, 0:128], 128, 4), (PCKV[:, :, 128:160], 32, 8)):
                    ins = dve.tensor_tensor(x, x, grs[:, at:at + 4].unsqueeze(2).broadcast_to([P, NT, n]), ALU.mult)
                ins.then_inc(sem(f"latent_ready{L}"), 1)
                dve.wait_ge(sem(f"latent_ready{L}"), 1)
                kr = PCKV[:, :, 128:160]
                then(dve.tensor_tensor(kr, kr, gains[:, L, G_LK + 64:G_LK + 96].unsqueeze(1).broadcast_to([P, NT, ROPE]), ALU.mult))
                rope(lambda t: PCKV[:, t, 128:160].unsqueeze(1), ROPE, C_COSL, C_SINL, 1,
                     lambda i: SQ[:, i, 0:32].unsqueeze(1))
                for t in range(NT):
                    o, free = take_out(dve, ("mlakv", L, t))
                    kv = o[:, :].rearrange("p (h d) -> p h d", h=LH)
                    dve.tensor_copy(KR[:, t, :, 64:96], PCKV[:, t, 128:160].unsqueeze(1).broadcast_to([P, LH, ROPE]))
                    dve.tensor_copy(KR[:, t, :, 0:64], kv[:, :, 0:64])
                    dve.tensor_copy(VM[:, t, :, :], kv[:, :, 64:128]).then_inc(free, 1)
                dve.wait_ge(sem(f"mla_squares{L}"), 1)
                sq = SQ[:, :, 0:384].rearrange("p t (h d) -> p t h d", h=LH)
                th = "p (t h) -> p t h"
                dve.tensor_reduce(gss[:, 0:16].rearrange(th, t=NT), sq[:, :, :, 0:64], AX.X, ALU.add)
                dve.tensor_reduce(gss[:, 16:32].rearrange(th, t=NT), sq[:, :, :, 64:96], AX.X, ALU.add)\
                    .then_inc(sem(f"mla_squares_read{L}"), 1)
                dve.wait_ge(sem(f"mla_squares{L}"), 2)
                sk = SQ[:, :, 0:256].rearrange("p t (h d) -> p t h d", h=LH)
                then(dve.tensor_reduce(gss[:, 32:48].rearrange(th, t=NT), sk, AX.X, ALU.add))
                dve.tensor_scalar(grs[:, 0:16], gss[:, 0:16], 1.0 / NOPE, EPS, ALU.mult, ALU.add)
                dve.tensor_scalar(grs[:, 16:32], gss[:, 16:32], 1.0 / ROPE, EPS, ALU.mult, ALU.add)
                mean(L, "mla", grs[:, 32:48], gss[:, 32:48], NOPE)
                rstd(L, "mla", grs[:, 0:48])
                for t in range(NT):
                    evacuated(dve, ("mlaq", L, t))
                for x, n, at in ((QR[:, :, :, 0:64], 64, 0), (QR[:, :, :, 64:96], 32, 16), (KR[:, :, :, 0:64], 64, 32)):
                    r = grs[:, at:at + 16].rearrange(th, t=NT)
                    for t in range(NT):
                        ins = dve.tensor_tensor(x[:, t], x[:, t], r[:, t, :].unsqueeze(2).broadcast_to([P, LH, n]), ALU.mult)
                then(ins)
                for t in range(NT):
                    dve.tensor_tensor(QR[:, t], QR[:, t], gains[:, L, G_LQ:G_LQ + LQK].unsqueeze(1).broadcast_to([P, LH, LQK]), ALU.mult)
                    ins = dve.tensor_tensor(KR[:, t, :, 0:64], KR[:, t, :, 0:64],
                                            gains[:, L, G_LK:G_LK + 64].unsqueeze(1).broadcast_to([P, LH, 64]), ALU.mult)
                then(ins)
                rope(lambda t: QR[:, t, :, 64:96], ROPE, C_COSL, C_SINL, LH,
                     lambda i: SQ[:, i, 0:128].rearrange("p (h d) -> p h d", h=LH))
                dve.tensor_copy(den[:, 0:1], grs[:, 0:1]).then_inc(sem(f"mla_ready{L}"), 1)
                for g in range(1, 8, 2):
                    o, free = take_out(dve, ("mlaH", L, g))
                    dve.tensor_copy(MT[0:LQK, g, :], o[0:LQK, :]).then_inc(free, 1)

            def heads(L):
                dve.wait_ge(sem(f"stab_exp{L}"), 1)
                seen = {"A": [], "M": []}

                def head_out(u, n):
                    kind, h, t = u
                    if kind == "A":
                        o, free = take_out(dve, ("O", L, u))
                        then(dve.reciprocal(rinv[:, 0:1], rsum[:, n % 4:n % 4 + 1]))
                        dve.tensor_scalar(OROW[:, t, MW + 64 * h:MW + 64 * (h + 1)], o[:, 0:64], rinv[:, 0:1], None, ALU.mult)\
                            .then_inc(free, 1)
                    else:
                        o, free = take_out(dve, ("O", L, u))
                        dve.tensor_copy(OROW[:, t, MD * h:MD * (h + 1)], o[:, 0:MD]).then_inc(free, 1)

                for u in mixer_units(L):
                    kind, h, t = u
                    nk = 256 if t < 2 else TOK
                    d = seen[kind]
                    if kind == "A":
                        o, _ = take_out(dve, ("S", L, u))
                        dve.tensor_reduce(nmax[:, 0:1], o[:, 0:nk], AX.X, ALU.max, negate=True).then_inc(sem(f"row_max{L}"), 1)
                    else:
                        o, free = take_out(dve, ("S", L, u))
                        evacuated(dve, ("CF", L, u))
                        dve.tensor_tensor_reduce(EF[:, 0:nk], EF[:, 0:nk], o[:, 0:nk], MD ** -0.5, 0.0, ALU.mult, ALU.add, den[:, 0:1])
                        evacuated(dve, ("CB", L, u))
                        dve.tensor_tensor_reduce(EB[:, 0:nk], EB[:, 0:nk], o[:, 0:nk], MD ** -0.5, 0.0, ALU.mult, ALU.add, den[:, 1:2])\
                            .then_inc(free, 1)
                        evacuated(dve, ("S", L, u))
                        then(dve.scalar_tensor_tensor(out=dabs[:, :], in0=den[:, :], scalar=-1.0, in1=den[:, :], op0=ALU.mult, op1=ALU.max))
                        then(dve.tensor_tensor(dabs[:, :], dabs[:, :], stab[:, 2:4, t, h], ALU.max))
                        then(dve.reciprocal(dabs[:, :], dabs[:, :]))
                        then(dve.tensor_scalar(EB[:, 0:nk], EB[:, 0:nk], dabs[:, 1:2], None, ALU.mult))
                        if d:
                            b, n = plan.at[("T", L, d[-1])]
                            dve.wait_ge(bank_full[b], n + 1)
                        dve.scalar_tensor_tensor(out=WT[:, 0:nk], in0=EF[:, 0:nk], scalar=dabs[:, 0:1], in1=EB[:, 0:nk],
                                                 op0=ALU.mult, op1=ALU.add).then_inc(sem(f"weights_ready{L}"), 1)
                    if len(d) > 1:
                        head_out(d[-2], len(d) - 2)
                    d.append(u)
                for d in seen.values():
                    head_out(d[-2], len(d) - 2)
                    head_out(d[-1], len(d) - 1)

            def out_project(L):
                t0 = query_tiles(L)[0]
                nt = NT - t0
                dve.wait_ge(sem(f"mlstm_squares{L}"), 1)
                then(dve.tensor_reduce(gss[:, 0:4 * nt].rearrange("p (t h) -> p t h", h=MH),
                                       SQ[:, t0:NT, 0:MW].rearrange("p t (h d) -> p t h d", h=MH), AX.X, ALU.add))
                mean(L, "mlstm", grs[:, 0:4 * nt], gss[:, 0:4 * nt], MD)
                rstd(L, "mlstm", grs[:, 0:4 * nt])
                x = OROW[:, t0:NT, 0:MW]
                for t in range(nt):
                    v = OROW[:, t0 + t, 0:MW].rearrange("p (h d) -> p h d", h=MH)
                    ins = dve.tensor_tensor(v, v, grs[:, 4 * t:4 * t + 4].unsqueeze(2).broadcast_to([P, MH, MD]), ALU.mult)
                then(ins)
                then(dve.tensor_tensor(x, x, gains[:, L, G_M:G_M + MW].unsqueeze(1).broadcast_to([P, nt, MW]), ALU.mult))
                dve.wait_ge(sem(f"out_gate{L}"), 1)
                dve.tensor_tensor(x, x, PMO[:, t0:NT, 0:MW], ALU.mult).then_inc(sem(f"mix_ready{L}"), 1)
                for k in range(1, KT, 2):
                    o, free = take_out(dve, ("outT", L, k))
                    dve.tensor_copy(HT[:, k, t0 * P:], o[:, t0 * P:]).then_inc(free, 1)
                for g in groups(L):
                    for half in range(2):
                        evacuated(dve, ("gateA", L, g, half))
                for c in range(2):
                    cols = slice(512 * c, 512 * (c + 1))
                    for t in query_tiles(L):
                        o, free = take_out(dve, ("out", L, c, t))
                        dve.tensor_tensor(SQ[:, t, :], o[:, :], GBC_A[:, t // 2, cols], ALU.mult).then_inc(free, 1)
                        evacuated(dve, ("out", L, c, t))
                        ins = dve.tensor_tensor(X[:, t, cols], X[:, t, cols], SQ[:, t, :], ALU.add)
                ins.then_inc(sem(f"x_updated_{L}f"), 1)

            def ffn():
                def hidden(s0, r):
                    b, n = ffn_place("G", s0)
                    dve.wait_ge(bank_free[b], r * FFN_STRIDE["G"] + (n + 1))
                    b, n = ffn_place("U", s0)
                    dve.wait_ge(bank_full[b], r * FFN_STRIDE["U"] + (n + 1))
                    dve.tensor_tensor(H[:, :], SIL[:, s0 % 2, :], bank[b][:, :], ALU.mult).then_inc(bank_free[b], 1)

                def add_up(s0, r, first):
                    for c in range(2):
                        b, n = ffn_place(f"Y{c}", s0)
                        dve.wait_ge(bank_full[b], r * FFN_STRIDE[f"Y{c}"] + (n + 1))
                        y = YACC[:, s0 % NT, 512 * c:512 * (c + 1)]
                        if first:
                            ins = dve.tensor_copy(y, bank[b][:, :])
                        else:
                            ins = dve.tensor_tensor(y, bank[b][:, :], y, ALU.add)
                        ins.then_inc(bank_free[b], 1)

                for s in range(NT):
                    hidden(s, 0)
                    if s:
                        add_up(s - 1, 0, True)
                then(dve.memset(YACC[:, NT - 1, :], 0.0))
                with dve.Fori(0, 3) as m:
                    for s in range(NT, 3 * NT):
                        hidden(s, m)
                        add_up(s - 1, m, False)
                add_up(NJ * NT - 1, 0, False)
                for half in range(2):
                    for g in range(2):
                        evacuated(dve, ("gateF", 0, g, half))
                evacuated(dve, ("Y", NJ * NT - 1, 1))
                for t in range(NT):
                    then(dve.tensor_tensor(YACC[:, t, :], YACC[:, t, :], GBC_F[0][:, t // 2, :], ALU.mult))
                    ins = dve.tensor_tensor(X[:, t, :], X[:, t, :], YACC[:, t, :], ALU.add)
                ins.then_inc(sem("x_updated_1a"), 1)

            def route():
                for t in range(2):
                    o, free = take_out(dve, ("router", t))
                    dve.tensor_copy(LG[:, t, :], o[:, 0:NE]).then_inc(free, 1)
                iota = cst[:, C_IOTA:C_IOTA + NE]
                for t in range(2):
                    evacuated(dve, ("router", t))
                    then(dve.max(MX[:, :], LG[:, t, :]))
                    then(dve.max_index(idx[:, :], MX[:, :], LG[:, t, :]))
                    then(dve.tensor_copy(IDXF[:, 2 * t:2 * t + 2], idx[:, 0:2]))
                    then(dve.tensor_tensor(wts[:, t:t + 1], MX[:, 1:2], MX[:, 0:1], ALU.subtract))
                dve.tensor_copy(TOT[:, 0:1], wts[:, 0:1]).then_inc(sem("expert_gap"), 1)
                dve.wait_ge(sem("expert_gap_exp"), 1)
                then(dve.tensor_scalar(wts[:, 2:4], wts[:, 0:2], 1.0, None, ALU.add))
                then(dve.reciprocal(wts[:, 2:4], wts[:, 2:4]))
                then(dve.tensor_tensor(wts[:, 0:2], wts[:, 0:2], wts[:, 2:4], ALU.mult))
                for t in range(2):
                    for c in range(2):
                        ins = dve.tensor_scalar(OH[:, c, :], iota, IDXF[:, 2 * t + c:2 * t + c + 1], None, ALU.is_equal)
                    then(ins)
                    dve.tensor_tensor(SELM[:, t, 0:NE], OH[:, 0, :], OH[:, 1, :], ALU.add)
                    then(dve.tensor_scalar(OH[:, 0, :], OH[:, 0, :], wts[:, 2 + t:3 + t], None, ALU.mult))
                    then(dve.scalar_tensor_tensor(out=COMB[:, t, 0:NE], in0=OH[:, 1, :], scalar=wts[:, t:t + 1],
                                                  in1=OH[:, 0, :], op0=ALU.mult, op1=ALU.add))
                dve.tensor_copy(TOT[:, 0:1], wts[:, 0:1]).then_inc(sem("routed"), 1)
                o, free = take_out(dve, ("pos",))
                dve.tensor_copy(POS[:, :, 0:NE], o[:, 0:2 * NE].rearrange("p (t e) -> p t e", t=2))
                then(dve.tensor_reduce(TOT[:, 1:2], o[:, 2 * NE:3 * NE], AX.X, ALU.max))
                then(dve.tensor_copy(TOT[:, 2:3], o[:, 0:1]))
                dve.tensor_copy(TOT[:, 3:4], o[:, 0:1]).then_inc(free, 1)
                dve.tensor_scalar(flag[:, :], TOT[:, 1:2], P + 0.5, None, ALU.is_gt).then_inc(sem("flag_ready"), 1)
                then(dve.memset(ACC[:, :, :], 0.0))

            def experts(p):
                def one_hot(dst, e, weight):
                    for t in range(2):
                        ins = dve.tensor_scalar(dst[:, t, :], cst[:, C_IOTA + p * P:C_IOTA + (p + 1) * P],
                                                POS[:, t, bass.ds(e, 1)], weight[:, t, bass.ds(e, 1)], ALU.is_equal, ALU.mult)
                    return ins

                def gathered(half, b, n):
                    dve.wait_ge(bank_full[b], n + 1)
                    for k in range(4):
                        f = 4 * half + k
                        ins = dve.tensor_scalar(XT[:, f, :], bank[b][:, k * P:(k + 1) * P], modT[:, 4, f, 1:2],
                                                modT[:, 3, f, 1:2], ALU.mult, ALU.add)
                    ins.then_inc(bank_free[b], 1)

                def scattered(i, b, n):
                    t, c = i // 2, i % 2
                    dve.wait_ge(bank_full[b], n + 1)
                    y = ACC[:, t, 512 * c:512 * (c + 1)]
                    dve.tensor_tensor(y, bank[b][:, :], y, ALU.add).then_inc(bank_free[b], 1)

                dve.memset(YROW[:, :], 0.0)
                dve.memset(SMT[:, :, :], 0.0).then_inc(sem("moe_cleared"), 1)
                one_hot(GM, 0, SELM).then_inc(sem("gather_ready"), 1)
                for half in range(2):
                    gathered(half, 5, moe_base(p, 5) - GA_PRO + half)
                with dve.Fori(0, NE) as e:
                    for j in range(NJ):
                        if j < 2:
                            scattered(2 * j, *moe_at(p, e, "SC", 2 * j))
                        b, n = moe_at(p, e, "G", j)
                        dve.wait_ge(bank_free[b], n + 1)
                        b, n = moe_at(p, e, "U", j)
                        dve.wait_ge(bank_full[b], n + 1)
                        dve.tensor_tensor(H[:, :], SIL[:, j % 2, :], bank[b][:, :], ALU.mult).then_inc(bank_free[b], 1)
                        if j < 2:
                            scattered(2 * j + 1, *moe_at(p, e, "SC", 2 * j + 1))
                        if j == 2:
                            one_hot(SM, e, COMB).then_inc(sem("scatter_ready"), 1)
                        if j == 4:
                            one_hot(GM, e + 1, SELM).then_inc(sem("gather_ready"), 1)
                    for half in range(2):
                        gathered(half, *moe_at(p, e, "GA", half))
                for i in range(4):
                    scattered(i, 5, moe_base(p, 5) + NE * MOE_USES[5] + i)

            def finish():
                for half in range(2):
                    evacuated(dve, ("gateF", 1, 1, half))
                for t in range(2):
                    then(dve.tensor_tensor(ACC[:, t, :], ACC[:, t, :], GBC_F[1][:, 1, :], ALU.mult))
                    dve.tensor_tensor(X[:, 2 + t, :], X[:, 2 + t, :], ACC[:, t, :], ALU.add).then_inc(sem("out_row_ready"), 1)

            for L in range(DEPTH):
                mod(L)
                norm(L, "a")
                project(L)
                prepare(L)
                heads(L)
                out_project(L)
                norm(L, "f")
                if L == 0:
                    ffn()
            route()
            experts(0)
            over = overflow(dve)
            with dve.If(over > 0):
                experts(1)
            then(dve.memset(SIL[:, 0, 0:1], 0.0))
            finish()


_INS = ['x', 'c', 'ctx', 'c_ctx', 'mod_w', 'mod_b', 'norm_mix', 'norm_ffn', 'w_in', 'm_conv', 'm_gate_b', 'm_norm',
        'a_qnorm', 'a_knorm', 'l_cq_norm', 'l_ckv_norm', 'l_wuq', 'l_wukv', 'l_qnorm', 'l_knorm', 'w_out',
        'ffn_wg', 'ffn_wu', 'ffn_wd', 'moe_router', 'moe_wg', 'moe_wu', 'moe_wd']


def kernel(**inputs):
    import numpy as _np
    import concourse.bacc as _bacc
    from concourse.bass_utils import run_bass_kernel_spmd as _run

    nc = _bacc.Bacc("TRN2", target_bir_lowering=False, num_devices=1)
    arrays, args = {}, {}
    for name in _INS:
        v = _np.ascontiguousarray(inputs[name])
        arrays[f"in_{name}"] = v
        args[name] = nc.dram_tensor(f"in_{name}", v.shape, F32, kind="ExternalInput").ap()
    arrays["in_constants"] = constants()
    consts = nc.dram_tensor("in_constants", (P, C_END), F32, kind="ExternalInput").ap()
    out = nc.dram_tensor("out", (1, 256, D), F32, kind="ExternalOutput").ap()
    build(nc, args, consts, out)
    r = _run(nc, [arrays], core_ids=[0])
    return r.results[0]["out"]
```

```python
from contextlib import ExitStack

import numpy as np
import concourse.bass as bass
from concourse import mybir

F32 = mybir.dt.float32
F32R = mybir.dt.float32r
I32 = mybir.dt.int32
U32 = mybir.dt.uint32
ALU = mybir.AluOpType
ACT = mybir.ActivationFunctionType
AX = mybir.AxisListType

P = 128
NT = 4
TOK = NT * P
D = 1024
KT = D // P
EPS = 1e-6
DEPTH = 2
MH, MD = 4, 96
MW = MH * MD
AH, AKV, AD = 6, 2, 64
LH, NOPE, ROPE = 4, 64, 32
LQK = NOPE + ROPE
QRANK, KVRANK = 256, 128
FF = 3584
NE = 8
FS = 512
NJ = FF // FS
NEG = -1e30
RING = 6
SLOT = 4 * 512
PAIRS = 3

C_ID, C_SEL, C_MF, C_MB = 0, 128, 640, 1024
C_COSA, C_SINA, C_COSL, C_SINL = 1408, 1536, 1664, 1728
C_TRI, C_ONE, C_IOTA, C_END = 1792, 1920, 2048, 2304
G_M, G_AQ, G_AK, G_LQ, G_LK, G_GB, G_END = 0, 384, 448, 512, 608, 704, 720
W_Q, W_K, W_OG, W_GQA, W_AVCQ, W_CKV, W_MV = (0, 384), (384, 384), (1152, 400), (1552, 512), (2064, 384), (2448, 160), (768, 384)
ROWS_OF_W = (W_OG, W_GQA, W_AVCQ, W_CKV, W_MV)


def constants():
    c = np.zeros((P, C_END), np.float32)
    c[:, C_ID:C_ID + P] = np.eye(P)
    for h in range(4):
        c[h, C_SEL + h * P:C_SEL + (h + 1) * P] = 1
    t, s = np.arange(P)[:, None], np.arange(P)[None, :]
    c[:, C_MF + 128:C_MF + 256] = np.where(s <= t, 0, NEG)
    c[:, C_MF + 256:C_MF + 384] = NEG
    c[:, C_MB:C_MB + 128] = NEG
    c[:, C_MB + 128:C_MB + 256] = np.where(s >= t, 0, NEG)
    tok = np.arange(256)
    rows, cols = (tok // 64).astype(np.float32), (tok % 64).astype(np.float32)
    for dim, cc, cs in ((AD, C_COSA, C_SINA), (ROPE, C_COSL, C_SINL)):
        nf = dim // 4
        inv = (np.float32(10000.0) ** (-np.arange(nf, dtype=np.float32) / np.float32(nf))).astype(np.float32)
        ar, ac = rows[:, None] * inv, cols[:, None] * inv
        ang = np.concatenate([ar, ar, ac, ac], -1)
        sign = np.tile(np.repeat(np.array([-1.0, 1.0], np.float32), nf), 2)
        cos, sin = np.cos(ang), np.sin(ang) * sign
        for i in range(2):
            c[:, cc + i * dim:cc + (i + 1) * dim] = cos[i * P:(i + 1) * P]
            c[:, cs + i * dim:cs + (i + 1) * dim] = sin[i * P:(i + 1) * P]
    c[:, C_TRI:C_TRI + P] = t < s
    c[:, C_ONE:C_ONE + P] = 1
    c[:, C_IOTA:C_IOTA + 256] = np.arange(256)
    return c


class BankPlan:

    def __init__(self):
        self.count = [0] * 8
        self.at = {}

    def add(self, name, bank):
        self.at[name] = (bank, self.count[bank])
        self.count[bank] += 1


def query_tiles(layer):
    return [0, 1, 2, 3] if layer == 0 else [2, 3]


def mixer_units(layer):
    att = [("A", h, t) for t in query_tiles(layer) for h in range(AH + LH)]
    mem = [("M", h, t) for t in query_tiles(layer) for h in range(MH)]
    out = []
    for i, u in enumerate(att):
        out.append(u)
        if (i + 1) * len(mem) // len(att) > i * len(mem) // len(att):
            out.append(mem.pop(0))
    return out + mem


def plan_banks():
    plan = BankPlan()
    for L in range(DEPTH):
        for i in range(12):
            plan.add(("mod", L, i), i % 2)
            if i:
                plan.add(("modT", L, i - 1), 2 + (i - 1) % 2)
        plan.add(("modT", L, 11), 3)
        for k in range(KT):
            plan.add(("norm", L, "a", k), k % 4)
        for h in range(8):
            plan.add(("conv", L, h), (h + 4) % 8)
        for s in range(len(ROWS_OF_W)):
            for t in range(NT):
                plan.add(("proj", L, s, t), 4 * ((s + 1) % 2) + t)
        for g in range(4):
            plan.add(("gateT", L, g), 4 + g)
        for g in range(4):
            plan.add(("gqaT", L, g), g)
        plan.add(("stab", L), 7)
        for g in range(3):
            plan.add(("mlaT", L, g), 4 + g)
        for t in range(NT):
            plan.add(("mlaq", L, t), 2 * (t % 2))
            plan.add(("mlakv", L, t), 2 * (t % 2) + 1)
        for g in range(8):
            plan.add(("mlaH", L, g), g)
        for unit in mixer_units(L):
            for part, b in ((("S", 0), ("T", 1), ("O", 2)) if unit[0] == "A" else
                            (("CF", 3), ("CB", 4), ("S", 5), ("T", 6), ("O", 7))):
                plan.add((part, L, unit), b)
        gs = (0, 1) if L == 0 else (1,)
        for k in range(KT):
            plan.add(("outT", L, k), k % 4)
        for g in gs:
            for half in range(2):
                plan.add(("gateA", L, g, half), 4 + half)
        for half in range(2):
            for t in query_tiles(L):
                plan.add(("out", L, half, t), 4 * half + t)
        for k in range(KT):
            plan.add(("norm", L, "f", k), k % 4)
        if L == 0:
            for j in range(NJ):
                for kind in ("G", "U", "HT", "Y0", "Y1"):
                    for t in range(NT):
                        plan.add((kind, j, t), (0 if kind in ("G", "HT") else 4) + t)
            for g in gs:
                for half in range(2):
                    plan.add(("gateF", L, g, half), 4 + half)
        else:
            for t in range(2):
                plan.add(("router", t), 4 + t)
            plan.add(("pos",), 4)
            for half in range(2):
                plan.add(("gateF", L, 1, half), 6 + half)
    return plan


MOE_USES = {0: 4, 1: 3, 2: 4, 3: 3, 4: 7, 5: 7, 6: 1, 7: 1}


def moe_place(name):
    kind, i = name
    if kind == "G":
        return i % 2, i // 2
    if kind == "U":
        return 2 + i % 2, i // 2
    if kind == "HT":
        return 4, i
    if kind == "SC":
        return 5, i
    if kind == "ST":
        return 5, 4
    if kind == "GA":
        return 5, 5 + i
    return 6 + i, 0


def moe_tiles():
    out = []
    for j in range(NJ):
        out += [("g", j, 0), ("g", j, 1), ("u", j, 0), ("u", j, 1)]
        if j:
            out += [("d", j - 1, 0), ("d", j - 1, 1)]
    return out + [("d", NJ - 1, 0), ("d", NJ - 1, 1)]


def build(nc, a, consts, out):
    plan = plan_banks()
    tiles = moe_tiles()
    PER = len(tiles)
    assert PER % RING == 0

    with ExitStack() as ctx:
        def sb(name, shape, dt=F32):
            return ctx.enter_context(nc.sbuf_tensor(name, shape, dt))

        sems = {}

        def sem(name):
            if name not in sems:
                sems[name] = ctx.enter_context(nc.semaphore(name))
            return sems[name]

        places = {}

        def placed_sb(name, shape):
            t = sb(name, shape)
            places[name] = nc.sbuf_base - 4 * int(np.prod(shape[1:]))
            return t

        def over(name, under, at, shape):
            return nc.alloc_sbuf_tensor_at(name, shape, F32R, offset=places[under] + 4 * at)

        ring = placed_sb("ring", [P, RING * SLOT])
        spare = placed_sb("spare", [P, SLOT])
        mix = placed_sb("mix", [P, 7 * SLOT])
        X = sb("X", [P, NT, D])
        hT = placed_sb("hT", [P, KT * TOK])
        bigA = placed_sb("bigA", [P, NT * D])
        bigB = placed_sb("bigB", [P, 8 * 512])
        cst = sb("cst", [P, C_END])
        gains = sb("gains", [P, DEPTH, G_END])
        scr = placed_sb("scr", [P, 2048])
        crow = sb("crow", [4, 2, 512])
        small = sb("small", [P, 360])
        modT = sb("modT", [P, 6, KT, 2])
        cvec = sb("cvec", [P, KT, 2])
        convw = sb("convw", [MD, DEPTH, 8, 3])
        idx = sb("idx", [P, 8], U32)
        flag = sb("flag", [P, 1], I32)

        def view(t, at, *dims):
            n = int(np.prod(dims))
            v = t[:, at:at + n]
            if len(dims) == 1:
                return v
            if len(dims) == 2:
                return v.rearrange("p (a b) -> p a b", a=dims[0])
            return v.rearrange("p (a b c) -> p a b c", a=dims[0], b=dims[1])

        PMO = view(mix, 0, NT, 400)
        PG = view(mix, 1600, NT, 512)
        PAVCQ = view(mix, 3648, NT, 384)
        PCKV = view(mix, 5184, NT, 160)
        PMV = view(mix, 5824, NT, 384)
        QK = view(mix, 7360, 8, TOK)
        GT = view(mix, 11456, 4, TOK)
        GA = view(mix, 13504, NT, 16)
        LF = view(mix, 13568, NT, 8)
        gtmp = view(mix, 13632, NT, 8)
        assert 13632 + 64 <= 7 * SLOT
        PROJ = {W_OG: PMO, W_GQA: PG, W_AVCQ: PAVCQ, W_CKV: PCKV, W_MV: PMV}
        HT = view(hT, 0, KT, TOK)
        VM = view(hT, 0, NT, LH, 64)
        CT = view(hT, 1024, 3, TOK)
        PA = view(hT, 1024, 2, 512)
        PT = view(hT, 2048, 512)
        EF = view(hT, 2560, 512)
        EB = view(hT, 3072, 512)
        WT = view(hT, 3584, 512)
        PTM = view(mix, 1600, 512)
        XN = view(bigA, 0, NT, D)
        OROW = XN
        QR = view(bigA, 0, NT, LH, LQK)
        KR = view(bigA, 1536, NT, LH, LQK)
        rows_f = view(bigA, 3072, 2, 512)
        rows_b = view(hT, 2560, 2, 512)
        MT = view(bigB, 0, 8, TOK)
        YACC = view(bigA, 0, NT, D)
        GBC_A = view(mix, 0, 2, D)
        TMPX = view(mix, 2048, 2, 512)
        TMPK = view(mix, 12288, 2, 512)
        ACC = view(bigB, 0, 2, D)
        XTF = view(bigB, 2048, KT, P)
        YROW = view(bigB, 3072, D)
        GM = view(bigA, 0, 2, P)
        SM = view(bigA, 256, 2, P)
        SMT = view(bigA, 512, 2, P)
        GBC_F = view(hT, 0, 2, D)
        SQ = view(scr, 0, NT, 512)
        SIL = view(scr, 0, 2, 512)
        H = view(scr, 1024, 512)
        SILF = view(scr, 0, NT, 512)
        MODROW = view(scr, 0, 2, 512)
        MODB = view(scr, 1024, 2, 512)
        ident = cst[:, C_ID:C_ID + P]

        HH, HL = over("HH", "hT", 0, [P, KT, TOK]), over("HL", "bigB", 0, [P, KT, TOK])
        TH, TL = over("TH", "mix", 12288, [P, NT, 512]), over("TL", "spare", 0, [P, NT, 512])
        pairs = {"A": (over("WAH", "spare", 0, [P, SLOT]), over("WAL", "scr", 0, [P, SLOT])),
                 "B": (over("WBH", "bigA", 0, [P, SLOT]), over("WBL", "bigA", SLOT, [P, SLOT]))}
        for i in range(PAIRS):
            pairs[i] = (over(f"W{i}H", "mix", 2 * SLOT * i, [P, SLOT]), over(f"W{i}L", "mix", 2 * SLOT * i + SLOT, [P, SLOT]))
        XTH, XTL = TH[:, 2:4, :].rearrange("p a (b c) -> p (a b) c", c=P), TL[:, 2:4, :].rearrange("p a (b c) -> p (a b) c", c=P)

        at_small = [0]

        def tiny(n):
            at_small[0] += n
            assert at_small[0] <= 360
            return small[:, at_small[0] - n:at_small[0]]

        normG = tiny(32).rearrange("p (l w k) -> p l w k", l=2, w=2)
        cqG = tiny(6).rearrange("p (l k) -> p l k", l=2)
        ss, rs = tiny(8), tiny(4)
        gss = tiny(48)
        grs = tiny(48)
        nmax, rsum, rinv = tiny(1), tiny(4), tiny(1)
        den = tiny(2)
        dabs = tiny(2)
        stab = tiny(64).rearrange("p (k t h) -> p k t h", k=4, t=4)
        LG = tiny(16).rearrange("p (t e) -> p t e", t=2)
        RT = tiny(64).rearrange("p (k e) -> p k e", k=8)
        MX, IDXF = tiny(8), tiny(4)
        wts = tiny(4)
        TOT = tiny(8)
        rt = sb("rt", [P, 3, 2, 9])
        SELM, COMB, POS = rt[:, 0], rt[:, 1], rt[:, 2]
        OH = view(scr, 0, 2, 8)

        bank = [ctx.enter_context(nc.psum_tensor(f"bank{b}", [P, 512], F32)) for b in range(8)]
        bank_full = [sem(f"bank_full{b}") for b in range(8)]
        bank_free = [sem(f"bank_free{b}") for b in range(8)]
        slot_full = [sem(f"slot_full{s}") for s in range(RING)]
        tile_used = sem("tile_used")
        split_hi, split_lo = sem("split_hi"), sem("split_lo")

        def take_out(eng, name):
            b, n = plan.at[name]
            eng.wait_ge(bank_full[b], n + 1)
            return bank[b], bank_free[b]

        def evacuated(eng, name):
            b, n = plan.at[name]
            eng.wait_ge(bank_free[b], n + 1)

        FFN_STRIDE = {"G": 2, "HT": 2, "U": 3, "Y0": 3, "Y1": 3}

        def ffn_at(kind, j, t):
            b, n = plan.at[(kind, 0, t)]
            return b, j * FFN_STRIDE[kind] + n

        SC_PER, GA_PRO = 4, 2

        def moe_base(p, b):
            per_pass = NE * MOE_USES[b] + ((GA_PRO + SC_PER) if b == 5 else 0)
            return plan.count[b] + p * per_pass + (GA_PRO if b == 5 else 0)

        def moe_at(p, e, kind, i=0):
            b, k = moe_place((kind, i))
            return b, e * MOE_USES[b] + (moe_base(p, b) + k)

        loads, freed, splits = [], [], []
        used = [0]

        def kn(ap, k0, nk, c0, n):
            return ap[k0 * P:(k0 + nk) * P, c0:c0 + n].rearrange("(k p) n -> p k n", p=P)

        def load(src, nk, n, last, pair=None):
            if last is None:
                used[0] += 1
            free = ("product", last) if last else ("used", used[0])
            if pair is None:
                freed.append(free)
            else:
                splits.append((len(loads), pair, free))
                freed.append(("split", len(splits)))
            loads.append((len(loads) % RING, src, nk, n))

        starts = {}
        for L in range(DEPTH):
            for i in range(12):
                for half in range(2):
                    load(kn(a["mod_w"][L], 4 * half, 4, 512 * i, 512), 4, 512, ("mod", L, i))
            starts["in", L] = len(splits)
            for s, (c0, n) in enumerate((W_Q, W_K) + ROWS_OF_W):
                last = ("conv", L, 4 * s + 3) if s < 2 else ("proj", L, s - 2, NT - 1)
                for half in range(2):
                    load(kn(a["w_in"][L], 4 * half, 4, c0, n), 4, n, last if half else None, "AB"[half])
            load(kn(a["l_wuq"][L], 0, 2, 0, LH * LQK), 2, LH * LQK, ("mlaq", L, NT - 1))
            load(kn(a["l_wukv"][L], 0, 1, 0, 512), 1, 512, ("mlakv", L, NT - 1))
            starts["out", L] = len(splits)
            for c in range(2):
                for half in range(2):
                    load(kn(a["w_out"][L], 4 * half, 4, 512 * c, 512), 4, 512, ("out", L, c, NT - 1) if half else None, "AB"[half])
            if L == 0:
                starts["ffn"] = len(splits)
                ffn_from = len(loads)
                for j in range(NJ):
                    for n, (w, kind) in enumerate((("ffn_wg", "G"), ("ffn_wu", "U"))):
                        for half in range(2):
                            load(kn(a[w][0], 4 * half, 4, FS * j, FS), 4, FS, (kind, j, NT - 1) if half else None, (2 * n + half) % PAIRS)
                    for c in range(2):
                        load(kn(a["ffn_wd"][0], 4 * j, 4, 512 * c, 512), 4, 512, (f"Y{c}", j, NT - 1), (4 + c) % PAIRS)
                ffn_to = len(loads)
        assert PER % PAIRS == 0 and 6 % PAIRS == 0 and RING == 6
        N0, M0, U0 = len(loads), len(splits), used[0]
        slot_uses = [0] * RING
        use_of = []
        for slot, *_ in loads:
            use_of.append(slot_uses[slot])
            slot_uses[slot] += 1
        first_slot = N0 % RING

        def slot_ap(slot, nk, n):
            return view(ring, slot * SLOT, nk * n).rearrange("p (k n) -> p k n", k=nk)

        def pair_ap(pair, nk, n):
            return [x[:, 0:nk * n].rearrange("p (k n) -> p k n", k=nk) for x in pairs[pair]]

        def is_free(eng, free):
            kind, what = free
            if kind == "product":
                b, n = plan.at[what]
                eng.wait_ge(bank_full[b], n + 1)
            elif kind == "used":
                eng.wait_ge(tile_used, what)
            else:
                eng.wait_ge(split_lo, what)

        moe_used = [m == "d" and j < NJ - 1 or m != "d" and c == 0 for m, j, c in tiles]
        USED_PER = sum(moe_used)

        def moe_src(e, tile):
            m, j, c = tile
            w = {"g": "moe_wg", "u": "moe_wu", "d": "moe_wd"}[m]
            w = a[w][0].rearrange("e r c -> (e r) c")
            if m == "d":
                src = w[bass.ds(e * FF + FS * j, FS), 512 * c:512 * (c + 1)]
            else:
                src = w[bass.ds(e * D + 512 * c, 512), FS * j:FS * (j + 1)]
            return src.rearrange("(k p) n -> p k n", p=P)

        def moe_left(eng, p, e, i):
            m, j, c = tiles[i]
            if moe_used[i]:
                eng.wait_ge(tile_used, e * USED_PER + (U0 + p * NE * USED_PER + sum(moe_used[:i + 1])))
            else:
                b, n = moe_at(p, e, {"g": "G", "u": "U", "d": "Y"}[m], j if m != "d" else c)
                eng.wait_ge(bank_full[b], n + 1)

        def tile_no(p, e, i):
            return e * PER + (M0 + p * NE * PER + i)

        def moe_slot(p, e, i):
            slot = (first_slot + i) % RING
            return slot, e * (16 * PER // RING) + 16 * (slot_uses[slot] + p * NE * (PER // RING) + i // RING + 1)

        def round_tile(act, hi, raw):
            act.activation(hi, raw, ACT.Copy).then_inc(split_hi, 1)

        def rest_tile(dve, n, hi, lo, raw):
            dve.wait_ge(split_hi, n)
            dve.tensor_tensor(lo, raw, hi.bitcast(F32), ALU.subtract).then_inc(split_lo, 1)

        def static_split(eng, n):
            tile, pair, _ = splits[n]
            slot, _, nk, w = loads[tile]
            hi, lo = pair_ap(pair, nk, w)
            raw = slot_ap(slot, nk, w)
            if eng is rest:
                rest_tile(nc.vector, n + 1, hi, lo, raw)
                return
            before = [m for m in range(n) if splits[m][1] == pair]
            if before:
                is_free(nc.scalar, splits[before[-1]][2])
            nc.scalar.wait_ge(slot_full[slot], 16 * (use_of[tile] + 1))
            round_tile(nc.scalar, hi, raw)

        rest = "VectorE"

        def ffn_split(eng, j, i):
            slot = (ffn_from + i) % RING
            hi, lo = pair_ap(i % PAIRS, 4, 512)
            raw = slot_ap(slot, 4, 512)
            if eng is rest:
                rest_tile(nc.vector, j * 6 + (starts["ffn"] + i + 1), hi, lo, raw)
                return
            nc.scalar.wait_ge(slot_full[slot], j * 16 + 16 * (use_of[ffn_from + i] + 1))
            round_tile(nc.scalar, hi, raw)

        def ffn_left(act, j, i):
            if i in (0, 2):
                act.wait_ge(tile_used, j * 2 + (splits[starts["ffn"] + i][2][1]))
            else:
                b, n = ffn_at({1: "G", 3: "U", 4: "Y0", 5: "Y1"}[i], j, NT - 1)
                act.wait_ge(bank_full[b], n + 1)

        def moe_split(eng, p, e, i):
            hi, lo = pair_ap(i % PAIRS, 4, 512)
            slot, landed = moe_slot(p, e, i)
            raw = slot_ap(slot, 4, 512)
            if eng is rest:
                rest_tile(nc.vector, tile_no(p, e, i) + 1, hi, lo, raw)
                return
            nc.scalar.wait_ge(slot_full[slot], landed)
            round_tile(nc.scalar, hi, raw)

        def overflow(eng):
            eng.wait_ge(sem("flag_ready"), 1)
            return eng.value_load(flag[0:1, 0:1], min_val=0, max_val=1)

        def groups(L):
            return (0, 1) if L == 0 else (1,)

        def paired(t, o):
            return (PG[:, t, 0:384].rearrange("p (n g d) -> p g n d", g=AKV, d=AD),
                    o[:, 0:384].rearrange("p (g n d) -> p g n d", g=AKV, d=AD))

        def modulated(eng, to, o, L, w, k, g0):
            shift, scale = (0, 1) if w == "a" else (3, 4)
            for g in range(g0, 2):
                cols = slice(256 * g, 256 * (g + 1))
                sc, sh = modT[:, scale, k, g:g + 1], modT[:, shift, k, g:g + 1]
                if eng is nc.scalar:
                    ins = eng.activation(to[:, cols], o[:, cols], ACT.Identity, scale=sc, bias=sh)
                else:
                    ins = eng.tensor_scalar(to[:, cols], o[:, cols], sc, sh, ALU.mult, ALU.add)
            return ins

        block = ctx.enter_context(nc.Block())

        @block.sync
        def _(sp):
            def fill(n):
                slot, src, nk, w = loads[n]
                if n >= RING:
                    is_free(sp, freed[n - RING])
                sp.dma_start(slot_ap(slot, nk, w), src).then_inc(slot_full[slot], 16)

            for n in range(ffn_from + 6):
                fill(n)
            wg, wu, wd = a["ffn_wg"][0], a["ffn_wu"][0], a["ffn_wd"][0]
            with sp.Fori(1, NJ) as j:
                for i in range(6):
                    slot = (ffn_from + i) % RING
                    sp.wait_ge(split_lo, (j - 1) * 6 + (starts["ffn"] + i + 1))
                    if i < 4:
                        src = (wg, wu)[i // 2][512 * (i % 2):512 * (i % 2 + 1), bass.ds(j * FS, FS)]
                    else:
                        src = wd[bass.ds(j * FS, FS), 512 * (i % 2):512 * (i % 2 + 1)]
                    sp.dma_start(slot_ap(slot, 4, 512), src.rearrange("(k p) n -> p k n", p=P)).then_inc(slot_full[slot], 16)
            for n in range(ffn_to, len(loads)):
                fill(n)

            def expert(p, e, i):
                slot, _ = moe_slot(p, e, i)
                sp.dma_start(slot_ap(slot, 4, 512), moe_src(e, tiles[i])).then_inc(slot_full[slot], 16)

            def experts(p):
                for i in range(RING):
                    if p:
                        sp.wait_ge(split_lo, tile_no(0, NE - 1, PER - RING + i) + 1)
                    else:
                        is_free(sp, freed[N0 - RING + i])
                    expert(p, 0, i)

                def rest_of(e, n):
                    for i in range(RING, n):
                        sp.wait_ge(split_lo, tile_no(p, e, i - RING) + 1)
                        expert(p, e + i // PER, i % PER)
                with sp.Fori(0, NE - 1) as e:
                    rest_of(e, PER + RING)
                rest_of(NE - 1, PER)

            experts(0)
            over = overflow(sp)
            with sp.If(over > 0):
                experts(1)
            for t in range(2):
                sp.wait_ge(sem("out_row_ready"), t + 1)
                sp.dma_start(out[0, t * P:(t + 1) * P, :], X[:, 2 + t, :]).then_inc(sem("stored"), 16)
            sp.wait_ge(sem("stored"), 32)

        @block.gpsimd
        def _(pool):
            with nc.allow_non_contiguous_dma("small parameters"):
                pool.dma_start(cst[:, :], consts).then_inc(sem("consts_loaded"), 16)
                for i in range(2):
                    pool.dma_start(MODB[0:2, i, :], a["mod_b"][0, 512 * i:512 * (i + 1)].partition_broadcast(2))\
                        .then_inc(sem(f"modb_loaded{i}"), 16)
                for L in range(DEPTH):
                    for w, name in enumerate(("norm_mix", "norm_ffn")):
                        pool.dma_start(normG[:, L, w, :], a[name][L].rearrange("(k p) -> p k", p=P)).then_inc(sem("params_loaded"), 16)
                    pool.dma_start(cqG[:, L, 0:2], a["l_cq_norm"][L].rearrange("(k p) -> p k", p=P)).then_inc(sem("params_loaded"), 16)
                    pool.dma_start(cqG[:, L, 2:3], a["l_ckv_norm"][L].rearrange("(k p) -> p k", p=P)).then_inc(sem("params_loaded"), 16)
                    for at, name, n in ((G_M, "m_norm", MW), (G_AQ, "a_qnorm", AD), (G_AK, "a_knorm", AD),
                                        (G_LQ, "l_qnorm", LQK), (G_LK, "l_knorm", LQK), (G_GB, "m_gate_b", 16)):
                        pool.dma_start(gains[:, L, at:at + n], a[name][L].partition_broadcast(P)).then_inc(sem("params_loaded"), 16)
                    for h in range(8):
                        pool.dma_start(convw[:, L, h, :], a["m_conv"][L, :, h * MD:(h + 1) * MD].rearrange("k c -> c k"))\
                            .then_inc(sem("params_loaded"), 16)
                pool.dma_start(RT[:, :, :], a["moe_router"][0].rearrange("(k p) e -> p k e", p=P)).then_inc(sem("params_loaded"), 16)
                for L in range(DEPTH):
                    for i in range(12):
                        if L == 0 and i < 2:
                            continue
                        if i < 2:
                            evacuated(pool, ("Y1", NJ - 1, NT - 1))
                        else:
                            evacuated(pool, ("mod", L, i - 2))
                        pool.dma_start(MODB[0:2, i % 2, :], a["mod_b"][L, 512 * i:512 * (i + 1)].partition_broadcast(2))\
                            .then_inc(sem(f"modb_loaded{i % 2}"), 16)
        PARAMS = 16 * (DEPTH * (2 + 2 + 6 + 8) + 1)

        @block.tensor
        def _(pe):
            taken = [0]

            def tile():
                n = taken[0]
                taken[0] += 1
                slot, _, nk, w = loads[n]
                pe.wait_ge(slot_full[slot], 16 * (use_of[n] + 1))
                return slot_ap(slot, nk, w)

            split_taken = [0]

            def split_tile():
                n = split_taken[0]
                split_taken[0] += 1
                tile, pair, _ = splits[n]
                _, _, nk, w = loads[tile]
                taken[0] = tile + 1
                pe.wait_ge(split_lo, n + 1)
                return pair_ap(pair, nk, w)

            def three(o, x, w, start, stop):
                pe.matmul(o, x[0], w[0], start=start, stop=False)
                pe.matmul(o, x[0], w[1], start=False, stop=False)
                return pe.matmul(o, x[1], w[0], start=False, stop=stop)

            def product(name):
                b, n = plan.at[name]
                if n:
                    pe.wait_ge(bank_free[b], n)
                return bank[b], bank_full[b]

            def mod(L):
                def turn(i):
                    evacuated(pe, ("mod", L, i))
                    o, full = product(("modT", L, i))
                    for k in range(4):
                        mm = pe.transpose(o[:, 2 * k:2 * k + 2], MODROW[0:2, i % 2, k * P:(k + 1) * P], ident[0:2, 0:2])
                    mm.then_inc(full, 1)
                for i in range(12):
                    o, full = product(("mod", L, i))
                    for half in range(2):
                        w = tile()
                        for k in range(4):
                            kk = 4 * half + k
                            mm = pe.matmul(o[0:2, :], cvec[:, kk, :], w[:, k, :], start=kk == 0, stop=kk == KT - 1)
                    mm.then_inc(full, 1)
                    if i:
                        turn(i - 1)
                turn(11)

            def norm(L, w):
                ts = [t for g in (groups(L) if w == "f" else (0, 1)) for t in (2 * g, 2 * g + 1)]
                pe.wait_ge(sem(f"normed_{L}{w}"), len(ts))
                for k in range(KT):
                    o, full = product(("norm", L, w, k))
                    for t in ts:
                        mm = pe.transpose(o[:, t * P:(t + 1) * P], XN[:, t, k * P:(k + 1) * P], ident)
                    mm.then_inc(full, 1)

            def columns_ready(L, kind, *w):
                evacuated(pe, (kind, L, *w, KT - 2))
                evacuated(pe, (kind, L, *w, KT - 1))

            def features(k, cols):
                return HH[:, k, cols], HL[:, k, cols]

            def project(L):
                pe.wait_ge(sem(f"features_{L}a"), KT)
                for c in range(2):
                    banks = [product(("conv", L, 4 * c + h)) for h in range(4)]
                    for half in range(2):
                        w = split_tile()
                        for h, (o, full) in enumerate(banks):
                            for k in range(4):
                                cols = slice(h * MD, (h + 1) * MD)
                                x, y = (w[0][:, k, cols], w[1][:, k, cols]), features(4 * half + k, slice(0, TOK))
                                mm = three(o[0:MD, :], x, y, half + k == 0, half + k == 4)
                            if half:
                                mm.then_inc(full, 1)
                        if not half:
                            mm.then_inc(tile_used, 1)
                for s, (_, n) in enumerate(ROWS_OF_W):
                    rows_product([("proj", L, s, t) for t in range(NT)], range(NT), n)

            def rows_product(names, ts, n):
                banks = [product(name) for name in names]
                for half in range(2):
                    w = split_tile()
                    for t, (o, full) in zip(ts, banks):
                        for k in range(4):
                            mm = three(o[:, 0:n], features(4 * half + k, slice(t * P, (t + 1) * P)),
                                       (w[0][:, k, :], w[1][:, k, :]), half + k == 0, half + k == 4)
                        if half:
                            mm.then_inc(full, 1)
                    if not half:
                        mm.then_inc(tile_used, 1)

            def prepare(L):
                pe.wait_ge(sem(f"gates_ready{L}"), 1)
                for g, src in enumerate((GA[:, :, 0:4], LF[:, :, 0:4], GA[:, :, 8:12], LF[:, :, 4:8])):
                    o, full = product(("gateT", L, g))
                    for t in range(NT):
                        mm = pe.transpose(o[0:4, t * P:(t + 1) * P], src[:, t, :], ident)
                    mm.then_inc(full, 1)
                pe.wait_ge(sem(f"gqa_ready{L}"), 1)
                for g in range(4):
                    o, full = product(("gqaT", L, g))
                    for t in range(NT):
                        mm = pe.transpose(o[:, t * P:(t + 1) * P], PG[:, t, g * P:(g + 1) * P], ident)
                    mm.then_inc(full, 1)
                pe.wait_ge(sem(f"stabilisers{L}"), 2)
                o, full = product(("stab", L))
                for k, (rows, r) in enumerate(((rows_f, 1), (rows_b, 1), (rows_f, 0), (rows_b, 0))):
                    for t in range(NT):
                        mm = pe.transpose(o[:, 16 * k + 4 * t:16 * k + 4 * t + 4], rows[0:4, r, t * P:(t + 1) * P],
                                          ident[0:4, 0:4])
                mm.then_inc(full, 1)
                pe.wait_ge(sem(f"latent_ready{L}"), 1)
                for g in range(3):
                    o, full = product(("mlaT", L, g))
                    for t in range(NT):
                        src = PAVCQ[:, t, 128 + g * P:128 + (g + 1) * P] if g < 2 else PCKV[:, t, 0:P]
                        mm = pe.transpose(o[:, t * P:(t + 1) * P], src, ident)
                    mm.then_inc(full, 1)
                for g in range(3):
                    evacuated(pe, ("mlaT", L, g))
                wq, wkv = tile(), tile()
                for t in range(NT):
                    o, full = product(("mlaq", L, t))
                    for k in range(2):
                        mm = pe.matmul(o[:, 0:LH * LQK], CT[:, k, t * P:(t + 1) * P], wq[:, k, :], start=k == 0, stop=k == 1)
                    mm.then_inc(full, 1)
                    o, full = product(("mlakv", L, t))
                    pe.matmul(o[:, :], CT[:, 2, t * P:(t + 1) * P], wkv[:, 0, :], start=True, stop=True).then_inc(full, 1)
                pe.wait_ge(sem(f"mla_ready{L}"), 1)
                for g in range(8):
                    o, full = product(("mlaH", L, g))
                    for t in range(NT):
                        mm = pe.transpose(o[0:LQK, t * P:(t + 1) * P], (QR if g < 4 else KR)[:, t, g % 4, :], ident)
                    mm.then_inc(full, 1)

            def heads(L):
                for g in range(4):
                    evacuated(pe, ("gqaT", L, g))
                for g in range(8):
                    evacuated(pe, ("mlaH", L, g))
                pe.wait_ge(sem(f"qk_ready{L}"), 2)

                def scores(u):
                    kind, h, t = u
                    nk = 256 if t < 2 else TOK
                    rows = slice(t * P, (t + 1) * P)
                    if kind == "A":
                        o, full = product(("S", L, u))
                        if h < AH:
                            p = slice(64 * (h // 3), 64 * (h // 3) + 64)
                            mm = pe.matmul(o[:, 0:nk], GT[p, h % 3, rows], GT[p, 3, 0:nk], start=True, stop=True)
                        else:
                            m = h - AH
                            mm = pe.matmul(o[:, 0:nk], MT[0:LQK, m, rows], MT[0:LQK, 4 + m, 0:nk], start=True, stop=True)
                        mm.then_inc(full, 1)
                        return
                    for i, (part, mask) in enumerate((("CF", C_MF), ("CB", C_MB))):
                        o, full = product((part, L, u))
                        m0 = mask + (0 if t % 2 else P)
                        pe.matmul(o[:, 0:nk], cst[0:4, C_SEL + h * P:C_SEL + (h + 1) * P], crow[0:4, i, 0:nk],
                                  start=True, stop=False)
                        pe.matmul(o[:, nk - 256:nk], ident, cst[:, m0:m0 + 256], start=False, stop=True).then_inc(full, 1)
                    o, full = product(("S", L, u))
                    pe.matmul(o[:, 0:nk], QK[0:MD, h, rows], QK[0:MD, 4 + h, 0:nk], start=True, stop=True).then_inc(full, 1)

                def turn(u, n):
                    kind, h, t = u
                    src = PA[:, n % 2, :] if kind == "A" else WT
                    if kind == "A":
                        evacuated(pe, ("S", L, u))
                    else:
                        pe.wait_ge(sem(f"weights_ready{L}"), n + 1)
                    o, full = product(("T", L, u))
                    for b in range(2 if t < 2 else NT):
                        mm = pe.transpose(o[:, b * P:(b + 1) * P], src[:, b * P:(b + 1) * P], ident)
                    mm.then_inc(full, 1)

                def values(u):
                    kind, h, t = u
                    evacuated(pe, ("T", L, u))
                    o, full = product(("O", L, u))
                    nb = 2 if t < 2 else NT
                    for b in range(nb):
                        if kind == "M":
                            w, v, n = PTM, PMV[:, b, h * MD:(h + 1) * MD], MD
                        elif h < AH:
                            w, v, n = PT, PAVCQ[:, b, 64 * (h // 3):64 * (h // 3) + 64], 64
                        else:
                            w, v, n = PT, VM[:, b, h - AH, :], 64
                        mm = pe.matmul(o[:, 0:n], w[:, b * P:(b + 1) * P], v, start=b == 0, stop=b == nb - 1)
                    mm.then_inc(full, 1)

                done = {"A": [], "M": []}
                for u in mixer_units(L):
                    d = done[u[0]]
                    scores(u)
                    if len(d) > 1:
                        values(d[-2])
                    if d:
                        turn(d[-1], len(d) - 1)
                    d.append(u)
                for d in done.values():
                    values(d[-2])
                    turn(d[-1], len(d) - 1)
                    values(d[-1])

            def spread(L, kind, sec):
                for g in groups(L):
                    for half in range(2):
                        o, full = product((kind, L, g, half))
                        for k in range(4):
                            col = modT[:, sec, 4 * half + k, g:g + 1].broadcast_to([P, P])
                            mm = pe.matmul(o[:, k * P:(k + 1) * P], col, ident, start=True, stop=True)
                        mm.then_inc(full, 1)

            def out_project(L):
                pe.wait_ge(sem(f"mix_ready{L}"), 1)
                for k in range(KT):
                    o, full = product(("outT", L, k))
                    for t in query_tiles(L):
                        mm = pe.transpose(o[:, t * P:(t + 1) * P], OROW[:, t, k * P:(k + 1) * P], ident)
                    mm.then_inc(full, 1)
                spread(L, "gateA", 2)
                columns_ready(L, "outT")
                for c in range(2):
                    rows_product([("out", L, c, t) for t in query_tiles(L)], query_tiles(L), 512)

            def bank_ready(b, n):
                pe.wait_ge(bank_free[b], n)
                return bank[b], bank_full[b]

            def ffn():
                pe.wait_ge(sem("features_0f"), KT)

                def step(j):
                    def split_of(i):
                        pe.wait_ge(split_lo, j * 6 + (starts["ffn"] + i + 1))
                        return pair_ap(i % PAIRS, 4, 512)

                    for n, kind in enumerate(("G", "U")):
                        for half in range(2):
                            w = split_of(2 * n + half)
                            for t in range(NT):
                                b, k = ffn_at(kind, j, t)
                                if not half:
                                    pe.wait_ge(bank_free[b], k)
                                for k in range(4):
                                    mm = three(bank[b][:, :], features(4 * half + k, slice(t * P, (t + 1) * P)),
                                               (w[0][:, k, :], w[1][:, k, :]), half + k == 0, half + k == 4)
                                if half:
                                    mm.then_inc(bank_full[b], 1)
                            if not half:
                                mm.then_inc(tile_used, 1)
                    for t in range(NT):
                        b, n = ffn_at("U", j, t)
                        pe.wait_ge(bank_free[b], n + 1)
                        o, full = bank_ready(*ffn_at("HT", j, t))
                        for k in range(4):
                            mm = pe.transpose(o[:, k * P:(k + 1) * P], SILF[:, t, k * P:(k + 1) * P], ident)
                        mm.then_inc(full, 1)
                    for c in range(2):
                        w = split_of(4 + c)
                        for t in range(NT):
                            b, n = ffn_at("HT", j, t)
                            pe.wait_ge(bank_free[b], n + 1)
                            o, full = bank_ready(*ffn_at(f"Y{c}", j, t))
                            for k in range(4):
                                cols = slice(k * P, (k + 1) * P)
                                mm = three(o[:, :], (TH[:, t, cols], TL[:, t, cols]), (w[0][:, k, :], w[1][:, k, :]), k == 0, k == 3)
                            mm.then_inc(full, 1)

                with pe.Fori(0, NJ) as j:
                    step(j)
                taken[0] = ffn_to
                split_taken[0] = starts["ffn"] + 6 * NJ
                spread(0, "gateF", 5)

            def route():
                columns_ready(1, "norm", "f")
                for t in range(2):
                    o, full = product(("router", t))
                    for k in range(KT):
                        mm = pe.matmul(o[:, 0:NE], HT[:, k, (2 + t) * P:(3 + t) * P], RT[:, k, :], start=k == 0, stop=k == KT - 1)
                    mm.then_inc(full, 1)
                spread(1, "gateF", 5)
                pe.wait_ge(sem("routed"), 1)
                o, full = product(("pos",))
                tri, one = cst[:, C_TRI:C_TRI + P], cst[:, C_ONE:C_ONE + P]
                s0, s1 = SELM[:, 0, 0:NE], SELM[:, 1, 0:NE]
                pe.matmul(o[:, 0:NE], tri, s0, start=True, stop=True)
                pe.matmul(o[:, NE:2 * NE], one, s0, start=True, stop=False)
                pe.matmul(o[:, NE:2 * NE], tri, s1, start=False, stop=True)
                pe.matmul(o[:, 2 * NE:3 * NE], one, s0, start=True, stop=False)
                pe.matmul(o[:, 2 * NE:3 * NE], one, s1, start=False, stop=True).then_inc(full, 1)

            def experts(p):
                def gather(half, b, n):
                    o, full = bank_ready(b, n)
                    for k in range(4):
                        f = 4 * half + k
                        for t in range(2):
                            mm = pe.matmul(o[:, k * P:(k + 1) * P], XN[:, 2 + t, f * P:(f + 1) * P], GM[:, t, :],
                                           start=t == 0, stop=t == 1)
                    mm.then_inc(full, 1)

                def scatter(i, b, n):
                    o, full = bank_ready(b, n)
                    t, c = i // 2, i % 2
                    pe.matmul(o[:, :], SMT[:, t, :], YROW[:, 512 * c:512 * (c + 1)], start=True, stop=True).then_inc(full, 1)

                def expert(e):
                    at = [0]

                    def next_tile():
                        i = at[0]
                        at[0] += 1
                        pe.wait_ge(split_lo, tile_no(p, e, i) + 1)
                        return pair_ap(i % PAIRS, 4, 512)

                    def gate_or_up(kind, j):
                        o, full = bank_ready(*moe_at(p, e, kind, j))
                        for c in range(2):
                            w = next_tile()
                            for k in range(4):
                                mm = three(o[:, :], (XTH[:, 4 * c + k, :], XTL[:, 4 * c + k, :]), (w[0][:, k, :], w[1][:, k, :]),
                                           c + k == 0, c + k == 4)
                            mm.then_inc(full if c else tile_used, 1)

                    def turn(j):
                        b, n = moe_at(p, e, "U", j)
                        pe.wait_ge(bank_free[b], n + 1)
                        o, full = bank_ready(*moe_at(p, e, "HT", j))
                        for k in range(4):
                            mm = pe.transpose(o[:, k * P:(k + 1) * P], H[:, k * P:(k + 1) * P], ident)
                        mm.then_inc(full, 1)

                    def down(j):
                        b, n = moe_at(p, e, "HT", j)
                        pe.wait_ge(bank_free[b], n + 1)
                        for c in range(2):
                            b, n = moe_at(p, e, "Y", c)
                            if j == 0:
                                pe.wait_ge(bank_free[b], n)
                            w = next_tile()
                            for k in range(4):
                                cols = slice(k * P, (k + 1) * P)
                                mm = three(bank[b][:, :], (TH[:, 0, cols], TL[:, 0, cols]), (w[0][:, k, :], w[1][:, k, :]),
                                           j + k == 0, j == NJ - 1 and k == 3)
                            mm.then_inc(bank_full[b] if j == NJ - 1 else tile_used, 1)

                    pe.wait_ge(sem("tokens_ready"), e * 2 + 2 * (p * (NE + 1) + 1))
                    for j in range(NJ):
                        gate_or_up("G", j)
                        if j < 2:
                            if j == 0:
                                for c in range(2):
                                    b, n = moe_at(p, e, "Y", c)
                                    pe.wait_ge(bank_free[b], n)
                            scatter(2 * j, *moe_at(p, e, "SC", 2 * j))
                        if j:
                            turn(j - 1)
                        gate_or_up("U", j)
                        if j < 2:
                            scatter(2 * j + 1, *moe_at(p, e, "SC", 2 * j + 1))
                        if j == NJ - 1:
                            pe.wait_ge(sem("gather_ready"), e + (p * (NE + 1) + 2))
                            gather(0, *moe_at(p, e, "GA", 0))
                        if j:
                            down(j - 1)
                        if j == 3:
                            pe.wait_ge(sem("scatter_ready"), e + (p * NE + 1))
                            o, full = bank_ready(*moe_at(p, e, "ST"))
                            for t in range(2):
                                mm = pe.transpose(o[:, t * P:(t + 1) * P], SM[:, t, :], ident)
                            mm.then_inc(full, 1)
                    turn(NJ - 1)
                    gather(1, *moe_at(p, e, "GA", 1))
                    down(NJ - 1)

                pe.wait_ge(sem("moe_cleared"), p + 1)
                pe.wait_ge(sem("gather_ready"), p * (NE + 1) + 1)
                for half in range(2):
                    gather(half, 5, moe_base(p, 5) - GA_PRO + half)
                with pe.Fori(0, NE) as e:
                    expert(e)
                for c in range(2):
                    b, n = moe_at(p, NE, "Y", c)
                    pe.wait_ge(bank_free[b], n)
                for i in range(4):
                    scatter(i, 5, moe_base(p, 5) + NE * MOE_USES[5] + i)

            pe.wait_ge(sem("consts_loaded"), 16)
            pe.wait_ge(sem("cvec_ready"), 1)
            for L in range(DEPTH):
                mod(L)
                norm(L, "a")
                project(L)
                prepare(L)
                heads(L)
                out_project(L)
                norm(L, "f")
                if L == 0:
                    ffn()
            route()
            experts(0)
            over = overflow(pe)
            with pe.If(over > 0):
                experts(1)

        @block.scalar
        def _(act):
            step = sem("act_step")
            steps = [0]

            def then(ins):
                steps[0] += 1
                ins.then_inc(step, 1)
                act.wait_ge(step, steps[0])

            def sqrt_of(L, name, v):
                act.wait_ge(sem(f"{name}_mean{L}"), 1)
                act.activation(v, v, ACT.Sqrt).then_inc(sem(f"{name}_root{L}"), 1)

            def norm(L, w):
                g0 = groups(L)[0] if w == "f" else 0
                if L == 0 and w == "a":
                    act.wait_ge(sem("x_loaded"), 32)
                else:
                    act.wait_ge(sem(f"x_updated_{L}{w}"), 1)
                for t in range(2 * g0, NT):
                    act.activation(bigB[:, t * D:(t + 1) * D], X[:, t, :], ACT.Square, accum_out=ss[:, t:t + 1]).then_inc(sem(f"squares_{L}{w}"), 1)
                sqrt_of(L, f"x{w}", rs[:, 2 * g0:NT])
                evacuated(act, ("modT", L, 11))
                first = starts["in", L] if w == "a" else starts["ffn"]
                if w == "a":
                    static_split("ScalarE", first)
                elif L == 0:
                    for i in range(PAIRS):
                        static_split("ScalarE", first + i)
                if (L, w) == (1, "f"):
                    for k in range(0, KT, 2):
                        o, free = take_out(act, ("norm", L, w, k))
                        modulated(act, HT[:, k, :], o, L, w, k, g0).then_inc(free, 1)
                    return
                for k in range(KT):
                    if k > 1:
                        act.wait_ge(sem(f"features_{L}{w}"), k - 1)
                    o, free = take_out(act, ("norm", L, w, k))
                    modulated(act, TMPK[:, k % 2, :], o, L, w, k, g0).then_inc(free, 1)
                if w == "a":
                    static_split("ScalarE", first + 1)

            act.dma_start(cvec[:, :, 1], a["c"][0].rearrange("(k p) -> p k", p=P), allow_slow_non_contiguous=True).then_inc(sem("cvec_loaded"), 16)
            act.dma_start(cvec[:, :, 0], a["c_ctx"].rearrange("(k p) -> p k", p=P), allow_slow_non_contiguous=True).then_inc(sem("cvec_loaded"), 16)
            act.dma_start(X[:, 0:2, :], a["ctx"][0].rearrange("(t p) d -> p t d", p=P)).then_inc(sem("x_loaded"), 16)
            act.dma_start(X[:, 2:4, :], a["x"][0].rearrange("(t p) d -> p t d", p=P)).then_inc(sem("x_loaded"), 16)
            act.wait_ge(sem("cvec_loaded"), 32)
            act.activation(cvec[:, :, :], cvec[:, :, :], ACT.Silu).then_inc(sem("cvec_ready"), 1)
            act.wait_ge(sem("params_loaded"), PARAMS)

            def project(L):
                for c in range(2):
                    static_split("ScalarE", starts["in", L] + 2 * c + 2)
                    for h in range(4 * c, 4 * c + 4):
                        o, _ = take_out(act, ("conv", L, h))
                        act.activation(QK[0:MD, h, :], o[0:MD, :], ACT.Identity, scale=convw[:, L, h, 1:2]).then_inc(sem(f"middle_tap{L}"), 1)
                    static_split("ScalarE", starts["in", L] + 2 * c + 3)
                for s, w in enumerate(ROWS_OF_W):
                    more = s + 1 < len(ROWS_OF_W)
                    if more:
                        static_split("ScalarE", starts["in", L] + 2 * s + 6)
                    for t in (0, 2):
                        o, free = take_out(act, ("proj", L, s, t))
                        if w == W_GQA:
                            to, src = paired(t, o)
                            act.activation(to, src, ACT.Copy)
                            act.activation(PG[:, t, 384:512], o[:, 384:512], ACT.Copy).then_inc(free, 1)
                        else:
                            act.activation(PROJ[w][:, t, :], o[:, 0:w[1]], ACT.Copy).then_inc(free, 1)
                    if more:
                        static_split("ScalarE", starts["in", L] + 2 * s + 7)

            def prepare(L):
                for c in range(2):
                    evacuated(act, ("conv", L, 4 + 3))
                    evacuated(act, ("conv", L, 4 + 2))
                    act.activation(QK[0:MD, 4 * c:4 * c + 4, :], QK[0:MD, 4 * c:4 * c + 4, :], ACT.Silu).then_inc(sem(f"qk_ready{L}"), 1)
                act.wait_ge(sem(f"gate_negated{L}"), 1)
                then(act.activation(gtmp[:, :, :], gtmp[:, :, :], ACT.Exp))
                act.activation(gtmp[:, :, :], gtmp[:, :, :], ACT.Ln, bias=1.0).then_inc(sem(f"gate_log{L}"), 1)
                for t in (1, 3):
                    evacuated(act, ("proj", L, 1, t))
                act.activation(SQ[:, :, :], PG[:, :, :], ACT.Square).then_inc(sem(f"gqa_squares{L}"), 1)
                sqrt_of(L, "gqa", grs[:, 0:32])
                for t in (1, 3):
                    evacuated(act, ("proj", L, 2, t))
                    evacuated(act, ("proj", L, 3, t))
                act.wait_ge(sem(f"gqa_ready{L}"), 1)
                act.activation(SQ[:, :, 0:256], PAVCQ[:, :, 128:384], ACT.Square)
                act.activation(SQ[:, :, 256:416], PCKV[:, :, :], ACT.Square).then_inc(sem(f"latent_squares{L}"), 1)
                sqrt_of(L, "latent", grs[:, 0:12])
                o, free = take_out(act, ("stab", L))
                act.activation(stab[:, :, :, :], o[:, 0:64].rearrange("p (k t h) -> p k t h", k=4, t=4), ACT.Copy, scale=-1.0)\
                    .then_inc(free, 1)
                evacuated(act, ("stab", L))
                act.activation(stab[:, 2:4, :, :], stab[:, 2:4, :, :], ACT.Exp).then_inc(sem(f"stab_exp{L}"), 1)
                for g in range(3):
                    o, free = take_out(act, ("mlaT", L, g))
                    act.activation(CT[:, g, :], o[:, :], ACT.Identity, scale=cqG[:, L, g:g + 1]).then_inc(free, 1)
                for t in range(NT):
                    o, free = take_out(act, ("mlaq", L, t))
                    act.activation(QR[:, t, :, :], o[:, 0:LH * LQK].rearrange("p (h d) -> p h d", h=LH), ACT.Copy).then_inc(free, 1)
                for t in range(NT):
                    evacuated(act, ("mlaq", L, t))
                    evacuated(act, ("mlakv", L, t))
                act.activation(SQ[:, :, 0:384].rearrange("p t (h d) -> p t h d", h=LH), QR[:, :, :, :], ACT.Square).then_inc(sem(f"mla_squares{L}"), 1)
                act.wait_ge(sem(f"mla_squares_read{L}"), 1)
                act.activation(SQ[:, :, 0:256].rearrange("p t (h d) -> p t h d", h=LH), KR[:, :, :, 0:64], ACT.Square).then_inc(sem(f"mla_squares{L}"), 1)
                sqrt_of(L, "mla", grs[:, 0:48])
                for g in range(0, 8, 2):
                    o, free = take_out(act, ("mlaH", L, g))
                    act.activation(MT[0:LQK, g, :], o[0:LQK, :], ACT.Copy).then_inc(free, 1)

            def heads(L):
                count = {"A": 0, "M": 0}
                before = {"A": None, "M": None}

                def turned(u):
                    kind, h, t = u
                    nk = 256 if t < 2 else TOK
                    o, free = take_out(act, ("T", L, u))
                    act.activation((PT if kind == "A" else PTM)[:, 0:nk], o[:, 0:nk], ACT.Copy).then_inc(free, 1)

                for u in mixer_units(L):
                    kind, h, t = u
                    n = count[kind]
                    count[kind] += 1
                    nk = 256 if t < 2 else TOK
                    if before[kind]:
                        pass
                    if kind == "A":
                        act.wait_ge(sem(f"row_max{L}"), n + 1)
                        o, free = take_out(act, ("S", L, u))
                        act.activation(PA[:, n % 2, 0:nk], o[:, 0:nk], ACT.Exp, bias=nmax[:, 0:1],
                                       accum_out=rsum[:, n % 4:n % 4 + 1]).then_inc(free, 1)
                    else:
                        if n:
                            act.wait_ge(sem(f"weights_ready{L}"), n)
                        for i, (part, e) in enumerate((("CF", EF), ("CB", EB))):
                            o, free = take_out(act, (part, L, u))
                            act.activation(e[:, 0:nk], o[:, 0:nk], ACT.Exp, bias=stab[:, i, t, h:h + 1]).then_inc(free, 1)
                    if before[kind]:
                        turned(before[kind])
                    before[kind] = u
                turned(before["A"])
                turned(before["M"])

            def out_project(L):
                t0 = query_tiles(L)[0]
                last = [u for u in mixer_units(L) if u[0] == "M"][-1]
                evacuated(act, ("O", L, last))
                act.activation(SQ[:, t0:NT, 0:MW], OROW[:, t0:NT, 0:MW], ACT.Square).then_inc(sem(f"mlstm_squares{L}"), 1)
                sqrt_of(L, "mlstm", grs[:, 0:4 * (NT - t0)])
                act.activation(PMO[:, t0:NT, 0:MW], PMO[:, t0:NT, 0:MW], ACT.Sigmoid).then_inc(sem(f"out_gate{L}"), 1)
                first = starts["out", L]
                act.wait_ge(sem(f"mix_ready{L}"), 1)
                static_split("ScalarE", first)
                for k in range(KT):
                    o, _ = take_out(act, ("outT", L, k))
                    act.activation(HH[:, k, t0 * P:], o[:, t0 * P:], ACT.Copy).then_inc(sem(f"mix_rounded{L}"), 1)
                static_split("ScalarE", first + 1)
                spread(L, "gateA", GBC_A)
                static_split("ScalarE", first + 2)
                static_split("ScalarE", first + 3)

            def spread(L, kind, to):
                for g in groups(L):
                    for half in range(2):
                        o, free = take_out(act, (kind, L, g, half))
                        act.activation(to[:, g, 512 * half:512 * (half + 1)], o[:, :], ACT.Copy).then_inc(free, 1)

            def ffn():
                def step(j, more):
                    for i in range(6):
                        if i == 1:
                            for t in range(NT):
                                b, n = ffn_at("G", j, t)
                                act.wait_ge(bank_full[b], n + 1)
                                act.activation(SILF[:, t, :], bank[b][:, :], ACT.Silu).then_inc(bank_free[b], 1)
                        if i == 3:
                            for t in range(NT):
                                b, n = ffn_at("HT", j, t)
                                act.wait_ge(bank_full[b], n + 1)
                                act.activation(TH[:, t, :], bank[b][:, :], ACT.Copy).then_inc(sem("hidden_rounded"), 1)
                        if i < 3 or more:
                            ffn_left(act, j, i)
                            ffn_split("ScalarE", j + (i + PAIRS) // 6, (i + PAIRS) % 6)

                with act.Fori(0, NJ - 1) as j:
                    step(j, True)
                step(NJ - 1, False)
                spread(0, "gateF", GBC_F)

            def experts(p):
                def gathered(half, b, n):
                    act.wait_ge(bank_full[b], n + 1)
                    for k in range(4):
                        f = 4 * half + k
                        ins = act.activation(XTF[:, f, :], bank[b][:, k * P:(k + 1) * P], ACT.Identity,
                                             scale=modT[:, 4, f, 1:2], bias=modT[:, 3, f, 1:2])
                    ins.then_inc(bank_free[b], 1)

                def expert(e, more):
                    def turned(j):
                        b, n = moe_at(p, e, "HT", j)
                        act.wait_ge(bank_full[b], n + 1)
                        act.activation(TH[:, 0, :], bank[b][:, :], ACT.Copy).then_inc(sem("expert_rounded"), 1)

                    for i, (m, j, c) in enumerate(tiles):
                        if (m, c) == ("g", 1):
                            b, n = moe_at(p, e, "G", j)
                            act.wait_ge(bank_full[b], n + 1)
                            act.activation(SIL[:, j % 2, :], bank[b][:, :], ACT.Silu).then_inc(bank_free[b], 1)
                            if j:
                                turned(j - 1)
                        if (m, j, c) == ("u", NJ - 1, 1):
                            gathered(0, *moe_at(p, e, "GA", 0))
                        if (m, j, c) == ("d", 2, 1):
                            b, n = moe_at(p, e, "ST")
                            act.wait_ge(bank_full[b], n + 1)
                            act.activation(SMT[:, :, :], bank[b][:, 0:2 * P].rearrange("p (t s) -> p t s", t=2), ACT.Copy)\
                                .then_inc(bank_free[b], 1)
                        if (m, j, c) == ("d", NJ - 2, 1):
                            turned(NJ - 1)
                            gathered(1, *moe_at(p, e, "GA", 1))
                        if (m, j) == ("d", NJ - 1):
                            b, n = moe_at(p, e, "Y", c)
                            act.wait_ge(bank_full[b], n + 1)
                            act.activation(YROW[:, 512 * c:512 * (c + 1)], bank[b][:, :], ACT.Copy).then_inc(bank_free[b], 1)
                        if i + PAIRS < PER or more:
                            moe_left(act, p, e, i)
                            moe_split("ScalarE", p, e + (i + PAIRS) // PER, (i + PAIRS) % PER)

                for i in range(PAIRS):
                    if p:
                        moe_left(act, 0, NE - 1, PER - PAIRS + i)
                    moe_split("ScalarE", p, 0, i)
                for half in range(2):
                    gathered(half, 5, moe_base(p, 5) - GA_PRO + half)
                with act.Fori(0, NE - 1) as e:
                    expert(e, True)
                expert(NE - 1, False)

            for L in range(DEPTH):
                norm(L, "a")
                project(L)
                prepare(L)
                heads(L)
                out_project(L)
                norm(L, "f")
                if L == 0:
                    ffn()
            act.wait_ge(sem("expert_gap"), 1)
            act.activation(wts[:, 0:2], wts[:, 0:2], ACT.Exp).then_inc(sem("expert_gap_exp"), 1)
            spread(1, "gateF", GBC_F)
            act.wait_ge(sem("moe_cleared"), 1)
            experts(0)
            over = overflow(act)
            with act.If(over > 0):
                act.wait_ge(sem("moe_cleared"), 2)
                experts(1)

        @block.vector
        def _(dve):
            step = sem("dve_step")
            steps = [0]

            def then(ins):
                steps[0] += 1
                ins.then_inc(step, 1)
                dve.wait_ge(step, steps[0])

            def mean(L, name, dst, src, n):
                then(dve.tensor_scalar(dst, src, 1.0 / n, EPS, ALU.mult, ALU.add)) if name is None else \
                    dve.tensor_scalar(dst, src, 1.0 / n, EPS, ALU.mult, ALU.add).then_inc(sem(f"{name}_mean{L}"), 1)

            def rstd(L, name, v):
                dve.wait_ge(sem(f"{name}_root{L}"), 1)
                then(dve.reciprocal(v, v))

            dve.wait_ge(sem("params_loaded"), PARAMS)
            dve.wait_ge(sem("consts_loaded"), 16)
            for L in range(DEPTH):
                then(dve.tensor_scalar(gains[:, L, G_AQ:G_AQ + AD], gains[:, L, G_AQ:G_AQ + AD], AD ** -0.5, None, ALU.mult))
                then(dve.tensor_scalar(gains[:, L, G_LQ:G_LQ + LQK], gains[:, L, G_LQ:G_LQ + LQK], LQK ** -0.5, None, ALU.mult))
            then(dve.memset(rt[:, :, :, :], 0.0))

            def mod(L):
                def columns_of(i):
                    s, half = i // 2, i % 2
                    o, free = take_out(dve, ("modT", L, i))
                    src = o[:, 0:8].rearrange("p (k g) -> p k g", g=2)
                    dst = modT[:, s, 4 * half:4 * half + 4, :]
                    if s in (1, 4):
                        g = normG[:, L, s // 4, 4 * half:4 * half + 4].unsqueeze(2).broadcast_to([P, 4, 2])
                        ins = dve.scalar_tensor_tensor(out=dst, in0=src, scalar=1.0, in1=g, op0=ALU.add, op1=ALU.mult)
                    else:
                        ins = dve.tensor_copy(dst, src)
                    ins.then_inc(free, 1)
                for i in range(12):
                    if i > 1:
                        b, n = plan.at[("modT", L, i - 2)]
                        dve.wait_ge(bank_full[b], n + 1)
                    dve.wait_ge(sem(f"modb_loaded{i % 2}"), 16 * (6 * L + i // 2 + 1))
                    o, free = take_out(dve, ("mod", L, i))
                    dve.tensor_tensor(MODROW[0:2, i % 2, :], o[0:2, :], MODB[0:2, i % 2, :], ALU.add).then_inc(free, 1)
                    if i:
                        columns_of(i - 1)
                columns_of(11)

            def norm(L, w):
                g0 = groups(L)[0] if w == "f" else 0
                dve.wait_ge(sem(f"squares_{L}{w}"), NT - 2 * g0)
                mean(L, f"x{w}", rs[:, 2 * g0:NT], ss[:, 2 * g0:NT], D)
                rstd(L, f"x{w}", rs[:, 2 * g0:NT])
                for t in range(2 * g0, NT):
                    dve.tensor_scalar(XN[:, t, :], X[:, t, :], rs[:, t:t + 1], None, ALU.mult).then_inc(sem(f"normed_{L}{w}"), 1)
                first = starts["in", L] if w == "a" else starts["ffn"]
                if w == "a":
                    static_split(rest, first)
                elif L == 0:
                    for i in range(PAIRS):
                        static_split(rest, first + i)
                if (L, w) == (1, "f"):
                    for k in range(1, KT, 2):
                        o, free = take_out(dve, ("norm", L, w, k))
                        modulated(dve, HT[:, k, :], o, L, w, k, g0).then_inc(free, 1)
                    return
                for k in range(KT):
                    evacuated(dve, ("norm", L, w, k))
                    then(dve.tensor_copy(HH[:, k, :], TMPK[:, k % 2, :]))
                    dve.tensor_tensor(HL[:, k, :], TMPK[:, k % 2, :], HH[:, k, :].bitcast(F32), ALU.subtract)\
                        .then_inc(sem(f"features_{L}{w}"), 1)
                if w == "a":
                    static_split(rest, first + 1)

            def project(L):
                two = "p (s t) -> p s t"
                for c in range(2):
                    static_split(rest, starts["in", L] + 2 * c + 2)
                    for h in range(4 * c, 4 * c + 4):
                        dve.wait_ge(sem(f"middle_tap{L}"), h + 1)
                        o, free = take_out(dve, ("conv", L, h))
                        src, dst = o[0:MD, :].rearrange(two, s=2), QK[0:MD, h, :].rearrange(two, s=2)
                        then(dve.scalar_tensor_tensor(out=dst[:, :, 1:256], in0=src[:, :, 0:255], scalar=convw[:, L, h, 0:1],
                                                      in1=dst[:, :, 1:256], op0=ALU.mult, op1=ALU.add))
                        dve.scalar_tensor_tensor(out=dst[:, :, 0:255], in0=src[:, :, 1:256], scalar=convw[:, L, h, 2:3],
                                                 in1=dst[:, :, 0:255], op0=ALU.mult, op1=ALU.add).then_inc(free, 1)
                    static_split(rest, starts["in", L] + 2 * c + 3)
                for s, w in enumerate(ROWS_OF_W):
                    more = s + 1 < len(ROWS_OF_W)
                    if more:
                        static_split(rest, starts["in", L] + 2 * s + 6)
                    for t in (1, 3):
                        o, free = take_out(dve, ("proj", L, s, t))
                        if w == W_GQA:
                            dve.tensor_copy(*paired(t, o))
                            dve.tensor_copy(PG[:, t, 384:512], o[:, 384:512]).then_inc(free, 1)
                        else:
                            dve.tensor_copy(PROJ[w][:, t, :], o[:, 0:w[1]]).then_inc(free, 1)
                    if more:
                        static_split(rest, starts["in", L] + 2 * s + 7)

            def rope(xs, dim, cos_at, sin_at, heads_n, tmp):
                for i in range(2):
                    x, tm = xs(2 + i), tmp(i)
                    for q in range(2):
                        sin = cst[:, sin_at + i * dim:sin_at + (i + 1) * dim].rearrange("p (a b c) -> p a b c", a=2, b=2)[:, :, q, :]
                        xo = x.rearrange("p h (a b c) -> p h a b c", a=2, b=2)[:, :, :, 1 - q, :]
                        to = tm.rearrange("p h (a b c) -> p h a b c", a=2, b=2)[:, :, :, q, :]
                        for half in range(2):
                            ins = dve.tensor_tensor(to[:, :, half, :], xo[:, :, half, :],
                                                    sin[:, half, :].unsqueeze(1).broadcast_to([P, heads_n, dim // 4]), ALU.mult)
                    then(ins)
                    cos = cst[:, cos_at + i * dim:cos_at + (i + 1) * dim].unsqueeze(1).broadcast_to([P, heads_n, dim])
                    then(dve.tensor_tensor(x, x, cos, ALU.mult))
                    then(dve.tensor_tensor(x, x, tm, ALU.add))

            def prepare(L):
                for t in range(NT):
                    evacuated(dve, ("proj", L, 0, t))
                bias = gains[:, L, G_GB:G_GB + 16].unsqueeze(1).broadcast_to([P, NT, 16])
                then(dve.tensor_tensor(GA[:, :, :], PMO[:, :, 384:400], bias, ALU.add))
                f = GA[:, :, :].rearrange("p t (d x h) -> p t d x h", d=2, x=2)[:, :, :, 1, :]
                g = gtmp[:, :, :].rearrange("p t (d h) -> p t d h", d=2)
                for d in range(2):
                    ins = dve.scalar_tensor_tensor(out=g[:, :, d, :], in0=f[:, :, d, :], scalar=-1.0, in1=f[:, :, d, :],
                                                   op0=ALU.mult, op1=ALU.min)
                ins.then_inc(sem(f"gate_negated{L}"), 1)
                dve.wait_ge(sem(f"gate_log{L}"), 1)
                lf = LF[:, :, :].rearrange("p t (d h) -> p t d h", d=2)
                for d in range(2):
                    ins = dve.scalar_tensor_tensor(out=lf[:, :, d, :], in0=f[:, :, d, :], scalar=0.0, in1=g[:, :, d, :],
                                                   op0=ALU.min, op1=ALU.subtract)
                ins.then_inc(sem(f"gates_ready{L}"), 1)

                dve.wait_ge(sem(f"gqa_squares{L}"), 1)
                then(dve.tensor_reduce(gss[:, 0:32].rearrange("p (t h) -> p t h", t=NT),
                                       SQ[:, :, :].rearrange("p t (h d) -> p t h d", d=AD), AX.X, ALU.add))
                mean(L, "gqa", grs[:, 0:32], gss[:, 0:32], AD)
                rstd(L, "gqa", grs[:, 0:32])
                for t in range(NT):
                    evacuated(dve, ("proj", L, 1, t))
                heads_v = PG[:, :, :].rearrange("p t (h d) -> p t h d", d=AD)
                then(dve.tensor_tensor(heads_v, heads_v, grs[:, 0:32].rearrange("p (t h) -> p t h", t=NT).unsqueeze(3)
                                       .broadcast_to([P, NT, 8, AD]), ALU.mult))
                for h0, h1, at in ((0, AH, G_AQ), (AH, 8, G_AK)):
                    for t in range(NT):
                        ins = dve.tensor_tensor(heads_v[:, t, h0:h1, :], heads_v[:, t, h0:h1, :],
                                                gains[:, L, at:at + AD].unsqueeze(1).broadcast_to([P, h1 - h0, AD]), ALU.mult)
                then(ins)
                rope(lambda t: PG[:, t, :].rearrange("p (h d) -> p h d", d=AD), AD, C_COSA, C_SINA, 8,
                     lambda i: SQ[:, i, :].rearrange("p (h d) -> p h d", d=AD))
                then(dve.tensor_copy(den[:, 0:1], grs[:, 0:1]))
                dve.tensor_copy(den[:, 1:2], grs[:, 0:1]).then_inc(sem(f"gqa_ready{L}"), 1)

                ones = cst[0:4, C_ONE:C_ONE + 1]
                parts_f = [(slice(0, 512), None)]
                for d, (rows, ki, kf) in enumerate(((rows_f, 0, 1), (rows_b, 2, 3))):
                    fo, f_free = take_out(dve, ("gateT", L, kf))
                    io, i_free = take_out(dve, ("gateT", L, ki))
                    parts = ((0, 512),) if d == 0 else ((0, 256), (256, 512))

                    def seg(x, lo, hi):
                        return x[:, lo:hi] if d == 0 else x[:, lo:hi][:, ::-1]
                    for n, (lo, hi) in enumerate(parts):
                        init = 0.0 if n == 0 else rows[0:4, 0, 0:1]
                        then(dve.tensor_tensor_scan(seg(rows[0:4, 0, :], lo, hi), ones.broadcast_to([4, hi - lo]),
                                                    seg(fo[0:4, :], lo, hi), init, ALU.mult, ALU.add))
                    dve.tensor_copy(rinv[0:4, 0:1], fo[0:4, 0:1]).then_inc(f_free, 1)
                    dve.tensor_tensor(crow[0:4, d, :], io[0:4, :], rows[0:4, 0, :], ALU.subtract).then_inc(i_free, 1)
                    evacuated(dve, ("gateT", L, ki))
                    for n, (lo, hi) in enumerate(parts):
                        init = 0.0 if n == 0 else rows[0:4, 1, 0:1]
                        c = seg(crow[0:4, d, :], lo, hi)
                        then(dve.tensor_tensor_scan(seg(rows[0:4, 1, :], lo, hi), c, c, init, ALU.max, ALU.max))
                    dve.tensor_tensor(rows[0:4, 0, :], rows[0:4, 0, :], rows[0:4, 1, :], ALU.add).then_inc(sem(f"stabilisers{L}"), 1)

                for g in range(4):
                    o, free = take_out(dve, ("gqaT", L, g))
                    dve.tensor_copy(GT[:, g, :], o[:, :]).then_inc(free, 1)
                dve.wait_ge(sem(f"latent_squares{L}"), 1)
                dve.tensor_reduce(gss[:, 0:4], SQ[:, :, 0:256], AX.X, ALU.add)
                dve.tensor_reduce(gss[:, 4:8], SQ[:, :, 256:384], AX.X, ALU.add)
                then(dve.tensor_reduce(gss[:, 8:12], SQ[:, :, 384:416], AX.X, ALU.add))
                dve.tensor_scalar(grs[:, 0:4], gss[:, 0:4], 1.0 / QRANK, EPS, ALU.mult, ALU.add)
                dve.tensor_scalar(grs[:, 4:8], gss[:, 4:8], 1.0 / KVRANK, EPS, ALU.mult, ALU.add)
                mean(L, "latent", grs[:, 8:12], gss[:, 8:12], ROPE)
                rstd(L, "latent", grs[:, 0:12])
                for t in range(NT):
                    evacuated(dve, ("proj", L, 2, t))
                    evacuated(dve, ("proj", L, 3, t))
                for x, n, at in ((PAVCQ[:, :, 128:384], 256, 0), (PCKV[:, :, 0:128], 128, 4), (PCKV[:, :, 128:160], 32, 8)):
                    ins = dve.tensor_tensor(x, x, grs[:, at:at + 4].unsqueeze(2).broadcast_to([P, NT, n]), ALU.mult)
                ins.then_inc(sem(f"latent_ready{L}"), 1)
                dve.wait_ge(sem(f"latent_ready{L}"), 1)
                kr = PCKV[:, :, 128:160]
                then(dve.tensor_tensor(kr, kr, gains[:, L, G_LK + 64:G_LK + 96].unsqueeze(1).broadcast_to([P, NT, ROPE]), ALU.mult))
                rope(lambda t: PCKV[:, t, 128:160].unsqueeze(1), ROPE, C_COSL, C_SINL, 1,
                     lambda i: SQ[:, i, 0:32].unsqueeze(1))
                for t in range(NT):
                    o, free = take_out(dve, ("mlakv", L, t))
                    kv = o[:, :].rearrange("p (h d) -> p h d", h=LH)
                    dve.tensor_copy(KR[:, t, :, 64:96], PCKV[:, t, 128:160].unsqueeze(1).broadcast_to([P, LH, ROPE]))
                    dve.tensor_copy(KR[:, t, :, 0:64], kv[:, :, 0:64])
                    dve.tensor_copy(VM[:, t, :, :], kv[:, :, 64:128]).then_inc(free, 1)
                dve.wait_ge(sem(f"mla_squares{L}"), 1)
                sq = SQ[:, :, 0:384].rearrange("p t (h d) -> p t h d", h=LH)
                th = "p (t h) -> p t h"
                dve.tensor_reduce(gss[:, 0:16].rearrange(th, t=NT), sq[:, :, :, 0:64], AX.X, ALU.add)
                dve.tensor_reduce(gss[:, 16:32].rearrange(th, t=NT), sq[:, :, :, 64:96], AX.X, ALU.add)\
                    .then_inc(sem(f"mla_squares_read{L}"), 1)
                dve.wait_ge(sem(f"mla_squares{L}"), 2)
                sk = SQ[:, :, 0:256].rearrange("p t (h d) -> p t h d", h=LH)
                then(dve.tensor_reduce(gss[:, 32:48].rearrange(th, t=NT), sk, AX.X, ALU.add))
                dve.tensor_scalar(grs[:, 0:16], gss[:, 0:16], 1.0 / NOPE, EPS, ALU.mult, ALU.add)
                dve.tensor_scalar(grs[:, 16:32], gss[:, 16:32], 1.0 / ROPE, EPS, ALU.mult, ALU.add)
                mean(L, "mla", grs[:, 32:48], gss[:, 32:48], NOPE)
                rstd(L, "mla", grs[:, 0:48])
                for t in range(NT):
                    evacuated(dve, ("mlaq", L, t))
                for x, n, at in ((QR[:, :, :, 0:64], 64, 0), (QR[:, :, :, 64:96], 32, 16), (KR[:, :, :, 0:64], 64, 32)):
                    r = grs[:, at:at + 16].rearrange(th, t=NT)
                    for t in range(NT):
                        ins = dve.tensor_tensor(x[:, t], x[:, t], r[:, t, :].unsqueeze(2).broadcast_to([P, LH, n]), ALU.mult)
                then(ins)
                for t in range(NT):
                    dve.tensor_tensor(QR[:, t], QR[:, t], gains[:, L, G_LQ:G_LQ + LQK].unsqueeze(1).broadcast_to([P, LH, LQK]), ALU.mult)
                    ins = dve.tensor_tensor(KR[:, t, :, 0:64], KR[:, t, :, 0:64],
                                            gains[:, L, G_LK:G_LK + 64].unsqueeze(1).broadcast_to([P, LH, 64]), ALU.mult)
                then(ins)
                rope(lambda t: QR[:, t, :, 64:96], ROPE, C_COSL, C_SINL, LH,
                     lambda i: SQ[:, i, 0:128].rearrange("p (h d) -> p h d", h=LH))
                dve.tensor_copy(den[:, 0:1], grs[:, 0:1]).then_inc(sem(f"mla_ready{L}"), 1)
                for g in range(1, 8, 2):
                    o, free = take_out(dve, ("mlaH", L, g))
                    dve.tensor_copy(MT[0:LQK, g, :], o[0:LQK, :]).then_inc(free, 1)

            def heads(L):
                dve.wait_ge(sem(f"stab_exp{L}"), 1)
                seen = {"A": [], "M": []}

                def head_out(u, n):
                    kind, h, t = u
                    if kind == "A":
                        o, free = take_out(dve, ("O", L, u))
                        then(dve.reciprocal(rinv[:, 0:1], rsum[:, n % 4:n % 4 + 1]))
                        dve.tensor_scalar(OROW[:, t, MW + 64 * h:MW + 64 * (h + 1)], o[:, 0:64], rinv[:, 0:1], None, ALU.mult)\
                            .then_inc(free, 1)
                    else:
                        o, free = take_out(dve, ("O", L, u))
                        dve.tensor_copy(OROW[:, t, MD * h:MD * (h + 1)], o[:, 0:MD]).then_inc(free, 1)

                for u in mixer_units(L):
                    kind, h, t = u
                    nk = 256 if t < 2 else TOK
                    d = seen[kind]
                    if kind == "A":
                        o, _ = take_out(dve, ("S", L, u))
                        dve.tensor_reduce(nmax[:, 0:1], o[:, 0:nk], AX.X, ALU.max, negate=True).then_inc(sem(f"row_max{L}"), 1)
                    else:
                        o, free = take_out(dve, ("S", L, u))
                        evacuated(dve, ("CF", L, u))
                        dve.tensor_tensor_reduce(EF[:, 0:nk], EF[:, 0:nk], o[:, 0:nk], MD ** -0.5, 0.0, ALU.mult, ALU.add, den[:, 0:1])
                        evacuated(dve, ("CB", L, u))
                        dve.tensor_tensor_reduce(EB[:, 0:nk], EB[:, 0:nk], o[:, 0:nk], MD ** -0.5, 0.0, ALU.mult, ALU.add, den[:, 1:2])\
                            .then_inc(free, 1)
                        evacuated(dve, ("S", L, u))
                        then(dve.scalar_tensor_tensor(out=dabs[:, :], in0=den[:, :], scalar=-1.0, in1=den[:, :], op0=ALU.mult, op1=ALU.max))
                        then(dve.tensor_tensor(dabs[:, :], dabs[:, :], stab[:, 2:4, t, h], ALU.max))
                        then(dve.reciprocal(dabs[:, :], dabs[:, :]))
                        then(dve.tensor_scalar(EB[:, 0:nk], EB[:, 0:nk], dabs[:, 1:2], None, ALU.mult))
                        if d:
                            b, n = plan.at[("T", L, d[-1])]
                            dve.wait_ge(bank_full[b], n + 1)
                        dve.scalar_tensor_tensor(out=WT[:, 0:nk], in0=EF[:, 0:nk], scalar=dabs[:, 0:1], in1=EB[:, 0:nk],
                                                 op0=ALU.mult, op1=ALU.add).then_inc(sem(f"weights_ready{L}"), 1)
                    if len(d) > 1:
                        head_out(d[-2], len(d) - 2)
                    d.append(u)
                for d in seen.values():
                    head_out(d[-2], len(d) - 2)
                    head_out(d[-1], len(d) - 1)

            def out_project(L):
                t0 = query_tiles(L)[0]
                nt = NT - t0
                dve.wait_ge(sem(f"mlstm_squares{L}"), 1)
                then(dve.tensor_reduce(gss[:, 0:4 * nt].rearrange("p (t h) -> p t h", h=MH),
                                       SQ[:, t0:NT, 0:MW].rearrange("p t (h d) -> p t h d", h=MH), AX.X, ALU.add))
                mean(L, "mlstm", grs[:, 0:4 * nt], gss[:, 0:4 * nt], MD)
                rstd(L, "mlstm", grs[:, 0:4 * nt])
                x = OROW[:, t0:NT, 0:MW]
                for t in range(nt):
                    v = OROW[:, t0 + t, 0:MW].rearrange("p (h d) -> p h d", h=MH)
                    ins = dve.tensor_tensor(v, v, grs[:, 4 * t:4 * t + 4].unsqueeze(2).broadcast_to([P, MH, MD]), ALU.mult)
                then(ins)
                then(dve.tensor_tensor(x, x, gains[:, L, G_M:G_M + MW].unsqueeze(1).broadcast_to([P, nt, MW]), ALU.mult))
                dve.wait_ge(sem(f"out_gate{L}"), 1)
                dve.tensor_tensor(x, x, PMO[:, t0:NT, 0:MW], ALU.mult).then_inc(sem(f"mix_ready{L}"), 1)
                first = starts["out", L]
                static_split(rest, first)
                for k in range(KT):
                    o, free = take_out(dve, ("outT", L, k))
                    dve.wait_ge(sem(f"mix_rounded{L}"), k + 1)
                    dve.tensor_tensor(HL[:, k, t0 * P:], o[:, t0 * P:], HH[:, k, t0 * P:].bitcast(F32), ALU.subtract).then_inc(free, 1)
                static_split(rest, first + 1)
                static_split(rest, first + 2)
                for g in groups(L):
                    for half in range(2):
                        evacuated(dve, ("gateA", L, g, half))
                for c in range(2):
                    cols = slice(512 * c, 512 * (c + 1))
                    if c == 0:
                        static_split(rest, first + 3)
                    for t in query_tiles(L):
                        o, free = take_out(dve, ("out", L, c, t))
                        dve.tensor_tensor(TMPX[:, t % 2, :], o[:, :], GBC_A[:, t // 2, cols], ALU.mult).then_inc(free, 1)
                        evacuated(dve, ("out", L, c, t))
                        ins = dve.tensor_tensor(X[:, t, cols], X[:, t, cols], TMPX[:, t % 2, :], ALU.add)
                        if t % 2:
                            then(ins) if (c, t) != (1, NT - 1) else None
                ins.then_inc(sem(f"x_updated_{L}f"), 1)

            def ffn():
                then(dve.memset(YACC[:, :, :], 0.0))

                def step(j, more):
                    for i in range(6):
                        if i == 3:
                            for t in range(NT):
                                b, n = ffn_at("G", j, t)
                                dve.wait_ge(bank_free[b], n + 1)
                                b, n = ffn_at("U", j, t)
                                dve.wait_ge(bank_full[b], n + 1)
                                dve.tensor_tensor(SILF[:, t, :], SILF[:, t, :], bank[b][:, :], ALU.mult).then_inc(bank_free[b], 1)
                            for t in range(NT):
                                b, n = ffn_at("HT", j, t)
                                dve.wait_ge(sem("hidden_rounded"), j * NT + (t + 1))
                                dve.tensor_tensor(TL[:, t, :], bank[b][:, :], TH[:, t, :].bitcast(F32), ALU.subtract)\
                                    .then_inc(bank_free[b], 1)
                        if i > 3:
                            c = i - 4
                            for t in range(NT):
                                b, n = ffn_at(f"Y{c}", j, t)
                                dve.wait_ge(bank_full[b], n + 1)
                                y = YACC[:, t, 512 * c:512 * (c + 1)]
                                dve.tensor_tensor(y, bank[b][:, :], y, ALU.add).then_inc(bank_free[b], 1)
                        if i < 3 or more:
                            ffn_split(rest, j + (i + PAIRS) // 6, (i + PAIRS) % 6)

                with dve.Fori(0, NJ - 1) as j:
                    step(j, True)
                step(NJ - 1, False)
                for half in range(2):
                    for g in range(2):
                        evacuated(dve, ("gateF", 0, g, half))
                evacuated(dve, ("Y1", NJ - 1, NT - 1))
                for t in range(NT):
                    then(dve.tensor_tensor(YACC[:, t, :], YACC[:, t, :], GBC_F[:, t // 2, :], ALU.mult))
                    ins = dve.tensor_tensor(X[:, t, :], X[:, t, :], YACC[:, t, :], ALU.add)
                ins.then_inc(sem("x_updated_1a"), 1)

            def route():
                for t in range(2):
                    o, free = take_out(dve, ("router", t))
                    dve.tensor_copy(LG[:, t, :], o[:, 0:NE]).then_inc(free, 1)
                iota = cst[:, C_IOTA:C_IOTA + NE]
                for t in range(2):
                    evacuated(dve, ("router", t))
                    then(dve.max(MX[:, :], LG[:, t, :]))
                    then(dve.max_index(idx[:, :], MX[:, :], LG[:, t, :]))
                    then(dve.tensor_copy(IDXF[:, 2 * t:2 * t + 2], idx[:, 0:2]))
                    then(dve.tensor_tensor(wts[:, t:t + 1], MX[:, 1:2], MX[:, 0:1], ALU.subtract))
                dve.tensor_copy(TOT[:, 0:1], wts[:, 0:1]).then_inc(sem("expert_gap"), 1)
                dve.wait_ge(sem("expert_gap_exp"), 1)
                then(dve.tensor_scalar(wts[:, 2:4], wts[:, 0:2], 1.0, None, ALU.add))
                then(dve.reciprocal(wts[:, 2:4], wts[:, 2:4]))
                then(dve.tensor_tensor(wts[:, 0:2], wts[:, 0:2], wts[:, 2:4], ALU.mult))
                for t in range(2):
                    for c in range(2):
                        ins = dve.tensor_scalar(OH[:, c, :], iota, IDXF[:, 2 * t + c:2 * t + c + 1], None, ALU.is_equal)
                    then(ins)
                    dve.tensor_tensor(SELM[:, t, 0:NE], OH[:, 0, :], OH[:, 1, :], ALU.add)
                    then(dve.tensor_scalar(OH[:, 0, :], OH[:, 0, :], wts[:, 2 + t:3 + t], None, ALU.mult))
                    then(dve.scalar_tensor_tensor(out=COMB[:, t, 0:NE], in0=OH[:, 1, :], scalar=wts[:, t:t + 1],
                                                  in1=OH[:, 0, :], op0=ALU.mult, op1=ALU.add))
                dve.tensor_copy(TOT[:, 0:1], wts[:, 0:1]).then_inc(sem("routed"), 1)
                o, free = take_out(dve, ("pos",))
                dve.tensor_copy(POS[:, :, 0:NE], o[:, 0:2 * NE].rearrange("p (t e) -> p t e", t=2))
                then(dve.tensor_reduce(TOT[:, 1:2], o[:, 2 * NE:3 * NE], AX.X, ALU.max))
                then(dve.tensor_copy(TOT[:, 2:3], o[:, 0:1]))
                dve.tensor_copy(TOT[:, 3:4], o[:, 0:1]).then_inc(free, 1)
                dve.tensor_scalar(flag[:, :], TOT[:, 1:2], P + 0.5, None, ALU.is_gt).then_inc(sem("flag_ready"), 1)
                then(dve.memset(ACC[:, :, :], 0.0))

            def experts(p):
                def one_hot(dst, e, weight):
                    for t in range(2):
                        ins = dve.tensor_scalar(dst[:, t, :], cst[:, C_IOTA + p * P:C_IOTA + (p + 1) * P],
                                                POS[:, t, bass.ds(e, 1)], weight[:, t, bass.ds(e, 1)], ALU.is_equal, ALU.mult)
                    return ins

                def tokens(half, b, n):
                    dve.wait_ge(bank_free[b], n + 1)
                    fs = slice(4 * half, 4 * half + 4)
                    dve.tensor_copy(XTH[:, fs, :], XTF[:, fs, :]).then_inc(sem("tokens_rounded"), 1)

                def tokens_rest(half, count):
                    fs = slice(4 * half, 4 * half + 4)
                    dve.wait_ge(sem("tokens_rounded"), count)
                    dve.tensor_tensor(XTL[:, fs, :], XTF[:, fs, :], XTH[:, fs, :].bitcast(F32), ALU.subtract).then_inc(sem("tokens_ready"), 1)

                def scattered(i, b, n):
                    t, c = i // 2, i % 2
                    dve.wait_ge(bank_full[b], n + 1)
                    y = ACC[:, t, 512 * c:512 * (c + 1)]
                    dve.tensor_tensor(y, bank[b][:, :], y, ALU.add).then_inc(bank_free[b], 1)

                dve.memset(YROW[:, :], 0.0)
                dve.memset(SMT[:, :, :], 0.0).then_inc(sem("moe_cleared"), 1)
                one_hot(GM, 0, SELM).then_inc(sem("gather_ready"), 1)
                for i in range(PAIRS):
                    moe_split(rest, p, 0, i)
                before = 2 * p * (NE + 1)
                for half in range(2):
                    tokens(half, 5, moe_base(p, 5) - GA_PRO + half)
                    tokens_rest(half, before + half + 1)

                def expert(e, more):
                    def turned(j):
                        b, n = moe_at(p, e, "HT", j)
                        dve.wait_ge(sem("expert_rounded"), e * NJ + (p * NE * NJ + j + 1))
                        dve.tensor_tensor(TL[:, 0, :], bank[b][:, :], TH[:, 0, :].bitcast(F32), ALU.subtract).then_inc(bank_free[b], 1)

                    for i, (m, j, c) in enumerate(tiles):
                        if (m, c) == ("g", 1):
                            if j < 2:
                                scattered(2 * j, *moe_at(p, e, "SC", 2 * j))
                            if j:
                                turned(j - 1)
                        if (m, c) == ("u", 1):
                            b, n = moe_at(p, e, "G", j)
                            dve.wait_ge(bank_free[b], n + 1)
                            b, n = moe_at(p, e, "U", j)
                            dve.wait_ge(bank_full[b], n + 1)
                            dve.tensor_tensor(H[:, :], SIL[:, j % 2, :], bank[b][:, :], ALU.mult).then_inc(bank_free[b], 1)
                            if j < 2:
                                scattered(2 * j + 1, *moe_at(p, e, "SC", 2 * j + 1))
                            if j == 2:
                                one_hot(SM, e, COMB).then_inc(sem("scatter_ready"), 1)
                            if j == 4:
                                one_hot(GM, e + 1, SELM).then_inc(sem("gather_ready"), 1)
                            if j == NJ - 1:
                                tokens(0, *moe_at(p, e, "GA", 0))
                                tokens_rest(0, e * 2 + (before + 3))
                        if (m, j, c) == ("d", NJ - 2, 1):
                            turned(NJ - 1)
                            tokens(1, *moe_at(p, e, "GA", 1))
                            tokens_rest(1, e * 2 + (before + 4))
                        if i + PAIRS < PER or more:
                            moe_split(rest, p, e + (i + PAIRS) // PER, (i + PAIRS) % PER)

                with dve.Fori(0, NE - 1) as e:
                    expert(e, True)
                expert(NE - 1, False)
                for i in range(4):
                    scattered(i, 5, moe_base(p, 5) + NE * MOE_USES[5] + i)

            def finish():
                for half in range(2):
                    evacuated(dve, ("gateF", 1, 1, half))
                for t in range(2):
                    then(dve.tensor_tensor(ACC[:, t, :], ACC[:, t, :], GBC_F[:, 1, :], ALU.mult))
                    dve.tensor_tensor(X[:, 2 + t, :], X[:, 2 + t, :], ACC[:, t, :], ALU.add).then_inc(sem("out_row_ready"), 1)

            for L in range(DEPTH):
                mod(L)
                norm(L, "a")
                project(L)
                prepare(L)
                heads(L)
                out_project(L)
                norm(L, "f")
                if L == 0:
                    ffn()
            route()
            experts(0)
            over = overflow(dve)
            with dve.If(over > 0):
                experts(1)
            then(dve.memset(SIL[:, 0, 0:1], 0.0))
            finish()


_INS = ['x', 'c', 'ctx', 'c_ctx', 'mod_w', 'mod_b', 'norm_mix', 'norm_ffn', 'w_in', 'm_conv', 'm_gate_b', 'm_norm',
        'a_qnorm', 'a_knorm', 'l_cq_norm', 'l_ckv_norm', 'l_wuq', 'l_wukv', 'l_qnorm', 'l_knorm', 'w_out',
        'ffn_wg', 'ffn_wu', 'ffn_wd', 'moe_router', 'moe_wg', 'moe_wu', 'moe_wd']


def kernel(**inputs):
    import numpy as _np
    import concourse.bacc as _bacc
    from concourse.bass_utils import run_bass_kernel_spmd as _run

    nc = _bacc.Bacc("TRN2", target_bir_lowering=False, num_devices=1)
    arrays, args = {}, {}
    for name in _INS:
        v = _np.ascontiguousarray(inputs[name])
        arrays[f"in_{name}"] = v
        args[name] = nc.dram_tensor(f"in_{name}", v.shape, F32, kind="ExternalInput").ap()
    arrays["in_constants"] = constants()
    consts = nc.dram_tensor("in_constants", (P, C_END), F32, kind="ExternalInput").ap()
    out = nc.dram_tensor("out", (1, 256, D), F32, kind="ExternalOutput").ap()
    build(nc, args, consts, out)
    r = _run(nc, [arrays], core_ids=[0])
    return r.results[0]["out"]
```

```python
from contextlib import ExitStack

import numpy as np
import concourse.bass as bass
from concourse import mybir

F32 = mybir.dt.float32
F32R = mybir.dt.float32r
I32 = mybir.dt.int32
U32 = mybir.dt.uint32
ALU = mybir.AluOpType
ACT = mybir.ActivationFunctionType
AX = mybir.AxisListType

P = 128
NT = 4
TOK = NT * P
D = 1024
KT = D // P
EPS = 1e-6
DEPTH = 2
MH, MD = 4, 96
MW = MH * MD
AH, AKV, AD = 6, 2, 64
LH, NOPE, ROPE = 4, 64, 32
LQK = NOPE + ROPE
QRANK, KVRANK = 256, 128
FF = 3584
NE = 8
FS = 512
NJ = FF // FS
NEG = -1e30
WARM_UP = {"norm_a": (0, 15), "norm_f": (6, 4), "mla": (14, 14), "heads": (3, 3), "out": (2, 1)}
RING = 6
SLOT = 4 * 512
PAIRS = 3

C_ID, C_SEL, C_MF, C_MB = 0, 128, 640, 1024
C_COSA, C_SINA, C_COSL, C_SINL = 1408, 1536, 1664, 1728
C_TRI, C_ONE, C_IOTA, C_STACK, C_END = 1792, 1920, 2048, 2304, 2306
G_M, G_AQ, G_AK, G_LQ, G_LK, G_GB, G_END = 0, 384, 448, 512, 608, 704, 720
W_Q, W_K, W_OG, W_GQA, W_AVCQ, W_CKV, W_MV = (0, 384), (384, 384), (1152, 400), (1552, 512), (2064, 384), (2448, 160), (768, 384)
ROWS_OF_W = (W_AVCQ, W_CKV, W_OG, W_GQA, W_MV)


def constants():
    c = np.zeros((P, C_END), np.float32)
    c[:, C_ID:C_ID + P] = np.eye(P)
    for h in range(4):
        c[h, C_SEL + h * P:C_SEL + (h + 1) * P] = 1
    t, s = np.arange(P)[:, None], np.arange(P)[None, :]
    c[:, C_MF + 128:C_MF + 256] = np.where(s <= t, 0, NEG)
    c[:, C_MF + 256:C_MF + 384] = NEG
    c[:, C_MB:C_MB + 128] = NEG
    c[:, C_MB + 128:C_MB + 256] = np.where(s >= t, 0, NEG)
    tok = np.arange(256)
    rows, cols = (tok // 64).astype(np.float32), (tok % 64).astype(np.float32)
    for dim, cc, cs in ((AD, C_COSA, C_SINA), (ROPE, C_COSL, C_SINL)):
        nf = dim // 4
        inv = (np.float32(10000.0) ** (-np.arange(nf, dtype=np.float32) / np.float32(nf))).astype(np.float32)
        ar, ac = rows[:, None] * inv, cols[:, None] * inv
        ang = np.concatenate([ar, ar, ac, ac], -1)
        sign = np.tile(np.repeat(np.array([-1.0, 1.0], np.float32), nf), 2)
        cos, sin = np.cos(ang), np.sin(ang) * sign
        for i in range(2):
            c[:, cc + i * dim:cc + (i + 1) * dim] = cos[i * P:(i + 1) * P]
            c[:, cs + i * dim:cs + (i + 1) * dim] = sin[i * P:(i + 1) * P]
    c[:, C_TRI:C_TRI + P] = t < s
    c[:, C_ONE:C_ONE + P] = 1
    c[:, C_IOTA:C_IOTA + 256] = np.arange(256)
    c[:, C_STACK:C_END] = t % 2 == np.arange(2)
    return c


class BankPlan:

    def __init__(self):
        self.count = [0] * 8
        self.at = {}

    def add(self, name, bank):
        self.at[name] = (bank, self.count[bank])
        self.count[bank] += 1


def query_tiles(layer):
    return [0, 1, 2, 3] if layer == 0 else [2, 3]


def mixer_units(layer):
    att = [("A", h, t) for t in query_tiles(layer) for h in range(AH + LH)]
    mem = [("M", h, t) for t in query_tiles(layer) for h in range(MH)]
    out = []
    for i, u in enumerate(att):
        out.append(u)
        if (i + 1) * len(mem) // len(att) > i * len(mem) // len(att):
            out.append(mem.pop(0))
    return out + mem


def modulation_pieces():
    units = mixer_units(0)
    return {units[(i + 1) * len(units) // 14]: i for i in range(13)}


def plan_banks():
    plan = BankPlan()
    for i in range(12):
        plan.add(("mod", 0, i), i % 2)
        if i:
            plan.add(("modT", 0, i - 1), 2 + (i - 1) % 2)
    plan.add(("modT", 0, 11), 3)
    pieces = modulation_pieces()
    for L in range(DEPTH):
        for k in range(KT):
            plan.add(("norm", L, "a", k), k % 4)
        for h in range(8):
            plan.add(("conv", L, h), (h + 4) % 8)
        for s in range(len(ROWS_OF_W)):
            for t in range(NT):
                plan.add(("proj", L, s, t), 4 * ((s + 1) % 2) + t)
        for g in range(3):
            plan.add(("mlaT", L, g), g)
        for g in range(4):
            plan.add(("gateT", L, g), 4 + g)
        for g in range(4):
            plan.add(("gqaT", L, g), g)
        for t in range(NT):
            plan.add(("mlaq", L, t), 2 * (t % 2))
            plan.add(("mlakv", L, t), 2 * (t % 2) + 1)
        plan.add(("stab", L), 7)
        for g in range(8):
            plan.add(("mlaH", L, g), (g + 4) % 8)
        for unit in mixer_units(L):
            for part, b in ((("S", 0), ("T", 1), ("O", 2)) if unit[0] == "A" else
                            (("CF", 3), ("CB", 4), ("S", 5), ("T", 6), ("O", 7))):
                plan.add((part, L, unit), b)
            if L == 0 and unit in pieces:
                i = pieces[unit]
                if i < 12:
                    plan.add(("mod", 1, i), 3)
                if i:
                    plan.add(("modT", 1, i - 1), 4)
        gs = (0, 1) if L == 0 else (1,)
        for g in gs:
            for half in range(2):
                plan.add(("gateA", L, g, half), 4 + half)
        for k in range(KT):
            plan.add(("outT", L, k), k % 4)
        for half in range(2):
            for t in query_tiles(L):
                plan.add(("out", L, half, t), 4 * half + t)
        for k in range(KT):
            plan.add(("norm", L, "f", k), k % 4)
        if L == 0:
            for j in range(NJ):
                for kind in ("G", "U", "Y0", "Y1"):
                    for t in range(NT):
                        plan.add((kind, j, t), (0 if kind in ("G", "Y0") else 4) + t)
            for g in gs:
                for half in range(2):
                    plan.add(("gateF", L, g, half), 4 + half)
        else:
            for t in range(2):
                plan.add(("router", t), 4 + t)
            plan.add(("pos",), 4)
            for half in range(2):
                plan.add(("gateF", L, 1, half), 6 + half)
    return plan


MOE_USES = {0: 4, 1: 3, 2: 4, 3: 3, 4: 7, 5: 7, 6: 1, 7: 1}


def moe_place(name):
    kind, i = name
    if kind == "G":
        return i % 2, i // 2
    if kind == "U":
        return 2 + i % 2, i // 2
    if kind == "HT":
        return 4, i
    if kind == "SC":
        return 5, i
    if kind == "ST":
        return 5, 4
    if kind == "GA":
        return 5, 5 + i
    return 6 + i, 0


def moe_tiles():
    out = []
    for j in range(NJ):
        out += [("g", j, 0), ("g", j, 1), ("u", j, 0), ("u", j, 1)]
        if j:
            out += [("d", j - 1, 0), ("d", j - 1, 1)]
    return out + [("d", NJ - 1, 0), ("d", NJ - 1, 1)]


def build(nc, a, consts, out):
    plan = plan_banks()
    pieces = modulation_pieces()
    tiles = moe_tiles()
    PER = len(tiles)
    assert PER % RING == 0

    with ExitStack() as ctx:
        def sb(name, shape, dt=F32):
            return ctx.enter_context(nc.sbuf_tensor(name, shape, dt))

        sems = {}

        def sem(name):
            if name not in sems:
                sems[name] = ctx.enter_context(nc.semaphore(name))
            return sems[name]

        places = {}

        def placed_sb(name, shape):
            t = sb(name, shape)
            places[name] = nc.sbuf_base - 4 * int(np.prod(shape[1:]))
            return t

        def over(name, under, at, shape):
            return nc.alloc_sbuf_tensor_at(name, shape, F32R, offset=places[under] + 4 * at)

        ring = placed_sb("ring", [P, RING * SLOT])
        spare = placed_sb("spare", [P, SLOT])
        mix = placed_sb("mix", [P, 7 * SLOT])
        X = sb("X", [P, NT, D])
        hT = placed_sb("hT", [P, KT * TOK])
        bigA = placed_sb("bigA", [P, NT * D])
        bigB = placed_sb("bigB", [P, 8 * 512])
        cst = sb("cst", [P, C_END])
        gains = sb("gains", [P, DEPTH, G_END])
        scr = placed_sb("scr", [P, 2048])
        crow = sb("crow", [4, 2, 512])
        small = sb("small", [P, 360])
        modT = sb("modT", [P, DEPTH, 6, KT, 2])
        cvec = sb("cvec", [P, KT, 2])
        csplit = sb("csplit", [P, KT, 4], F32R)
        convw = sb("convw", [MD, DEPTH, 8, 3])
        idx = sb("idx", [P, 8], U32)
        flag = sb("flag", [P, 1], I32)

        def view(t, at, *dims):
            n = int(np.prod(dims))
            v = t[:, at:at + n]
            if len(dims) == 1:
                return v
            if len(dims) == 2:
                return v.rearrange("p (a b) -> p a b", a=dims[0])
            return v.rearrange("p (a b c) -> p a b c", a=dims[0], b=dims[1])

        PMO = view(mix, 0, NT, 400)
        PG = view(mix, 1600, NT, 512)
        PAVCQ = view(mix, 3648, NT, 384)
        PCKV = view(mix, 5184, NT, 160)
        PMV = view(mix, 5824, NT, 384)
        QK = view(mix, 7360, 8, TOK)
        GT = view(mix, 11456, 4, TOK)
        GA = view(mix, 13504, NT, 16)
        LF = view(mix, 13568, NT, 8)
        gtmp = view(mix, 13632, NT, 8)
        assert 13632 + 64 <= 7 * SLOT
        PROJ = {W_OG: PMO, W_GQA: PG, W_AVCQ: PAVCQ, W_CKV: PCKV, W_MV: PMV}
        HT = view(hT, 0, KT, TOK)
        VM = view(hT, 0, NT, LH, 64)
        CT = view(hT, 1024, 3, TOK)
        PA = view(hT, 1024, 2, 512)
        PT = view(hT, 2048, 512)
        EF = view(hT, 2560, 512)
        EB = view(hT, 3072, 512)
        WT = view(hT, 3584, 512)
        PTM = view(mix, 1600, 512)
        XN = view(bigA, 0, NT, D)
        OROW = XN
        QR = view(bigA, 0, NT, LH, LQK)
        KR = view(bigA, 1536, NT, LH, LQK)
        rows_f = view(bigA, 3072, 2, 512)
        rows_b = view(hT, 2560, 2, 512)
        MT = view(bigB, 0, 8, TOK)
        KSQ = view(bigB, 0, NT, LH, 64)
        YACC = view(bigA, 0, NT, D)
        GBC_A = view(mix, 2112, 2, D)
        TMPX = view(mix, 4608, 2, 512)
        TMPK = view(scr, 0, 2, 512)
        ACC = view(bigB, 0, 2, D)
        XTF = view(bigB, 2048, KT, P)
        YROW = view(bigB, 3072, D)
        GM = view(bigA, 0, 2, P)
        SM = view(bigA, 256, 2, P)
        SMT = view(bigA, 512, 2, P)
        GBC_F = view(hT, 0, 2, D)
        SQ = view(scr, 0, NT, 512)
        SIL = view(scr, 0, 2, 512)
        H = view(scr, 1024, 512)
        SILF = view(scr, 0, NT, 512)
        MODROW = view(scr, 0, 2, 512)
        MODB = view(scr, 1024, 2, 512)
        BIAS = ((hT[0:4, 0:4096], 0), (mix[0:4, 12288:14336], 4096))
        ident = cst[:, C_ID:C_ID + P]

        HH, HL = over("HH", "hT", 0, [P, KT, TOK]), over("HL", "bigB", 0, [P, KT, TOK])
        TH, TL = over("TH", "mix", 12288, [P, NT, 512]), over("TL", "spare", 0, [P, NT, 512])
        pairs = {"A": (over("WAH", "spare", 0, [P, SLOT]), over("WAL", "mix", 11456, [P, SLOT])),
                 "B": (over("WBH", "bigA", 0, [P, SLOT]), over("WBL", "bigA", SLOT, [P, SLOT]))}
        for i in range(PAIRS):
            pairs[i] = (over(f"W{i}H", "mix", 2 * SLOT * i, [P, SLOT]), over(f"W{i}L", "mix", 2 * SLOT * i + SLOT, [P, SLOT]))
        XTH, XTL = TH[:, 2:4, :].rearrange("p a (b c) -> p (a b) c", c=P), TL[:, 2:4, :].rearrange("p a (b c) -> p (a b) c", c=P)

        CH, CL = over("CH", "spare", 0, [P, 2, 512]), over("CL", "spare", 1024, [P, 2, 512])
        MASKS, SELECT, IDENT = over("MASKS", "mix", 2112, [P, 768]), over("SELECT", "mix", 2880, [P, 512]), over("IDENT", "mix", 3392, [P, P])

        at_small = [0]

        def tiny(n):
            at_small[0] += n
            assert at_small[0] <= 360
            return small[:, at_small[0] - n:at_small[0]]

        normG = tiny(32).rearrange("p (l w k) -> p l w k", l=2, w=2)
        cqG = tiny(6).rearrange("p (l k) -> p l k", l=2)
        ss, rs = tiny(8), tiny(4)
        gss = tiny(48)
        grs = tiny(48)
        nmax, rsum, rinv, warm = tiny(1), tiny(4), tiny(1), tiny(1)
        den = tiny(2)
        dabs = tiny(2)
        stab = tiny(64).rearrange("p (k t h) -> p k t h", k=4, t=4)
        LG = tiny(16).rearrange("p (t e) -> p t e", t=2)
        RT = tiny(64).rearrange("p (k e) -> p k e", k=8)
        MX, IDXF = tiny(8), tiny(4)
        wts = tiny(4)
        TOT = tiny(8)
        rt = sb("rt", [P, 3, 2, 9])
        SELM, COMB, POS = rt[:, 0], rt[:, 1], rt[:, 2]
        OH = view(scr, 0, 2, 8)

        bank = [ctx.enter_context(nc.psum_tensor(f"bank{b}", [P, 512], F32)) for b in range(8)]
        bank_full = [sem(f"bank_full{b}") for b in range(8)]
        bank_free = [sem(f"bank_free{b}") for b in range(8)]
        slot_full = [sem(f"slot_full{s}") for s in range(RING)]
        tile_used = sem("tile_used")
        split_hi, split_lo = sem("split_hi"), sem("split_lo")

        def take_out(eng, name):
            b, n = plan.at[name]
            eng.wait_ge(bank_full[b], n + 1)
            return bank[b], bank_free[b]

        def evacuated(eng, name):
            b, n = plan.at[name]
            eng.wait_ge(bank_free[b], n + 1)

        FFN_STRIDE = 2

        def ffn_at(kind, j, t):
            b, n = plan.at[(kind, 0, t)]
            return b, j * FFN_STRIDE + n

        GATHER_BANKS, SCATTER_BANKS = (4, 5), (0, 1, 2, 3)

        def moe_base(p, b):
            before, after = GATHER_BANKS.count(b), SCATTER_BANKS.count(b)
            return plan.count[b] + p * (NE * MOE_USES[b] + before + after) + before

        def first_gather(p, half):
            b = GATHER_BANKS[half]
            return b, moe_base(p, b) - 1

        def last_scatter(p, i):
            b = SCATTER_BANKS[i]
            return b, moe_base(p, b) + NE * MOE_USES[b]

        def moe_at(p, e, kind, i=0):
            b, k = moe_place((kind, i))
            return b, e * MOE_USES[b] + (moe_base(p, b) + k)

        loads, freed, splits = [], [], []
        used = [0]

        def kn(ap, k0, nk, c0, n):
            return ap[k0 * P:(k0 + nk) * P, c0:c0 + n].rearrange("(k p) n -> p k n", p=P)

        def load(src, nk, n, last, pair=None):
            if last is None:
                used[0] += 1
            free = ("product", last) if last else ("used", used[0])
            if pair is None:
                freed.append(free)
            else:
                splits.append((len(loads), pair, free))
                freed.append(("split", len(splits)))
            loads.append((len(loads) % RING, src, nk, n))

        starts = {}

        def load_modulation(L):
            for i in range(12):
                for half in range(2):
                    src = kn(a["mod_w"][L], 4 * half, 4, 512 * i, 512)
                    if L == 0:
                        load(src, 4, 512, ("mod", L, i) if half else None, (2 * i + half) % PAIRS)
                    else:
                        load(src, 4, 512, ("mod", L, i))

        load_modulation(0)
        for L in range(DEPTH):
            starts["in", L] = len(splits)
            for s, (c0, n) in enumerate((W_Q, W_K) + ROWS_OF_W):
                last = ("conv", L, 4 * s + 3) if s < 2 else ("proj", L, s - 2, NT - 1)
                for half in range(2):
                    load(kn(a["w_in"][L], 4 * half, 4, c0, n), 4, n, last if half else None, "AB"[half])
            load(kn(a["l_wuq"][L], 0, 2, 0, LH * LQK), 2, LH * LQK, ("mlaq", L, NT - 1))
            load(kn(a["l_wukv"][L], 0, 1, 0, 512), 1, 512, ("mlakv", L, NT - 1))
            if L == 0:
                load_modulation(1)
            starts["out", L] = len(splits)
            for c in range(2):
                for half in range(2):
                    load(kn(a["w_out"][L], 4 * half, 4, 512 * c, 512), 4, 512, ("out", L, c, NT - 1) if half else None, "AB"[half])
            if L == 0:
                starts["ffn"] = len(splits)
                ffn_from = len(loads)
                for j in range(NJ):
                    for n, (w, kind) in enumerate((("ffn_wg", "G"), ("ffn_wu", "U"))):
                        for half in range(2):
                            load(kn(a[w][0], 4 * half, 4, FS * j, FS), 4, FS, (kind, j, NT - 1) if half else None, (2 * n + half) % PAIRS)
                    for c in range(2):
                        load(kn(a["ffn_wd"][0], 4 * j, 4, 512 * c, 512), 4, 512, (f"Y{c}", j, NT - 1), (4 + c) % PAIRS)
                ffn_to = len(loads)
        assert PER % PAIRS == 0 and 6 % PAIRS == 0 and RING == 6
        N0, M0, U0 = len(loads), len(splits), used[0]
        slot_uses = [0] * RING
        use_of = []
        for slot, *_ in loads:
            use_of.append(slot_uses[slot])
            slot_uses[slot] += 1
        first_slot = N0 % RING

        def slot_ap(slot, nk, n):
            return view(ring, slot * SLOT, nk * n).rearrange("p (k n) -> p k n", k=nk)

        def pair_ap(pair, nk, n):
            return [x[:, 0:nk * n].rearrange("p (k n) -> p k n", k=nk) for x in pairs[pair]]

        def is_free(eng, free):
            kind, what = free
            if kind == "product":
                b, n = plan.at[what]
                eng.wait_ge(bank_full[b], n + 1)
            elif kind == "used":
                eng.wait_ge(tile_used, what)
            else:
                eng.wait_ge(split_lo, what)

        moe_used = [m == "d" and j < NJ - 1 or m != "d" and c == 0 for m, j, c in tiles]
        USED_PER = sum(moe_used)

        def moe_src(e, tile):
            m, j, c = tile
            w = {"g": "moe_wg", "u": "moe_wu", "d": "moe_wd"}[m]
            w = a[w][0].rearrange("e r c -> (e r) c")
            if m == "d":
                src = w[bass.ds(e * FF + FS * j, FS), 512 * c:512 * (c + 1)]
            else:
                src = w[bass.ds(e * D + 512 * c, 512), FS * j:FS * (j + 1)]
            return src.rearrange("(k p) n -> p k n", p=P)

        def moe_left(eng, p, e, i):
            m, j, c = tiles[i]
            if moe_used[i]:
                eng.wait_ge(tile_used, e * USED_PER + (U0 + p * NE * USED_PER + sum(moe_used[:i + 1])))
            else:
                b, n = moe_at(p, e, {"g": "G", "u": "U", "d": "Y"}[m], j if m != "d" else c)
                eng.wait_ge(bank_full[b], n + 1)

        def tile_no(p, e, i):
            return e * PER + (M0 + p * NE * PER + i)

        def moe_slot(p, e, i):
            slot = (first_slot + i) % RING
            return slot, e * (16 * PER // RING) + 16 * (slot_uses[slot] + p * NE * (PER // RING) + i // RING + 1)

        def round_tile(act, hi, raw):
            act.activation(hi, raw, ACT.Copy).then_inc(split_hi, 1)

        def rest_tile(dve, n, hi, lo, raw):
            dve.wait_ge(split_hi, n)
            dve.tensor_tensor(lo, raw, hi.bitcast(F32), ALU.subtract).then_inc(split_lo, 1)

        def static_split(eng, n):
            tile, pair, _ = splits[n]
            slot, _, nk, w = loads[tile]
            hi, lo = pair_ap(pair, nk, w)
            raw = slot_ap(slot, nk, w)
            if eng is rest:
                rest_tile(nc.vector, n + 1, hi, lo, raw)
                return
            before = [m for m in range(n) if splits[m][1] == pair]
            if before:
                is_free(nc.scalar, splits[before[-1]][2])
            nc.scalar.wait_ge(slot_full[slot], 16 * (use_of[tile] + 1))
            round_tile(nc.scalar, hi, raw)

        rest = "VectorE"

        def ffn_split(eng, j, i):
            slot = (ffn_from + i) % RING
            hi, lo = pair_ap(i % PAIRS, 4, 512)
            raw = slot_ap(slot, 4, 512)
            if eng is rest:
                rest_tile(nc.vector, j * 6 + (starts["ffn"] + i + 1), hi, lo, raw)
                return
            nc.scalar.wait_ge(slot_full[slot], j * 16 + 16 * (use_of[ffn_from + i] + 1))
            round_tile(nc.scalar, hi, raw)

        def ffn_left(act, j, i):
            if i in (0, 2):
                act.wait_ge(tile_used, j * 2 + (splits[starts["ffn"] + i][2][1]))
            else:
                b, n = ffn_at({1: "G", 3: "U", 4: "Y0", 5: "Y1"}[i], j, NT - 1)
                act.wait_ge(bank_full[b], n + 1)

        def moe_split(eng, p, e, i):
            hi, lo = pair_ap(i % PAIRS, 4, 512)
            slot, landed = moe_slot(p, e, i)
            raw = slot_ap(slot, 4, 512)
            if eng is rest:
                rest_tile(nc.vector, tile_no(p, e, i) + 1, hi, lo, raw)
                return
            nc.scalar.wait_ge(slot_full[slot], landed)
            round_tile(nc.scalar, hi, raw)

        def overflow(eng):
            eng.wait_ge(sem("flag_ready"), 1)
            return eng.value_load(flag[0:1, 0:1], min_val=0, max_val=1)

        def conv_from(L, h):
            return 256 if L == DEPTH - 1 and h < MH else 0

        def columns_for(L, w, t):
            return slice(MW if L == DEPTH - 1 and w == W_OG and t < 2 else 0, w[1])

        def groups(L):
            return (0, 1) if L == 0 else (1,)

        def paired(t, o):
            return (PG[:, t, 0:384].rearrange("p (n g d) -> p g n d", g=AKV, d=AD),
                    o[:, 0:384].rearrange("p (g n d) -> p g n d", g=AKV, d=AD))

        def modulated(eng, to, o, L, w, k, g0):
            shift, scale = (0, 1) if w == "a" else (3, 4)
            for g in range(g0, 2):
                cols = slice(256 * g, 256 * (g + 1))
                sc, sh = modT[:, L, scale, k, g:g + 1], modT[:, L, shift, k, g:g + 1]
                if eng is nc.scalar:
                    ins = eng.activation(to[:, cols], o[:, cols], ACT.Identity, scale=sc, bias=sh)
                else:
                    ins = eng.tensor_scalar(to[:, cols], o[:, cols], sc, sh, ALU.mult, ALU.add)
            return ins

        block = ctx.enter_context(nc.Block())

        @block.sync
        def _(sp):
            def fill(n):
                slot, src, nk, w = loads[n]
                if n >= RING:
                    is_free(sp, freed[n - RING])
                sp.dma_start(slot_ap(slot, nk, w), src).then_inc(slot_full[slot], 16)

            for n in range(ffn_from + 6):
                fill(n)
            wg, wu, wd = a["ffn_wg"][0], a["ffn_wu"][0], a["ffn_wd"][0]
            with sp.Fori(1, NJ) as j:
                for i in range(6):
                    slot = (ffn_from + i) % RING
                    sp.wait_ge(split_lo, (j - 1) * 6 + (starts["ffn"] + i + 1))
                    if i < 4:
                        src = (wg, wu)[i // 2][512 * (i % 2):512 * (i % 2 + 1), bass.ds(j * FS, FS)]
                    else:
                        src = wd[bass.ds(j * FS, FS), 512 * (i % 2):512 * (i % 2 + 1)]
                    sp.dma_start(slot_ap(slot, 4, 512), src.rearrange("(k p) n -> p k n", p=P)).then_inc(slot_full[slot], 16)
            for n in range(ffn_to, len(loads)):
                fill(n)

            def expert(p, e, i):
                slot, _ = moe_slot(p, e, i)
                sp.dma_start(slot_ap(slot, 4, 512), moe_src(e, tiles[i])).then_inc(slot_full[slot], 16)

            def experts(p):
                for i in range(RING):
                    if p:
                        sp.wait_ge(split_lo, tile_no(0, NE - 1, PER - RING + i) + 1)
                    else:
                        is_free(sp, freed[N0 - RING + i])
                    expert(p, 0, i)

                def rest_of(e, n):
                    for i in range(RING, n):
                        sp.wait_ge(split_lo, tile_no(p, e, i - RING) + 1)
                        expert(p, e + i // PER, i % PER)
                with sp.Fori(0, NE - 1) as e:
                    rest_of(e, PER + RING)
                rest_of(NE - 1, PER)

            experts(0)
            over = overflow(sp)
            with sp.If(over > 0):
                experts(1)
            for t in range(2):
                sp.wait_ge(sem("out_row_ready"), t + 1)
                sp.dma_start(out[0, t * P:(t + 1) * P, :], X[:, 2 + t, :]).then_inc(sem("stored"), 16)
            sp.wait_ge(sem("stored"), 32)

        @block.gpsimd
        def _(pool):
            with nc.allow_non_contiguous_dma("small parameters"):
                pool.dma_start(cst[:, :], consts).then_inc(sem("consts_loaded"), 16)
                for n, (rows, m) in enumerate(BIAS):
                    pool.memset(rows, 0.0).then_inc(sem("bias_cleared"), 1)
                    pool.wait_ge(sem("bias_cleared"), n + 1)
                    pool.dma_start(rows[0:2, :], a["mod_b"][0, m:m + rows.shape[-1]].partition_broadcast(2)).then_inc(sem(f"bias_loaded{n}"), 16)
                for L in range(DEPTH):
                    for w, name in enumerate(("norm_mix", "norm_ffn")):
                        pool.dma_start(normG[:, L, w, :], a[name][L].rearrange("(k p) -> p k", p=P)).then_inc(sem("norms_loaded"), 16)
                for L in range(DEPTH):
                    pool.dma_start(cqG[:, L, 0:2], a["l_cq_norm"][L].rearrange("(k p) -> p k", p=P)).then_inc(sem("params_loaded"), 16)
                    pool.dma_start(cqG[:, L, 2:3], a["l_ckv_norm"][L].rearrange("(k p) -> p k", p=P)).then_inc(sem("params_loaded"), 16)
                    for at, name, n in ((G_M, "m_norm", MW), (G_AQ, "a_qnorm", AD), (G_AK, "a_knorm", AD),
                                        (G_LQ, "l_qnorm", LQK), (G_LK, "l_knorm", LQK), (G_GB, "m_gate_b", 16)):
                        pool.dma_start(gains[:, L, at:at + n], a[name][L].partition_broadcast(P)).then_inc(sem("params_loaded"), 16)
                    for h in range(8):
                        pool.dma_start(convw[:, L, h, :], a["m_conv"][L, :, h * MD:(h + 1) * MD].rearrange("k c -> c k"))\
                            .then_inc(sem("params_loaded"), 16)
                pool.dma_start(RT[:, :, :], a["moe_router"][0].rearrange("(k p) e -> p k e", p=P)).then_inc(sem("params_loaded"), 16)
                for i in range(12):
                    if i < 2:
                        pool.wait_ge(sem("mla_ready0"), 1)
                    else:
                        evacuated(pool, ("mod", 1, i - 2))
                    pool.dma_start(MODB[0:2, i % 2, :], a["mod_b"][1, 512 * i:512 * (i + 1)].partition_broadcast(2))\
                        .then_inc(sem(f"modb_loaded{i % 2}"), 16)
                for k in range(KT):
                    b, n = plan.at["norm", 0, "f", k]
                    pool.wait_ge(bank_full[b], n + 1)
                pool.memset(YACC[:, :, :], 0.0).then_inc(sem("sums_cleared"), 1)
                pool.wait_ge(sem("x_updated_1f"), 1)
                pool.memset(ACC[:, :, :], 0.0).then_inc(sem("sums_cleared"), 1)
        PARAMS = 16 * (DEPTH * (2 + 6 + 8) + 1)

        @block.tensor
        def _(pe):
            taken = [0]

            def tile():
                n = taken[0]
                taken[0] += 1
                slot, _, nk, w = loads[n]
                pe.wait_ge(slot_full[slot], 16 * (use_of[n] + 1))
                return slot_ap(slot, nk, w)

            split_taken = [0]

            def split_tile():
                n = split_taken[0]
                split_taken[0] += 1
                tile, pair, _ = splits[n]
                _, _, nk, w = loads[tile]
                taken[0] = tile + 1
                pe.wait_ge(split_lo, n + 1)
                return pair_ap(pair, nk, w)

            def three(o, x, w, start, stop):
                pe.matmul(o, x[0], w[0], start=start, stop=False)
                pe.matmul(o, x[0], w[1], start=False, stop=False)
                return pe.matmul(o, x[1], w[0], start=False, stop=stop)

            def product(name):
                b, n = plan.at[name]
                if n:
                    pe.wait_ge(bank_free[b], n)
                return bank[b], bank_full[b]

            def keep_warm(before, times):
                o, _ = product(before)
                for _ in range(times):
                    pe.matmul(o[:, :], ident, cst[:, 0:512], start=True, stop=True)

            def modulation(L, i):
                if i < 12:
                    o, full = product(("mod", L, i))
                    for half in range(2):
                        w = split_tile() if L == 0 else tile()
                        for k in range(4):
                            kk = 4 * half + k
                            if L == 0:
                                pe.matmul(o[0:4, :], csplit[:, kk, :], w[0][:, k, :], start=kk == 0, stop=False)
                                mm = pe.matmul(o[0:4, :], csplit[:, kk, :], w[1][:, k, :], start=False, stop=kk == KT - 1)
                            else:
                                mm = pe.matmul(o[0:2, :], cvec[:, kk, :], w[:, k, :], start=kk == 0, stop=kk == KT - 1)
                        if L == 0 and not half:
                            mm.then_inc(tile_used, 1)
                    mm.then_inc(full, 1)
                if i:
                    evacuated(pe, ("mod", L, i - 1))
                    o, full = product(("modT", L, i - 1))
                    for k in range(4):
                        cols = slice(k * P, (k + 1) * P)
                        if L == 0:
                            mm = pe.matmul(o[:, 2 * k:2 * k + 2], MODROW[0:4, (i - 1) % 2, cols], cst[0:4, C_STACK:C_END], start=True, stop=True)
                        else:
                            mm = pe.transpose(o[:, 2 * k:2 * k + 2], MODROW[0:2, (i - 1) % 2, cols], ident[0:2, 0:2])
                    mm.then_inc(full, 1)

            def norm(L, w):
                ts = [t for g in (groups(L) if w == "f" else (0, 1)) for t in (2 * g, 2 * g + 1)]
                keep_warm(("norm", L, w, 0), WARM_UP[f"norm_{w}"][L])
                pe.wait_ge(sem(f"normed_{L}{w}"), len(ts))
                for k in range(KT):
                    o, full = product(("norm", L, w, k))
                    for t in ts:
                        mm = pe.transpose(o[:, t * P:(t + 1) * P], XN[:, t, k * P:(k + 1) * P], ident)
                    mm.then_inc(full, 1)

            def columns_ready(L, kind, *w):
                evacuated(pe, (kind, L, *w, KT - 2))
                evacuated(pe, (kind, L, *w, KT - 1))

            def features(k, cols):
                return HH[:, k, cols], HL[:, k, cols]

            def project(L):
                for c in range(2):
                    banks = [product(("conv", L, 4 * c + h)) for h in range(4)]
                    for half in range(2):
                        w = split_tile()
                        if c == 0:
                            pe.wait_ge(sem(f"features_{L}a"), 4 * half + 4)
                        for h, (o, full) in enumerate(banks):
                            for k in range(4):
                                cols = slice(h * MD, (h + 1) * MD)
                                toks = slice(conv_from(L, 4 * c), TOK)
                                x, y = (w[0][:, k, cols], w[1][:, k, cols]), features(4 * half + k, toks)
                                mm = three(o[0:MD, toks], x, y, half + k == 0, half + k == 4)
                            if half:
                                mm.then_inc(full, 1)
                        if not half:
                            mm.then_inc(tile_used, 1)
                for s, w in enumerate(ROWS_OF_W):
                    rows_product([("proj", L, s, t) for t in range(NT)], range(NT), [columns_for(L, w, t) for t in range(NT)])

            def rows_product(names, ts, columns):
                banks = [product(name) for name in names]
                for half in range(2):
                    w = split_tile()
                    for t, (o, full), cols in zip(ts, banks, columns):
                        for k in range(4):
                            mm = three(o[:, cols], features(4 * half + k, slice(t * P, (t + 1) * P)),
                                       (w[0][:, k, cols], w[1][:, k, cols]), half + k == 0, half + k == 4)
                        if half:
                            mm.then_inc(full, 1)
                    if not half:
                        mm.then_inc(tile_used, 1)

            def prepare(L):
                pe.wait_ge(sem(f"latent_ready{L}"), 1)
                for g in range(3):
                    o, full = product(("mlaT", L, g))
                    for t in range(NT):
                        src = PAVCQ[:, t, 128 + g * P:128 + (g + 1) * P] if g < 2 else PCKV[:, t, 0:P]
                        mm = pe.transpose(o[:, t * P:(t + 1) * P], src, ident)
                    mm.then_inc(full, 1)
                pe.wait_ge(sem(f"gates_ready{L}"), 1)
                for g, src in enumerate((GA[:, :, 0:4], LF[:, :, 0:4], GA[:, :, 8:12], LF[:, :, 4:8])):
                    o, full = product(("gateT", L, g))
                    for t in range(NT):
                        mm = pe.transpose(o[0:4, t * P:(t + 1) * P], src[:, t, :], ident)
                    mm.then_inc(full, 1)
                pe.wait_ge(sem(f"gqa_ready{L}"), 1)
                for g in range(4):
                    o, full = product(("gqaT", L, g))
                    for t in range(NT):
                        mm = pe.transpose(o[:, t * P:(t + 1) * P], PG[:, t, g * P:(g + 1) * P], ident)
                    mm.then_inc(full, 1)
                wq, wkv = tile(), tile()
                for t in range(NT):
                    o, full = product(("mlaq", L, t))
                    for k in range(2):
                        mm = pe.matmul(o[:, 0:LH * LQK], CT[:, k, t * P:(t + 1) * P], wq[:, k, :], start=k == 0, stop=k == 1)
                    mm.then_inc(full, 1)
                    o, full = product(("mlakv", L, t))
                    pe.matmul(o[:, :], CT[:, 2, t * P:(t + 1) * P], wkv[:, 0, :], start=True, stop=True).then_inc(full, 1)
                pe.wait_ge(sem(f"stabilisers{L}"), 2)
                o, full = product(("stab", L))
                for k, (rows, r) in enumerate(((rows_f, 1), (rows_b, 1), (rows_f, 0), (rows_b, 0))):
                    for t in range(NT):
                        mm = pe.transpose(o[:, 16 * k + 4 * t:16 * k + 4 * t + 4], rows[0:4, r, t * P:(t + 1) * P],
                                          ident[0:4, 0:4])
                mm.then_inc(full, 1)
                keep_warm(("mlaH", L, 0), WARM_UP["mla"][L])
                pe.wait_ge(sem(f"mla_ready{L}"), 1)
                for g in range(8):
                    o, full = product(("mlaH", L, g))
                    for t in range(NT):
                        mm = pe.transpose(o[0:LQK, t * P:(t + 1) * P], (QR if g < 4 else KR)[:, t, g % 4, :], ident)
                    mm.then_inc(full, 1)

            def heads(L):
                keep_warm(("CF", L, [u for u in mixer_units(L) if u[0] == "M"][0]), WARM_UP["heads"][L])
                for g in range(4):
                    evacuated(pe, ("gqaT", L, g))
                for g in range(8):
                    evacuated(pe, ("mlaH", L, g))
                pe.wait_ge(sem(f"qk_ready{L}"), 2)
                pe.wait_ge(sem(f"masks_ready{L}"), 1)

                def scores(u):
                    kind, h, t = u
                    nk = 256 if t < 2 else TOK
                    rows = slice(t * P, (t + 1) * P)
                    if kind == "A":
                        o, full = product(("S", L, u))
                        if h < AH:
                            p = slice(64 * (h // 3), 64 * (h // 3) + 64)
                            mm = pe.matmul(o[:, 0:nk], GT[p, h % 3, rows], GT[p, 3, 0:nk], start=True, stop=True)
                        else:
                            m = h - AH
                            mm = pe.matmul(o[:, 0:nk], MT[0:LQK, m, rows], MT[0:LQK, 4 + m, 0:nk], start=True, stop=True)
                        mm.then_inc(full, 1)
                        return
                    for i, (part, mask) in enumerate((("CF", C_MF), ("CB", C_MB))):
                        o, full = product((part, L, u))
                        m0 = mask - C_MF + (0 if t % 2 else P)
                        for n, c in enumerate((CH, CL)):
                            pe.matmul(o[:, 0:nk], SELECT[0:4, h * P:(h + 1) * P], c[0:4, i, 0:nk], start=n == 0, stop=False)
                        pe.matmul(o[:, nk - 256:nk], IDENT[:, :], MASKS[:, m0:m0 + 256], start=False, stop=True).then_inc(full, 1)
                    o, full = product(("S", L, u))
                    pe.matmul(o[:, 0:nk], QK[0:MD, h, rows], QK[0:MD, 4 + h, 0:nk], start=True, stop=True).then_inc(full, 1)

                def turn(u, n):
                    kind, h, t = u
                    src = PA[:, n % 2, :] if kind == "A" else WT
                    if kind == "A":
                        evacuated(pe, ("S", L, u))
                    else:
                        pe.wait_ge(sem(f"weights_ready{L}"), n + 1)
                    o, full = product(("T", L, u))
                    for b in range(2 if t < 2 else NT):
                        mm = pe.transpose(o[:, b * P:(b + 1) * P], src[:, b * P:(b + 1) * P], ident)
                    mm.then_inc(full, 1)

                def values(u):
                    kind, h, t = u
                    evacuated(pe, ("T", L, u))
                    o, full = product(("O", L, u))
                    nb = 2 if t < 2 else NT
                    for b in range(nb):
                        if kind == "M":
                            w, v, n = PTM, PMV[:, b, h * MD:(h + 1) * MD], MD
                        elif h < AH:
                            w, v, n = PT, PAVCQ[:, b, 64 * (h // 3):64 * (h // 3) + 64], 64
                        else:
                            w, v, n = PT, VM[:, b, h - AH, :], 64
                        mm = pe.matmul(o[:, 0:n], w[:, b * P:(b + 1) * P], v, start=b == 0, stop=b == nb - 1)
                    mm.then_inc(full, 1)

                done = {"A": [], "M": []}
                for u in mixer_units(L):
                    d = done[u[0]]
                    scores(u)
                    if len(d) > 1:
                        values(d[-2])
                    if d:
                        turn(d[-1], len(d) - 1)
                    d.append(u)
                    if L == 0 and u in pieces:
                        modulation(1, pieces[u])
                for d in done.values():
                    values(d[-2])
                    turn(d[-1], len(d) - 1)
                    values(d[-1])

            def spread(L, kind, sec):
                for g in groups(L):
                    for half in range(2):
                        o, full = product((kind, L, g, half))
                        for k in range(4):
                            col = modT[:, L, sec, 4 * half + k, g:g + 1].broadcast_to([P, P])
                            mm = pe.matmul(o[:, k * P:(k + 1) * P], col, ident, start=True, stop=True)
                        mm.then_inc(full, 1)

            def out_project(L):
                spread(L, "gateA", 2)
                keep_warm(("outT", L, 0), WARM_UP["out"][L])
                pe.wait_ge(sem(f"mix_ready{L}"), 1)
                for k in range(KT):
                    o, full = product(("outT", L, k))
                    for t in query_tiles(L):
                        mm = pe.transpose(o[:, t * P:(t + 1) * P], OROW[:, t, k * P:(k + 1) * P], ident)
                    mm.then_inc(full, 1)
                columns_ready(L, "outT")
                for c in range(2):
                    rows_product([("out", L, c, t) for t in query_tiles(L)], query_tiles(L), [slice(0, 512)] * NT)

            def bank_ready(b, n):
                pe.wait_ge(bank_free[b], n)
                return bank[b], bank_full[b]

            def ffn():
                def step(j):
                    def split_of(i):
                        pe.wait_ge(split_lo, j * 6 + (starts["ffn"] + i + 1))
                        return pair_ap(i % PAIRS, 4, 512)

                    for n, kind in enumerate(("G", "U")):
                        for half in range(2):
                            w = split_of(2 * n + half)
                            if n == 0:
                                pe.wait_ge(sem("features_0f"), 4 * half + 4)
                            for f in range(4):
                                b, m = ffn_at(kind, j, f)
                                cols = slice(f * P, (f + 1) * P)
                                if not half:
                                    pe.wait_ge(bank_free[b], m)
                                for k in range(4):
                                    mm = three(bank[b][:, :], (w[0][:, k, cols], w[1][:, k, cols]),
                                               features(4 * half + k, slice(0, TOK)), half + k == 0, half + k == 4)
                                if half:
                                    mm.then_inc(bank_full[b], 1)
                            if not half:
                                mm.then_inc(tile_used, 1)
                    for c in range(2):
                        w = split_of(4 + c)
                        banks = [bank_ready(*ffn_at(f"Y{c}", j, t)) for t in range(NT)]
                        for f in range(4):
                            if c == 0:
                                pe.wait_ge(sem("hidden_ready"), j * 4 + (f + 1))
                            for t, (o, full) in enumerate(banks):
                                cols = slice(t * P, (t + 1) * P)
                                mm = three(o[:, :], (TH[:, f, cols], TL[:, f, cols]), (w[0][:, f, :], w[1][:, f, :]), f == 0, f == 3)
                                if f == 3:
                                    mm.then_inc(full, 1)

                with pe.Fori(0, NJ) as j:
                    step(j)
                taken[0] = ffn_to
                split_taken[0] = starts["ffn"] + 6 * NJ
                spread(0, "gateF", 5)

            def route():
                columns_ready(1, "norm", "f")
                for t in range(2):
                    o, full = product(("router", t))
                    for k in range(KT):
                        mm = pe.matmul(o[:, 0:NE], HT[:, k, (2 + t) * P:(3 + t) * P], RT[:, k, :], start=k == 0, stop=k == KT - 1)
                    mm.then_inc(full, 1)
                spread(1, "gateF", 5)
                pe.wait_ge(sem("routed"), 1)
                o, full = product(("pos",))
                tri, one = cst[:, C_TRI:C_TRI + P], cst[:, C_ONE:C_ONE + P]
                s0, s1 = SELM[:, 0, 0:NE], SELM[:, 1, 0:NE]
                pe.matmul(o[:, 0:NE], tri, s0, start=True, stop=True)
                pe.matmul(o[:, NE:2 * NE], one, s0, start=True, stop=False)
                pe.matmul(o[:, NE:2 * NE], tri, s1, start=False, stop=True)
                pe.matmul(o[:, 2 * NE:3 * NE], one, s0, start=True, stop=False)
                pe.matmul(o[:, 2 * NE:3 * NE], one, s1, start=False, stop=True).then_inc(full, 1)

            def experts(p):
                def gather(half, b, n):
                    o, full = bank_ready(b, n)
                    for k in range(4):
                        f = 4 * half + k
                        for t in range(2):
                            mm = pe.matmul(o[:, k * P:(k + 1) * P], XN[:, 2 + t, f * P:(f + 1) * P], GM[:, t, :],
                                           start=t == 0, stop=t == 1)
                    mm.then_inc(full, 1)

                def scatter(i, b, n):
                    o, full = bank_ready(b, n)
                    t, c = i // 2, i % 2
                    pe.matmul(o[:, :], SMT[:, t, :], YROW[:, 512 * c:512 * (c + 1)], start=True, stop=True).then_inc(full, 1)

                def expert(e):
                    at = [0]

                    def next_tile():
                        i = at[0]
                        at[0] += 1
                        pe.wait_ge(split_lo, tile_no(p, e, i) + 1)
                        return pair_ap(i % PAIRS, 4, 512)

                    def gate_or_up(kind, j):
                        o, full = bank_ready(*moe_at(p, e, kind, j))
                        for c in range(2):
                            w = next_tile()
                            if kind == "G" and j == 0:
                                pe.wait_ge(sem("tokens_ready"), e * 2 + (2 * p * (NE + 1) + c + 1))
                            for k in range(4):
                                mm = three(o[:, :], (XTH[:, 4 * c + k, :], XTL[:, 4 * c + k, :]), (w[0][:, k, :], w[1][:, k, :]),
                                           c + k == 0, c + k == 4)
                            mm.then_inc(full if c else tile_used, 1)

                    def turn(j):
                        b, n = moe_at(p, e, "U", j)
                        pe.wait_ge(bank_free[b], n + 1)
                        o, full = bank_ready(*moe_at(p, e, "HT", j))
                        for k in range(4):
                            mm = pe.transpose(o[:, k * P:(k + 1) * P], H[:, k * P:(k + 1) * P], ident)
                        mm.then_inc(full, 1)

                    def down(j):
                        b, n = moe_at(p, e, "HT", j)
                        pe.wait_ge(bank_free[b], n + 1)
                        for c in range(2):
                            b, n = moe_at(p, e, "Y", c)
                            if j == 0:
                                pe.wait_ge(bank_free[b], n)
                            w = next_tile()
                            for k in range(4):
                                cols = slice(k * P, (k + 1) * P)
                                mm = three(bank[b][:, :], (TH[:, 0, cols], TL[:, 0, cols]), (w[0][:, k, :], w[1][:, k, :]),
                                           j + k == 0, j == NJ - 1 and k == 3)
                            mm.then_inc(bank_full[b] if j == NJ - 1 else tile_used, 1)

                    for j in range(NJ):
                        gate_or_up("G", j)
                        if j < 2:
                            if j == 0:
                                for c in range(2):
                                    b, n = moe_at(p, e, "Y", c)
                                    pe.wait_ge(bank_free[b], n)
                            scatter(2 * j, *moe_at(p, e, "SC", 2 * j))
                        if j:
                            turn(j - 1)
                        gate_or_up("U", j)
                        if j < 2:
                            scatter(2 * j + 1, *moe_at(p, e, "SC", 2 * j + 1))
                        if j == NJ - 1:
                            pe.wait_ge(sem("gather_ready"), e + (p * (NE + 1) + 2))
                            gather(0, *moe_at(p, e, "GA", 0))
                        if j:
                            down(j - 1)
                        if j == 3:
                            pe.wait_ge(sem("scatter_ready"), e + (p * NE + 1))
                            o, full = bank_ready(*moe_at(p, e, "ST"))
                            for t in range(2):
                                mm = pe.transpose(o[:, t * P:(t + 1) * P], SM[:, t, :], ident)
                            mm.then_inc(full, 1)
                    turn(NJ - 1)
                    gather(1, *moe_at(p, e, "GA", 1))
                    down(NJ - 1)

                pe.wait_ge(sem("moe_cleared"), p + 1)
                pe.wait_ge(sem("gather_ready"), p * (NE + 1) + 1)
                for half in range(2):
                    gather(half, *first_gather(p, half))
                with pe.Fori(0, NE) as e:
                    expert(e)
                for c in range(2):
                    b, n = moe_at(p, NE, "Y", c)
                    pe.wait_ge(bank_free[b], n)
                for i in range(4):
                    scatter(i, *last_scatter(p, i))

            pe.wait_ge(sem("consts_loaded"), 16)
            pe.wait_ge(sem("cvec_split"), 1)
            for i in range(13):
                modulation(0, i)
            for L in range(DEPTH):
                norm(L, "a")
                project(L)
                prepare(L)
                heads(L)
                out_project(L)
                norm(L, "f")
                if L == 0:
                    ffn()
            route()
            experts(0)
            over = overflow(pe)
            with pe.If(over > 0):
                experts(1)

        @block.scalar
        def _(act):
            step = sem("act_step")
            steps = [0]

            def then(ins):
                steps[0] += 1
                ins.then_inc(step, 1)
                act.wait_ge(step, steps[0])

            def sqrt_of(L, name, v):
                act.wait_ge(sem(f"{name}_mean{L}"), 1)
                act.activation(v, v, ACT.Sqrt).then_inc(sem(f"{name}_root{L}"), 1)

            def sqrt_ahead():
                act.activation(warm[:, :], cst[:, C_ONE:C_ONE + 1], ACT.Sqrt)

            def norm(L, w):
                g0 = groups(L)[0] if w == "f" else 0
                if L == 0 and w == "a":
                    act.wait_ge(sem("consts_loaded"), 16)
                    act.wait_ge(sem("x_loaded"), 32)
                sqrt_ahead()
                for t in range(2 * g0, NT):
                    if (L, w) != (0, "a"):
                        act.wait_ge(sem(f"x_updated_{L}{w}"), t - 2 * g0 + 1)
                    junk = bigB[:, t * D:(t + 1) * D]
                    if w == "f":
                        junk = scr[:, t % 2 * D:(t % 2 + 1) * D]
                        if t - 2 * g0 > 1:
                            act.wait_ge(sem(f"squares_{L}f"), t - 2 * g0 - 1)
                    act.activation(junk, X[:, t, :], ACT.Square, accum_out=ss[:, t:t + 1]).then_inc(sem(f"squares_{L}{w}"), 1)
                sqrt_of(L, f"x{w}", rs[:, 2 * g0:NT])
                evacuated(act, ("modT", L, 11))
                first = starts["in", L] if w == "a" else starts["ffn"]
                if w == "a":
                    static_split("ScalarE", first)
                elif L == 0:
                    for i in range(PAIRS):
                        static_split("ScalarE", first + i)
                if (L, w) == (1, "f"):
                    for k in range(0, KT, 2):
                        o, free = take_out(act, ("norm", L, w, k))
                        modulated(act, HT[:, k, :], o, L, w, k, g0).then_inc(free, 1)
                    return
                act.wait_ge(sem(f"squares_{L}{w}"), NT - 2 * g0)
                for k in range(KT):
                    if k > 1:
                        act.wait_ge(sem(f"features_{L}{w}"), k - 1)
                    o, free = take_out(act, ("norm", L, w, k))
                    modulated(act, TMPK[:, k % 2, :], o, L, w, k, g0).then_inc(free, 1)
                if w == "a":
                    static_split("ScalarE", first + 1)

            act.dma_start(cvec[:, :, 1], a["c"][0].rearrange("(k p) -> p k", p=P), allow_slow_non_contiguous=True).then_inc(sem("cvec_loaded"), 16)
            act.dma_start(cvec[:, :, 0], a["c_ctx"].rearrange("(k p) -> p k", p=P), allow_slow_non_contiguous=True).then_inc(sem("cvec_loaded"), 16)
            act.dma_start(X[:, 0:2, :], a["ctx"][0].rearrange("(t p) d -> p t d", p=P)).then_inc(sem("x_loaded"), 16)
            act.dma_start(X[:, 2:4, :], a["x"][0].rearrange("(t p) d -> p t d", p=P)).then_inc(sem("x_loaded"), 16)
            act.wait_ge(sem("cvec_loaded"), 32)
            act.activation(cvec[:, :, :], cvec[:, :, :], ACT.Silu).then_inc(sem("cvec_ready"), 1)
            act.wait_ge(sem("cvec_ready"), 1)
            act.activation(csplit[:, :, 0:2], cvec[:, :, :], ACT.Copy).then_inc(sem("cvec_rounded"), 1)
            for n in range(24):
                static_split("ScalarE", n)

            def project(L):
                work = {W_CKV: square_latents, W_OG: log_sigmoid, W_GQA: square_gqa}
                for c in range(2):
                    static_split("ScalarE", starts["in", L] + 2 * c + 2)
                    for h in range(4 * c, 4 * c + 4):
                        o, _ = take_out(act, ("conv", L, h))
                        toks = slice(conv_from(L, h), TOK)
                        act.activation(QK[0:MD, h, toks], o[0:MD, toks], ACT.Identity, scale=convw[:, L, h, 1:2]).then_inc(sem(f"middle_tap{L}"), 1)
                    static_split("ScalarE", starts["in", L] + 2 * c + 3)
                for s, w in enumerate(ROWS_OF_W):
                    more = s + 1 < len(ROWS_OF_W)
                    if more:
                        static_split("ScalarE", starts["in", L] + 2 * s + 6)
                    for t in (0, 2):
                        o, free = take_out(act, ("proj", L, s, t))
                        if w == W_GQA:
                            to, src = paired(t, o)
                            act.activation(to, src, ACT.Copy)
                            act.activation(PG[:, t, 384:512], o[:, 384:512], ACT.Copy).then_inc(free, 1)
                        else:
                            cols = columns_for(L, w, t)
                            act.activation(PROJ[w][:, t, cols], o[:, cols], ACT.Copy).then_inc(free, 1)
                    if more:
                        static_split("ScalarE", starts["in", L] + 2 * s + 7)
                    if s == 0:
                        silu_of_convolutions(L)
                    elif w in work:
                        work[w](L)

            def silu_of_convolutions(L):
                for h in (4 + 2, 4 + 3):
                    evacuated(act, ("conv", L, h))
                for c in range(2):
                    qk = QK[0:MD, 4 * c:4 * c + 4, conv_from(L, 4 * c):]
                    act.activation(qk, qk, ACT.Silu).then_inc(sem(f"qk_ready{L}"), 1)

            def square_latents(L):
                for t in range(NT):
                    for w in (W_AVCQ, W_CKV):
                        evacuated(act, ("proj", L, ROWS_OF_W.index(w), t))
                act.activation(SQ[:, :, 0:256], PAVCQ[:, :, 128:384], ACT.Square)
                act.activation(SQ[:, :, 256:416], PCKV[:, :, :], ACT.Square).then_inc(sem(f"latent_squares{L}"), 1)
                sqrt_of(L, "latent", grs[:, 0:12])

            def log_sigmoid(L):
                act.wait_ge(sem(f"gate_negated{L}"), 1)
                then(act.activation(gtmp[:, :, :], gtmp[:, :, :], ACT.Exp))
                act.activation(gtmp[:, :, :], gtmp[:, :, :], ACT.Ln, bias=1.0).then_inc(sem(f"gate_log{L}"), 1)
                for t in range(NT):
                    evacuated(act, ("proj", L, ROWS_OF_W.index(W_OG), t))
                gate = PMO[:, query_tiles(L)[0]:NT, 0:MW]
                act.activation(gate, gate, ACT.Sigmoid).then_inc(sem(f"out_gate{L}"), 1)

            def square_gqa(L):
                for t in range(NT):
                    evacuated(act, ("proj", L, ROWS_OF_W.index(W_GQA), t))
                act.wait_ge(sem(f"latent_rotated{L}"), 1)
                act.activation(SQ[:, :, :], PG[:, :, :], ACT.Square).then_inc(sem(f"gqa_squares{L}"), 1)
                sqrt_of(L, "gqa", grs[:, 16:48])

            def prepare(L):
                for g in range(3):
                    o, free = take_out(act, ("mlaT", L, g))
                    act.activation(CT[:, g, :], o[:, :], ACT.Identity, scale=cqG[:, L, g:g + 1]).then_inc(free, 1)
                for g in range(4):
                    o, free = take_out(act, ("gqaT", L, g))
                    act.activation(GT[:, g, :], o[:, :], ACT.Copy).then_inc(free, 1)
                act.activation(MASKS[:, :], cst[:, C_MF:C_MF + 768], ACT.Copy)
                act.activation(SELECT[0:4, :], cst[0:4, C_SEL:C_SEL + 512], ACT.Copy)
                act.activation(IDENT[:, :], ident, ACT.Copy).then_inc(sem(f"masks_ready{L}"), 1)
                for t in range(NT):
                    o, free = take_out(act, ("mlaq", L, t))
                    act.activation(QR[:, t, :, :], o[:, 0:LH * LQK].rearrange("p (h d) -> p h d", h=LH), ACT.Copy).then_inc(free, 1)
                sqrt_ahead()
                for t in range(NT):
                    evacuated(act, ("mlaq", L, t))
                act.activation(SQ[:, :, 0:384].rearrange("p t (h d) -> p t h d", h=LH), QR[:, :, :, :], ACT.Square).then_inc(sem(f"mla_squares{L}"), 1)
                for t in range(NT):
                    evacuated(act, ("mlakv", L, t))
                act.activation(KSQ[:, :, :, :], KR[:, :, :, 0:64], ACT.Square).then_inc(sem(f"mla_squares{L}"), 1)
                sqrt_of(L, "mla", grs[:, 0:48])
                o, free = take_out(act, ("stab", L))
                act.activation(stab[:, :, :, :], o[:, 0:64].rearrange("p (k t h) -> p k t h", k=4, t=4), ACT.Copy, scale=-1.0)\
                    .then_inc(free, 1)
                evacuated(act, ("stab", L))
                act.activation(stab[:, 2:4, :, :], stab[:, 2:4, :, :], ACT.Exp).then_inc(sem(f"stab_exp{L}"), 1)
                for g in range(0, 8, 2):
                    o, free = take_out(act, ("mlaH", L, g))
                    act.activation(MT[0:LQK, g, :], o[0:LQK, :], ACT.Copy).then_inc(free, 1)

            def heads(L):
                count = {"A": 0, "M": 0}
                before = {"A": None, "M": None}

                def turned(u):
                    kind, h, t = u
                    nk = 256 if t < 2 else TOK
                    o, free = take_out(act, ("T", L, u))
                    act.activation((PT if kind == "A" else PTM)[:, 0:nk], o[:, 0:nk], ACT.Copy).then_inc(free, 1)

                for u in mixer_units(L):
                    kind, h, t = u
                    n = count[kind]
                    count[kind] += 1
                    nk = 256 if t < 2 else TOK
                    if kind == "A":
                        act.wait_ge(sem(f"row_max{L}"), n + 1)
                        o, free = take_out(act, ("S", L, u))
                        act.activation(PA[:, n % 2, 0:nk], o[:, 0:nk], ACT.Exp, bias=nmax[:, 0:1],
                                       accum_out=rsum[:, n % 4:n % 4 + 1]).then_inc(free, 1)
                    else:
                        if n:
                            act.wait_ge(sem(f"weights_ready{L}"), n)
                        for i, (part, e) in enumerate((("CF", EF), ("CB", EB))):
                            o, free = take_out(act, (part, L, u))
                            act.activation(e[:, 0:nk], o[:, 0:nk], ACT.Exp, bias=stab[:, i, t, h:h + 1]).then_inc(free, 1)
                    if before[kind]:
                        turned(before[kind])
                    before[kind] = u
                turned(before["A"])
                turned(before["M"])

            def out_project(L):
                t0 = query_tiles(L)[0]
                sqrt_ahead()
                last = [u for u in mixer_units(L) if u[0] == "M"][-1]
                evacuated(act, ("O", L, last))
                evacuated(act, ("modT", 1, 11))
                act.activation(SQ[:, t0:NT, 0:MW], OROW[:, t0:NT, 0:MW], ACT.Square).then_inc(sem(f"mlstm_squares{L}"), 1)
                sqrt_of(L, "mlstm", grs[:, 0:4 * (NT - t0)])
                first = starts["out", L]
                static_split("ScalarE", first)
                spread(L, "gateA", GBC_A)
                for k in range(KT):
                    o, _ = take_out(act, ("outT", L, k))
                    act.activation(HH[:, k, t0 * P:], o[:, t0 * P:], ACT.Copy).then_inc(sem(f"mix_rounded{L}"), 1)
                static_split("ScalarE", first + 1)
                static_split("ScalarE", first + 2)
                static_split("ScalarE", first + 3)

            def spread(L, kind, to):
                for g in groups(L):
                    for half in range(2):
                        o, free = take_out(act, (kind, L, g, half))
                        act.activation(to[:, g, 512 * half:512 * (half + 1)], o[:, :], ACT.Copy).then_inc(free, 1)

            def ffn():
                def step(j, more):
                    for i in range(6):
                        if i == 1:
                            for t in range(NT):
                                b, n = ffn_at("G", j, t)
                                act.wait_ge(bank_full[b], n + 1)
                                act.activation(SILF[:, t, :], bank[b][:, :], ACT.Silu).then_inc(bank_free[b], 1)
                        if i == 3:
                            for f in range(4):
                                b, n = ffn_at("U", j, f)
                                act.wait_ge(bank_free[b], n + 1)
                                act.activation(TH[:, f, :], SILF[:, f, :], ACT.Copy).then_inc(sem("hidden_rounded"), 1)
                        if i < 3 or more:
                            ffn_left(act, j, i)
                            ffn_split("ScalarE", j + (i + PAIRS) // 6, (i + PAIRS) % 6)

                with act.Fori(0, NJ - 1) as j:
                    step(j, True)
                step(NJ - 1, False)
                spread(0, "gateF", GBC_F)

            def experts(p):
                def gathered(half, b, n):
                    act.wait_ge(bank_full[b], n + 1)
                    for k in range(4):
                        f = 4 * half + k
                        ins = act.activation(XTF[:, f, :], bank[b][:, k * P:(k + 1) * P], ACT.Identity,
                                             scale=modT[:, 1, 4, f, 1:2], bias=modT[:, 1, 3, f, 1:2])
                    ins.then_inc(bank_free[b], 1)

                def expert(e, more):
                    def turned(j):
                        b, n = moe_at(p, e, "HT", j)
                        act.wait_ge(bank_full[b], n + 1)
                        act.activation(TH[:, 0, :], bank[b][:, :], ACT.Copy).then_inc(sem("expert_rounded"), 1)

                    for i, (m, j, c) in enumerate(tiles):
                        if (m, c) == ("g", 1):
                            b, n = moe_at(p, e, "G", j)
                            act.wait_ge(bank_full[b], n + 1)
                            act.activation(SIL[:, j % 2, :], bank[b][:, :], ACT.Silu).then_inc(bank_free[b], 1)
                            if j:
                                turned(j - 1)
                        if (m, j, c) == ("u", NJ - 1, 1):
                            gathered(0, *moe_at(p, e, "GA", 0))
                        if (m, j, c) == ("d", 2, 1):
                            b, n = moe_at(p, e, "ST")
                            act.wait_ge(bank_full[b], n + 1)
                            act.activation(SMT[:, :, :], bank[b][:, 0:2 * P].rearrange("p (t s) -> p t s", t=2), ACT.Copy)\
                                .then_inc(bank_free[b], 1)
                        if (m, j, c) == ("d", NJ - 2, 1):
                            turned(NJ - 1)
                            gathered(1, *moe_at(p, e, "GA", 1))
                        if (m, j) == ("d", NJ - 1):
                            b, n = moe_at(p, e, "Y", c)
                            act.wait_ge(bank_full[b], n + 1)
                            act.activation(YROW[:, 512 * c:512 * (c + 1)], bank[b][:, :], ACT.Copy).then_inc(bank_free[b], 1)
                        if i + PAIRS < PER or more:
                            moe_left(act, p, e, i)
                            moe_split("ScalarE", p, e + (i + PAIRS) // PER, (i + PAIRS) % PER)

                for i in range(0 if p else 2, PAIRS):
                    if p:
                        moe_left(act, 0, NE - 1, PER - PAIRS + i)
                    moe_split("ScalarE", p, 0, i)
                for half in range(2):
                    gathered(half, *first_gather(p, half))
                with act.Fori(0, NE - 1) as e:
                    expert(e, True)
                expert(NE - 1, False)

            for L in range(DEPTH):
                norm(L, "a")
                if L == 0:
                    act.wait_ge(sem("params_loaded"), PARAMS)
                project(L)
                prepare(L)
                heads(L)
                out_project(L)
                norm(L, "f")
                if L == 0:
                    ffn()
            for i in range(2):
                moe_split("ScalarE", 0, 0, i)
            act.wait_ge(sem("expert_gap"), 1)
            act.activation(wts[:, 0:2], wts[:, 0:2], ACT.Exp).then_inc(sem("expert_gap_exp"), 1)
            spread(1, "gateF", GBC_F)
            act.wait_ge(sem("moe_cleared"), 1)
            experts(0)
            over = overflow(act)
            with act.If(over > 0):
                act.wait_ge(sem("moe_cleared"), 2)
                experts(1)

        @block.vector
        def _(dve):
            step = sem("dve_step")
            steps = [0]

            def then(ins):
                steps[0] += 1
                ins.then_inc(step, 1)
                dve.wait_ge(step, steps[0])

            def mean(L, name, dst, src, n):
                dve.tensor_scalar(dst, src, 1.0 / n, EPS, ALU.mult, ALU.add).then_inc(sem(f"{name}_mean{L}"), 1)

            def rstd(L, name, v):
                dve.wait_ge(sem(f"{name}_root{L}"), 1)
                then(dve.reciprocal(v, v))

            dve.wait_ge(sem("consts_loaded"), 16)
            then(dve.memset(rt[:, :, :, :], 0.0))

            def modulation(L, i):
                if i < 12:
                    if i > 1:
                        b, n = plan.at[("modT", L, i - 2)]
                        dve.wait_ge(bank_full[b], n + 1)
                    if L == 0:
                        dve.wait_ge(sem(f"bias_loaded{i // 8}"), 16)
                        n, bias = 4, BIAS[i // 8][0][:, 512 * (i % 8):512 * (i % 8 + 1)]
                    else:
                        dve.wait_ge(sem(f"modb_loaded{i % 2}"), 16 * (i // 2 + 1))
                        n, bias = 2, MODB[0:2, i % 2, :]
                    o, free = take_out(dve, ("mod", L, i))
                    dve.tensor_tensor(MODROW[0:n, i % 2, :], o[0:n, :], bias, ALU.add).then_inc(free, 1)
                if i:
                    s, half = (i - 1) // 2, (i - 1) % 2
                    o, free = take_out(dve, ("modT", L, i - 1))
                    src = o[:, 0:8].rearrange("p (k g) -> p k g", g=2)
                    dst = modT[:, L, s, 4 * half:4 * half + 4, :]
                    if s in (1, 4):
                        g = normG[:, L, s // 4, 4 * half:4 * half + 4].unsqueeze(2).broadcast_to([P, 4, 2])
                        ins = dve.scalar_tensor_tensor(out=dst, in0=src, scalar=1.0, in1=g, op0=ALU.add, op1=ALU.mult)
                    else:
                        ins = dve.tensor_copy(dst, src)
                    ins.then_inc(free, 1)

            def norm(L, w):
                g0 = groups(L)[0] if w == "f" else 0
                dve.wait_ge(sem(f"squares_{L}{w}"), NT - 2 * g0)
                mean(L, f"x{w}", rs[:, 2 * g0:NT], ss[:, 2 * g0:NT], D)
                rstd(L, f"x{w}", rs[:, 2 * g0:NT])
                for t in range(2 * g0, NT):
                    dve.tensor_scalar(XN[:, t, :], X[:, t, :], rs[:, t:t + 1], None, ALU.mult).then_inc(sem(f"normed_{L}{w}"), 1)
                first = starts["in", L] if w == "a" else starts["ffn"]
                if w == "a":
                    static_split(rest, first)
                elif L == 0:
                    for i in range(PAIRS):
                        static_split(rest, first + i)
                if (L, w) == (1, "f"):
                    for k in range(1, KT, 2):
                        o, free = take_out(dve, ("norm", L, w, k))
                        modulated(dve, HT[:, k, :], o, L, w, k, g0).then_inc(free, 1)
                    return
                for k in range(KT):
                    evacuated(dve, ("norm", L, w, k))
                    then(dve.tensor_copy(HH[:, k, :], TMPK[:, k % 2, :]))
                    dve.tensor_tensor(HL[:, k, :], TMPK[:, k % 2, :], HH[:, k, :].bitcast(F32), ALU.subtract)\
                        .then_inc(sem(f"features_{L}{w}"), 1)
                if w == "a":
                    static_split(rest, first + 1)

            def project(L):
                work = {W_CKV: norm_latents, W_OG: gates, W_GQA: norm_gqa}
                two = "p (s t) -> p s t"
                for c in range(2):
                    static_split(rest, starts["in", L] + 2 * c + 2)
                    for h in range(4 * c, 4 * c + 4):
                        dve.wait_ge(sem(f"middle_tap{L}"), h + 1)
                        o, free = take_out(dve, ("conv", L, h))
                        first = conv_from(L, h) // 256
                        src = o[0:MD, :].rearrange(two, s=2)[:, first:, :]
                        dst = QK[0:MD, h, :].rearrange(two, s=2)[:, first:, :]
                        then(dve.scalar_tensor_tensor(out=dst[:, :, 1:256], in0=src[:, :, 0:255], scalar=convw[:, L, h, 0:1],
                                                      in1=dst[:, :, 1:256], op0=ALU.mult, op1=ALU.add))
                        dve.scalar_tensor_tensor(out=dst[:, :, 0:255], in0=src[:, :, 1:256], scalar=convw[:, L, h, 2:3],
                                                 in1=dst[:, :, 0:255], op0=ALU.mult, op1=ALU.add).then_inc(free, 1)
                    static_split(rest, starts["in", L] + 2 * c + 3)
                for s, w in enumerate(ROWS_OF_W):
                    more = s + 1 < len(ROWS_OF_W)
                    if more:
                        static_split(rest, starts["in", L] + 2 * s + 6)
                    for t in (1, 3):
                        o, free = take_out(dve, ("proj", L, s, t))
                        if w == W_GQA:
                            dve.tensor_copy(*paired(t, o))
                            dve.tensor_copy(PG[:, t, 384:512], o[:, 384:512]).then_inc(free, 1)
                        else:
                            cols = columns_for(L, w, t)
                            dve.tensor_copy(PROJ[w][:, t, cols], o[:, cols]).then_inc(free, 1)
                    if more:
                        static_split(rest, starts["in", L] + 2 * s + 7)
                    if w in work:
                        work[w](L)

            def rope(xs, dim, cos_at, sin_at, heads_n, tmp):
                for i in range(2):
                    x, tm = xs(2 + i), tmp(i)
                    for q in range(2):
                        sin = cst[:, sin_at + i * dim:sin_at + (i + 1) * dim].rearrange("p (a b c) -> p a b c", a=2, b=2)[:, :, q, :]
                        xo = x.rearrange("p h (a b c) -> p h a b c", a=2, b=2)[:, :, :, 1 - q, :]
                        to = tm.rearrange("p h (a b c) -> p h a b c", a=2, b=2)[:, :, :, q, :]
                        for half in range(2):
                            ins = dve.tensor_tensor(to[:, :, half, :], xo[:, :, half, :],
                                                    sin[:, half, :].unsqueeze(1).broadcast_to([P, heads_n, dim // 4]), ALU.mult)
                    then(ins)
                    cos = cst[:, cos_at + i * dim:cos_at + (i + 1) * dim].unsqueeze(1).broadcast_to([P, heads_n, dim])
                    then(dve.tensor_tensor(x, x, cos, ALU.mult))
                    then(dve.tensor_tensor(x, x, tm, ALU.add))

            def gates(L):
                for t in range(NT):
                    evacuated(dve, ("proj", L, ROWS_OF_W.index(W_OG), t))
                bias = gains[:, L, G_GB:G_GB + 16].unsqueeze(1).broadcast_to([P, NT, 16])
                then(dve.tensor_tensor(GA[:, :, :], PMO[:, :, 384:400], bias, ALU.add))
                f = GA[:, :, :].rearrange("p t (d x h) -> p t d x h", d=2, x=2)[:, :, :, 1, :]
                g = gtmp[:, :, :].rearrange("p t (d h) -> p t d h", d=2)
                for d in range(2):
                    ins = dve.scalar_tensor_tensor(out=g[:, :, d, :], in0=f[:, :, d, :], scalar=-1.0, in1=f[:, :, d, :],
                                                   op0=ALU.mult, op1=ALU.min)
                ins.then_inc(sem(f"gate_negated{L}"), 1)
                dve.wait_ge(sem(f"gate_log{L}"), 1)
                lf = LF[:, :, :].rearrange("p t (d h) -> p t d h", d=2)
                for d in range(2):
                    ins = dve.scalar_tensor_tensor(out=lf[:, :, d, :], in0=f[:, :, d, :], scalar=0.0, in1=g[:, :, d, :],
                                                   op0=ALU.min, op1=ALU.subtract)
                ins.then_inc(sem(f"gates_ready{L}"), 1)

            def norm_gqa(L):
                dve.wait_ge(sem(f"out_gate{L}"), 1)
                gate = PMO[:, query_tiles(L)[0]:NT, 0:MW]
                then(dve.tensor_tensor(gate, gate, gains[:, L, G_M:G_M + MW].unsqueeze(1).broadcast_to([P, len(query_tiles(L)), MW]), ALU.mult))
                dve.wait_ge(sem(f"gqa_squares{L}"), 1)
                then(dve.tensor_reduce(gss[:, 0:32].rearrange("p (t h) -> p t h", t=NT),
                                       SQ[:, :, :].rearrange("p t (h d) -> p t h d", d=AD), AX.X, ALU.add))
                mean(L, "gqa", grs[:, 16:48], gss[:, 0:32], AD)
                rstd(L, "gqa", grs[:, 16:48])
                for t in range(NT):
                    evacuated(dve, ("proj", L, ROWS_OF_W.index(W_GQA), t))
                heads_v = PG[:, :, :].rearrange("p t (h d) -> p t h d", d=AD)
                then(dve.tensor_tensor(heads_v, heads_v, grs[:, 16:48].rearrange("p (t h) -> p t h", t=NT).unsqueeze(3)
                                       .broadcast_to([P, NT, 8, AD]), ALU.mult))
                for h0, h1, at in ((0, AH, G_AQ), (AH, 8, G_AK)):
                    for t in range(NT):
                        ins = dve.tensor_tensor(heads_v[:, t, h0:h1, :], heads_v[:, t, h0:h1, :],
                                                gains[:, L, at:at + AD].unsqueeze(1).broadcast_to([P, h1 - h0, AD]), ALU.mult)
                then(ins)
                rope(lambda t: PG[:, t, :].rearrange("p (h d) -> p h d", d=AD), AD, C_COSA, C_SINA, 8,
                     lambda i: SQ[:, i, :].rearrange("p (h d) -> p h d", d=AD))
                then(dve.tensor_copy(den[:, 0:1], grs[:, 0:1]))
                dve.tensor_copy(den[:, 1:2], grs[:, 0:1]).then_inc(sem(f"gqa_ready{L}"), 1)

            def norm_latents(L):
                dve.wait_ge(sem(f"latent_squares{L}"), 1)
                dve.tensor_reduce(gss[:, 0:4], SQ[:, :, 0:256], AX.X, ALU.add)
                dve.tensor_reduce(gss[:, 4:8], SQ[:, :, 256:384], AX.X, ALU.add)
                then(dve.tensor_reduce(gss[:, 8:12], SQ[:, :, 384:416], AX.X, ALU.add))
                dve.tensor_scalar(grs[:, 0:4], gss[:, 0:4], 1.0 / QRANK, EPS, ALU.mult, ALU.add)
                dve.tensor_scalar(grs[:, 4:8], gss[:, 4:8], 1.0 / KVRANK, EPS, ALU.mult, ALU.add)
                mean(L, "latent", grs[:, 8:12], gss[:, 8:12], ROPE)
                rstd(L, "latent", grs[:, 0:12])
                for t in range(NT):
                    evacuated(dve, ("proj", L, ROWS_OF_W.index(W_AVCQ), t))
                    evacuated(dve, ("proj", L, ROWS_OF_W.index(W_CKV), t))
                for x, n, at in ((PAVCQ[:, :, 128:384], 256, 0), (PCKV[:, :, 0:128], 128, 4), (PCKV[:, :, 128:160], 32, 8)):
                    ins = dve.tensor_tensor(x, x, grs[:, at:at + 4].unsqueeze(2).broadcast_to([P, NT, n]), ALU.mult)
                ins.then_inc(sem(f"latent_ready{L}"), 1)
                dve.wait_ge(sem(f"latent_ready{L}"), 1)
                kr = PCKV[:, :, 128:160]
                then(dve.tensor_tensor(kr, kr, gains[:, L, G_LK + 64:G_LK + 96].unsqueeze(1).broadcast_to([P, NT, ROPE]), ALU.mult))
                rope(lambda t: PCKV[:, t, 128:160].unsqueeze(1), ROPE, C_COSL, C_SINL, 1,
                     lambda i: SQ[:, i, 0:32].unsqueeze(1))
                then(dve.tensor_copy(den[:, 0:1], grs[:, 0:1]))
                dve.tensor_copy(den[:, 1:2], grs[:, 0:1]).then_inc(sem(f"latent_rotated{L}"), 1)

            def prepare(L):
                ones = cst[0:4, C_ONE:C_ONE + 1]
                for d, (rows, ki, kf) in enumerate(((rows_f, 0, 1), (rows_b, 2, 3))):
                    fo, f_free = take_out(dve, ("gateT", L, kf))
                    io, i_free = take_out(dve, ("gateT", L, ki))
                    parts = ((0, 512),) if d == 0 else ((0, 256), (256, 512))

                    def seg(x, lo, hi):
                        return x[:, lo:hi] if d == 0 else x[:, lo:hi][:, ::-1]
                    for n, (lo, hi) in enumerate(parts):
                        init = 0.0 if n == 0 else rows[0:4, 0, 0:1]
                        then(dve.tensor_tensor_scan(seg(rows[0:4, 0, :], lo, hi), ones.broadcast_to([4, hi - lo]),
                                                    seg(fo[0:4, :], lo, hi), init, ALU.mult, ALU.add))
                    dve.tensor_copy(rinv[0:4, 0:1], fo[0:4, 0:1]).then_inc(f_free, 1)
                    dve.tensor_tensor(crow[0:4, d, :], io[0:4, :], rows[0:4, 0, :], ALU.subtract).then_inc(i_free, 1)
                    evacuated(dve, ("gateT", L, ki))
                    for n, (lo, hi) in enumerate(parts):
                        init = 0.0 if n == 0 else rows[0:4, 1, 0:1]
                        c = seg(crow[0:4, d, :], lo, hi)
                        then(dve.tensor_tensor_scan(seg(rows[0:4, 1, :], lo, hi), c, c, init, ALU.max, ALU.max))
                    then(dve.tensor_copy(CH[0:4, d, :], crow[0:4, d, :]))
                    dve.tensor_tensor(CL[0:4, d, :], crow[0:4, d, :], CH[0:4, d, :].bitcast(F32), ALU.subtract)
                    dve.tensor_tensor(rows[0:4, 0, :], rows[0:4, 0, :], rows[0:4, 1, :], ALU.add).then_inc(sem(f"stabilisers{L}"), 1)

                for t in range(NT):
                    o, free = take_out(dve, ("mlakv", L, t))
                    kv = o[:, :].rearrange("p (h d) -> p h d", h=LH)
                    dve.tensor_copy(KR[:, t, :, 64:96], PCKV[:, t, 128:160].unsqueeze(1).broadcast_to([P, LH, ROPE]))
                    dve.tensor_copy(KR[:, t, :, 0:64], kv[:, :, 0:64])
                    dve.tensor_copy(VM[:, t, :, :], kv[:, :, 64:128]).then_inc(free, 1)
                dve.wait_ge(sem(f"mla_squares{L}"), 1)
                sq = SQ[:, :, 0:384].rearrange("p t (h d) -> p t h d", h=LH)
                th = "p (t h) -> p t h"
                dve.tensor_reduce(gss[:, 0:16].rearrange(th, t=NT), sq[:, :, :, 0:64], AX.X, ALU.add)
                dve.tensor_reduce(gss[:, 16:32].rearrange(th, t=NT), sq[:, :, :, 64:96], AX.X, ALU.add)
                dve.wait_ge(sem(f"mla_squares{L}"), 2)
                then(dve.tensor_reduce(gss[:, 32:48].rearrange(th, t=NT), KSQ[:, :, :, :], AX.X, ALU.add))
                dve.tensor_scalar(grs[:, 0:16], gss[:, 0:16], 1.0 / NOPE, EPS, ALU.mult, ALU.add)
                dve.tensor_scalar(grs[:, 16:32], gss[:, 16:32], 1.0 / ROPE, EPS, ALU.mult, ALU.add)
                mean(L, "mla", grs[:, 32:48], gss[:, 32:48], NOPE)
                rstd(L, "mla", grs[:, 0:48])
                for t in range(NT):
                    evacuated(dve, ("mlaq", L, t))
                for x, n, at in ((QR[:, :, :, 0:64], 64, 0), (QR[:, :, :, 64:96], 32, 16), (KR[:, :, :, 0:64], 64, 32)):
                    r = grs[:, at:at + 16].rearrange(th, t=NT)
                    for t in range(NT):
                        ins = dve.tensor_tensor(x[:, t], x[:, t], r[:, t, :].unsqueeze(2).broadcast_to([P, LH, n]), ALU.mult)
                then(ins)
                for t in range(NT):
                    ins = dve.tensor_tensor(QR[:, t], QR[:, t], gains[:, L, G_LQ:G_LQ + LQK].unsqueeze(1).broadcast_to([P, LH, LQK]), ALU.mult)
                then(ins)
                rope(lambda t: QR[:, t, :, 64:96], ROPE, C_COSL, C_SINL, LH,
                     lambda i: SQ[:, i, 0:128].rearrange("p (h d) -> p h d", h=LH))
                dve.tensor_copy(den[:, 0:1], grs[:, 0:1]).then_inc(sem(f"mla_ready{L}"), 1)
                for g in range(1, 8, 2):
                    o, free = take_out(dve, ("mlaH", L, g))
                    dve.tensor_copy(MT[0:LQK, g, :], o[0:LQK, :]).then_inc(free, 1)

            def heads(L):
                dve.wait_ge(sem(f"stab_exp{L}"), 1)
                seen = {"A": [], "M": []}

                def head_out(u, n):
                    kind, h, t = u
                    if kind == "A":
                        o, free = take_out(dve, ("O", L, u))
                        then(dve.reciprocal(rinv[:, 0:1], rsum[:, n % 4:n % 4 + 1]))
                        dve.tensor_scalar(OROW[:, t, MW + 64 * h:MW + 64 * (h + 1)], o[:, 0:64], rinv[:, 0:1], None, ALU.mult)\
                            .then_inc(free, 1)
                    else:
                        o, free = take_out(dve, ("O", L, u))
                        dve.tensor_copy(OROW[:, t, MD * h:MD * (h + 1)], o[:, 0:MD]).then_inc(free, 1)

                for u in mixer_units(L):
                    kind, h, t = u
                    nk = 256 if t < 2 else TOK
                    d = seen[kind]
                    if kind == "A":
                        o, _ = take_out(dve, ("S", L, u))
                        dve.tensor_reduce(nmax[:, 0:1], o[:, 0:nk], AX.X, ALU.max, negate=True).then_inc(sem(f"row_max{L}"), 1)
                    else:
                        o, free = take_out(dve, ("S", L, u))
                        evacuated(dve, ("CF", L, u))
                        dve.tensor_tensor_reduce(EF[:, 0:nk], EF[:, 0:nk], o[:, 0:nk], MD ** -0.5, 0.0, ALU.mult, ALU.add, den[:, 0:1])
                        evacuated(dve, ("CB", L, u))
                        dve.tensor_tensor_reduce(EB[:, 0:nk], EB[:, 0:nk], o[:, 0:nk], MD ** -0.5, 0.0, ALU.mult, ALU.add, den[:, 1:2])\
                            .then_inc(free, 1)
                        evacuated(dve, ("S", L, u))
                        then(dve.scalar_tensor_tensor(out=dabs[:, :], in0=den[:, :], scalar=-1.0, in1=den[:, :], op0=ALU.mult, op1=ALU.max))
                        then(dve.tensor_tensor(dabs[:, :], dabs[:, :], stab[:, 2:4, t, h], ALU.max))
                        then(dve.reciprocal(dabs[:, :], dabs[:, :]))
                        then(dve.tensor_scalar(EB[:, 0:nk], EB[:, 0:nk], dabs[:, 1:2], None, ALU.mult))
                        if d:
                            b, n = plan.at[("T", L, d[-1])]
                            dve.wait_ge(bank_full[b], n + 1)
                        dve.scalar_tensor_tensor(out=WT[:, 0:nk], in0=EF[:, 0:nk], scalar=dabs[:, 0:1], in1=EB[:, 0:nk],
                                                 op0=ALU.mult, op1=ALU.add).then_inc(sem(f"weights_ready{L}"), 1)
                    if len(d) > 1:
                        head_out(d[-2], len(d) - 2)
                    d.append(u)
                    if L == 0 and u in pieces:
                        modulation(1, pieces[u])
                for d in seen.values():
                    head_out(d[-2], len(d) - 2)
                    head_out(d[-1], len(d) - 1)

            def out_project(L):
                t0 = query_tiles(L)[0]
                nt = NT - t0
                dve.wait_ge(sem(f"mlstm_squares{L}"), 1)
                then(dve.tensor_reduce(gss[:, 0:4 * nt].rearrange("p (t h) -> p t h", h=MH),
                                       SQ[:, t0:NT, 0:MW].rearrange("p t (h d) -> p t h d", h=MH), AX.X, ALU.add))
                mean(L, "mlstm", grs[:, 0:4 * nt], gss[:, 0:4 * nt], MD)
                rstd(L, "mlstm", grs[:, 0:4 * nt])
                x = OROW[:, t0:NT, 0:MW]
                for t in range(nt):
                    v = OROW[:, t0 + t, 0:MW].rearrange("p (h d) -> p h d", h=MH)
                    ins = dve.tensor_tensor(v, v, grs[:, 4 * t:4 * t + 4].unsqueeze(2).broadcast_to([P, MH, MD]), ALU.mult)
                then(ins)
                dve.tensor_tensor(x, x, PMO[:, t0:NT, 0:MW], ALU.mult).then_inc(sem(f"mix_ready{L}"), 1)
                first = starts["out", L]
                static_split(rest, first)
                for k in range(KT):
                    o, free = take_out(dve, ("outT", L, k))
                    dve.wait_ge(sem(f"mix_rounded{L}"), k + 1)
                    dve.tensor_tensor(HL[:, k, t0 * P:], o[:, t0 * P:], HH[:, k, t0 * P:].bitcast(F32), ALU.subtract).then_inc(free, 1)
                static_split(rest, first + 1)
                static_split(rest, first + 2)
                for g in groups(L):
                    for half in range(2):
                        evacuated(dve, ("gateA", L, g, half))
                for c in range(2):
                    cols = slice(512 * c, 512 * (c + 1))
                    if c == 0:
                        static_split(rest, first + 3)
                    for t in query_tiles(L):
                        o, free = take_out(dve, ("out", L, c, t))
                        dve.tensor_tensor(TMPX[:, t % 2, :], o[:, :], GBC_A[:, t // 2, cols], ALU.mult).then_inc(free, 1)
                        evacuated(dve, ("out", L, c, t))
                        ins = dve.tensor_tensor(X[:, t, cols], X[:, t, cols], TMPX[:, t % 2, :], ALU.add)
                        if c:
                            ins.then_inc(sem(f"x_updated_{L}f"), 1)
                            if t % 2 and t < NT - 1:
                                dve.wait_ge(sem(f"x_updated_{L}f"), t - t0 + 1)
                        elif t % 2:
                            then(ins)

            def ffn():
                dve.wait_ge(sem("sums_cleared"), 1)

                def step(j, more):
                    for i in range(6):
                        if i == 3:
                            def rest_of_hidden(f):
                                dve.wait_ge(sem("hidden_rounded"), j * 4 + (f + 1))
                                dve.tensor_tensor(TL[:, f, :], SILF[:, f, :], TH[:, f, :].bitcast(F32), ALU.subtract)\
                                    .then_inc(sem("hidden_ready"), 1)

                            for f in range(4):
                                b, n = ffn_at("G", j, f)
                                dve.wait_ge(bank_free[b], n + 1)
                                b, n = ffn_at("U", j, f)
                                dve.wait_ge(bank_full[b], n + 1)
                                dve.tensor_tensor(SILF[:, f, :], SILF[:, f, :], bank[b][:, :], ALU.mult).then_inc(bank_free[b], 1)
                                if f:
                                    rest_of_hidden(f - 1)
                            rest_of_hidden(3)
                        if i > 3:
                            c = i - 4
                            for t in range(NT):
                                b, n = ffn_at(f"Y{c}", j, t)
                                dve.wait_ge(bank_full[b], n + 1)
                                y = YACC[:, t, 512 * c:512 * (c + 1)]
                                dve.tensor_tensor(y, bank[b][:, :], y, ALU.add).then_inc(bank_free[b], 1)
                        if i < 3 or more:
                            ffn_split(rest, j + (i + PAIRS) // 6, (i + PAIRS) % 6)

                with dve.Fori(0, NJ - 1) as j:
                    step(j, True)
                step(NJ - 1, False)
                for half in range(2):
                    for g in range(2):
                        evacuated(dve, ("gateF", 0, g, half))
                evacuated(dve, ("Y1", NJ - 1, NT - 1))
                for t in range(NT):
                    then(dve.tensor_tensor(YACC[:, t, :], YACC[:, t, :], GBC_F[:, t // 2, :], ALU.mult))
                    dve.tensor_tensor(X[:, t, :], X[:, t, :], YACC[:, t, :], ALU.add).then_inc(sem("x_updated_1a"), 1)

            def route():
                for t in range(2):
                    moe_split(rest, 0, 0, t)
                    o, free = take_out(dve, ("router", t))
                    dve.tensor_copy(LG[:, t, :], o[:, 0:NE]).then_inc(free, 1)
                iota = cst[:, C_IOTA:C_IOTA + NE]
                for t in range(2):
                    evacuated(dve, ("router", t))
                    then(dve.max(MX[:, :], LG[:, t, :]))
                    then(dve.max_index(idx[:, :], MX[:, :], LG[:, t, :]))
                    then(dve.tensor_copy(IDXF[:, 2 * t:2 * t + 2], idx[:, 0:2]))
                    then(dve.tensor_tensor(wts[:, t:t + 1], MX[:, 1:2], MX[:, 0:1], ALU.subtract))
                dve.tensor_copy(TOT[:, 0:1], wts[:, 0:1]).then_inc(sem("expert_gap"), 1)
                dve.wait_ge(sem("expert_gap_exp"), 1)
                then(dve.tensor_scalar(wts[:, 2:4], wts[:, 0:2], 1.0, None, ALU.add))
                then(dve.reciprocal(wts[:, 2:4], wts[:, 2:4]))
                then(dve.tensor_tensor(wts[:, 0:2], wts[:, 0:2], wts[:, 2:4], ALU.mult))
                for t in range(2):
                    for c in range(2):
                        ins = dve.tensor_scalar(OH[:, c, :], iota, IDXF[:, 2 * t + c:2 * t + c + 1], None, ALU.is_equal)
                    then(ins)
                    dve.tensor_tensor(SELM[:, t, 0:NE], OH[:, 0, :], OH[:, 1, :], ALU.add)
                    then(dve.tensor_scalar(OH[:, 0, :], OH[:, 0, :], wts[:, 2 + t:3 + t], None, ALU.mult))
                    then(dve.scalar_tensor_tensor(out=COMB[:, t, 0:NE], in0=OH[:, 1, :], scalar=wts[:, t:t + 1],
                                                  in1=OH[:, 0, :], op0=ALU.mult, op1=ALU.add))
                dve.tensor_copy(TOT[:, 0:1], wts[:, 0:1]).then_inc(sem("routed"), 1)
                o, free = take_out(dve, ("pos",))
                dve.tensor_copy(POS[:, :, 0:NE], o[:, 0:2 * NE].rearrange("p (t e) -> p t e", t=2))
                then(dve.tensor_reduce(TOT[:, 1:2], o[:, 2 * NE:3 * NE], AX.X, ALU.max))
                then(dve.tensor_copy(TOT[:, 2:3], o[:, 0:1]))
                dve.tensor_copy(TOT[:, 3:4], o[:, 0:1]).then_inc(free, 1)
                dve.tensor_scalar(flag[:, :], TOT[:, 1:2], P + 0.5, None, ALU.is_gt).then_inc(sem("flag_ready"), 1)
                dve.wait_ge(sem("sums_cleared"), 2)

            def experts(p):
                def one_hot(dst, e, weight):
                    for t in range(2):
                        ins = dve.tensor_scalar(dst[:, t, :], cst[:, C_IOTA + p * P:C_IOTA + (p + 1) * P],
                                                POS[:, t, bass.ds(e, 1)], weight[:, t, bass.ds(e, 1)], ALU.is_equal, ALU.mult)
                    return ins

                def tokens(half, b, n):
                    dve.wait_ge(bank_free[b], n + 1)
                    fs = slice(4 * half, 4 * half + 4)
                    dve.tensor_copy(XTH[:, fs, :], XTF[:, fs, :]).then_inc(sem("tokens_rounded"), 1)

                def tokens_rest(half, count):
                    fs = slice(4 * half, 4 * half + 4)
                    dve.wait_ge(sem("tokens_rounded"), count)
                    dve.tensor_tensor(XTL[:, fs, :], XTF[:, fs, :], XTH[:, fs, :].bitcast(F32), ALU.subtract).then_inc(sem("tokens_ready"), 1)

                def scattered(i, b, n):
                    t, c = i // 2, i % 2
                    dve.wait_ge(bank_full[b], n + 1)
                    y = ACC[:, t, 512 * c:512 * (c + 1)]
                    dve.tensor_tensor(y, bank[b][:, :], y, ALU.add).then_inc(bank_free[b], 1)

                dve.memset(YROW[:, :], 0.0)
                dve.memset(SMT[:, :, :], 0.0).then_inc(sem("moe_cleared"), 1)
                one_hot(GM, 0, SELM).then_inc(sem("gather_ready"), 1)
                for i in range(0 if p else 2, PAIRS):
                    moe_split(rest, p, 0, i)
                before = 2 * p * (NE + 1)
                for half in range(2):
                    tokens(half, *first_gather(p, half))
                    tokens_rest(half, before + half + 1)

                def expert(e, more):
                    def turned(j):
                        b, n = moe_at(p, e, "HT", j)
                        dve.wait_ge(sem("expert_rounded"), e * NJ + (p * NE * NJ + j + 1))
                        dve.tensor_tensor(TL[:, 0, :], bank[b][:, :], TH[:, 0, :].bitcast(F32), ALU.subtract).then_inc(bank_free[b], 1)

                    for i, (m, j, c) in enumerate(tiles):
                        if (m, c) == ("g", 1):
                            if j < 2:
                                scattered(2 * j, *moe_at(p, e, "SC", 2 * j))
                            if j:
                                turned(j - 1)
                        if (m, c) == ("u", 1):
                            b, n = moe_at(p, e, "G", j)
                            dve.wait_ge(bank_free[b], n + 1)
                            b, n = moe_at(p, e, "U", j)
                            dve.wait_ge(bank_full[b], n + 1)
                            dve.tensor_tensor(H[:, :], SIL[:, j % 2, :], bank[b][:, :], ALU.mult).then_inc(bank_free[b], 1)
                            if j < 2:
                                scattered(2 * j + 1, *moe_at(p, e, "SC", 2 * j + 1))
                            if j == 2:
                                one_hot(SM, e, COMB).then_inc(sem("scatter_ready"), 1)
                            if j == 4:
                                one_hot(GM, e + 1, SELM).then_inc(sem("gather_ready"), 1)
                            if j == NJ - 1:
                                tokens(0, *moe_at(p, e, "GA", 0))
                                tokens_rest(0, e * 2 + (before + 3))
                        if (m, j, c) == ("d", NJ - 2, 1):
                            turned(NJ - 1)
                            tokens(1, *moe_at(p, e, "GA", 1))
                            tokens_rest(1, e * 2 + (before + 4))
                        if i + PAIRS < PER or more:
                            moe_split(rest, p, e + (i + PAIRS) // PER, (i + PAIRS) % PER)

                with dve.Fori(0, NE - 1) as e:
                    expert(e, True)
                expert(NE - 1, False)
                for i in range(4):
                    scattered(i, *last_scatter(p, i))

            def finish():
                for half in range(2):
                    evacuated(dve, ("gateF", 1, 1, half))
                for t in range(2):
                    then(dve.tensor_tensor(ACC[:, t, :], ACC[:, t, :], GBC_F[:, 1, :], ALU.mult))
                    dve.tensor_tensor(X[:, 2 + t, :], X[:, 2 + t, :], ACC[:, t, :], ALU.add).then_inc(sem("out_row_ready"), 1)

            dve.wait_ge(sem("cvec_rounded"), 1)
            dve.tensor_tensor(csplit[:, :, 2:4], cvec[:, :, :], csplit[:, :, 0:2].bitcast(F32), ALU.subtract).then_inc(sem("cvec_split"), 1)
            for n in range(4):
                static_split(rest, n)
            for i in range(13):
                if i == 3:
                    dve.wait_ge(sem("norms_loaded"), 16 * 2 * DEPTH)
                modulation(0, i)
                for n in range(2 * i + 4, min(2 * i + 6, 24)):
                    static_split(rest, n)
            dve.wait_ge(sem("params_loaded"), PARAMS)
            for L in range(DEPTH):
                then(dve.tensor_scalar(gains[:, L, G_AQ:G_AQ + AD], gains[:, L, G_AQ:G_AQ + AD], AD ** -0.5, None, ALU.mult))
                then(dve.tensor_scalar(gains[:, L, G_LQ:G_LQ + LQK], gains[:, L, G_LQ:G_LQ + LQK], LQK ** -0.5, None, ALU.mult))
                then(dve.tensor_tensor(gains[:, L, G_LQ:G_LQ + NOPE], gains[:, L, G_LQ:G_LQ + NOPE], gains[:, L, G_LK:G_LK + NOPE], ALU.mult))
            for L in range(DEPTH):
                norm(L, "a")
                project(L)
                prepare(L)
                heads(L)
                out_project(L)
                norm(L, "f")
                if L == 0:
                    ffn()
            route()
            experts(0)
            over = overflow(dve)
            with dve.If(over > 0):
                experts(1)
            then(dve.memset(SIL[:, 0, 0:1], 0.0))
            finish()


_INS = ['x', 'c', 'ctx', 'c_ctx', 'mod_w', 'mod_b', 'norm_mix', 'norm_ffn', 'w_in', 'm_conv', 'm_gate_b', 'm_norm',
        'a_qnorm', 'a_knorm', 'l_cq_norm', 'l_ckv_norm', 'l_wuq', 'l_wukv', 'l_qnorm', 'l_knorm', 'w_out',
        'ffn_wg', 'ffn_wu', 'ffn_wd', 'moe_router', 'moe_wg', 'moe_wu', 'moe_wd']


def kernel(**inputs):
    import numpy as _np
    import concourse.bacc as _bacc
    from concourse.bass_utils import run_bass_kernel_spmd as _run

    nc = _bacc.Bacc("TRN2", target_bir_lowering=False, num_devices=1)
    arrays, args = {}, {}
    for name in _INS:
        v = _np.ascontiguousarray(inputs[name])
        arrays[f"in_{name}"] = v
        args[name] = nc.dram_tensor(f"in_{name}", v.shape, F32, kind="ExternalInput").ap()
    arrays["in_constants"] = constants()
    consts = nc.dram_tensor("in_constants", (P, C_END), F32, kind="ExternalInput").ap()
    out = nc.dram_tensor("out", (1, 256, D), F32, kind="ExternalOutput").ap()
    build(nc, args, consts, out)
    r = _run(nc, [arrays], core_ids=[0])
    return r.results[0]["out"]
```
